# Optimizing a Trainium2 kernel written in Bass

```python
import math
import jax, jax.numpy as jnp
from jax import lax
import numpy as np

D_MODEL = 1024
BATCH = 1
SEQ = 256
DEPTH = 1

D_MIX = D_MODEL
HEAD_DIM = 64
RET_WIDTH = D_MIX // 2
SB_WIDTH = D_MIX - RET_WIDTH
N_RET_HEADS = RET_WIDTH // HEAD_DIM
N_SB_HEADS = SB_WIDTH // HEAD_DIM
RET_CHUNK = 128
SB_BLOCK = 128
ROPE_BASE = 10000.0
IN_COLS = 4 * RET_WIDTH + 3 * SB_WIDTH
N_KEYS = 128
N_EXPERTS = N_KEYS * N_KEYS
PEER_HEADS = 8
PEER_TOPK = 16
PEER_QDIM = 256
PEER_HALF = PEER_QDIM // 2
PEER_BLOCK = 128
EPS = 1e-6


def rms_norm(x, gain):
    xf = x.astype(jnp.float32)
    y = xf * lax.rsqrt(jnp.mean(xf * xf, axis=-1, keepdims=True) + EPS)
    return (y * gain.astype(jnp.float32)).astype(x.dtype)

def rotary(x, positions):
    half = HEAD_DIM // 2
    inv_freq = ROPE_BASE ** (-jnp.arange(half, dtype=jnp.float32) / half)
    ang = positions.astype(jnp.float32)[..., None] * inv_freq
    cos = jnp.cos(ang)[:, :, None, :]
    sin = jnp.sin(ang)[:, :, None, :]
    x1 = x[..., :half].astype(jnp.float32)
    x2 = x[..., half:].astype(jnp.float32)
    out = jnp.concatenate([x1 * cos - x2 * sin, x2 * cos + x1 * sin], axis=-1)
    return out.astype(x.dtype)

def retention(q, k, v, positions):
    B, S, H, D = q.shape
    C = RET_CHUNK
    NC = S // C
    q = rotary(q, positions)
    k = rotary(k, positions) * (D ** -0.5)
    log_g = jnp.log1p(-(2.0 ** (-5.0 - jnp.arange(H, dtype=jnp.float32))))
    idx = jnp.arange(C, dtype=jnp.float32)
    rel = idx[:, None] - idx[None, :]
    decay_intra = jnp.where(rel >= 0, jnp.exp(log_g[:, None, None] * jnp.maximum(rel, 0.0)), 0.0)
    xi = jnp.exp(log_g[:, None] * (idx + 1.0))
    zeta = jnp.exp(log_g[:, None] * (C - 1.0 - idx))
    chunk_decay = jnp.exp(log_g * C)
    qc = q.reshape(B, NC, C, H, D)
    kc = k.reshape(B, NC, C, H, D)
    vc = v.reshape(B, NC, C, H, D)
    scores = jnp.einsum('bnihd,bnjhd->bnhij', qc, kc) * decay_intra
    y_intra = jnp.einsum('bnhij,bnjhd->bnihd', scores, vc)
    kv = jnp.einsum('bnjhd,hj,bnjhe->nbhde', kc, zeta, vc).astype(jnp.float32)

    def step(state, kv_i):
        return chunk_decay[None, :, None, None] * state + kv_i, state

    _, states = lax.scan(step, jnp.zeros((B, H, D, D), jnp.float32), kv)
    y_cross = jnp.einsum('bnihd,nbhde,hi->bnihe', qc, states, xi)
    return (y_intra + y_cross).reshape(B, S, H, D)

def head_group_norm(y, gain):
    B, S, H, D = y.shape
    yf = y.astype(jnp.float32)
    mu = jnp.mean(yf, axis=-1, keepdims=True)
    var = jnp.mean(jnp.square(yf - mu), axis=-1, keepdims=True)
    yn = (yf - mu) * lax.rsqrt(var + EPS)
    return yn.reshape(B, S, H * D) * gain.astype(jnp.float32)

def stick_breaking(q, k, v):
    B, S, H, D = q.shape
    NB = S // SB_BLOCK
    q_blocks = q.reshape(B, NB, SB_BLOCK, H, D).transpose(1, 0, 3, 2, 4)
    kt = k.transpose(0, 2, 1, 3)
    vt = v.transpose(0, 2, 1, 3)
    key_pos = jnp.arange(S)
    scale = D ** -0.5

    def block(args):
        qi, start = args
        z = jnp.einsum('bhqd,bhsd->bhqs', qi, kt).astype(jnp.float32) * scale
        q_pos = start + jnp.arange(SB_BLOCK)
        mask = key_pos[None, :] < q_pos[:, None]
        log_beta = jax.nn.log_sigmoid(z)
        log_stay = jnp.where(mask, log_beta - z, 0.0)
        log_w = log_beta + lax.cumsum(log_stay, axis=3, reverse=True) - log_stay
        w = jnp.where(mask, jnp.exp(log_w), 0.0)
        return jnp.einsum('bhqs,bhsd->bhqd', w.astype(vt.dtype), vt)

    starts = jnp.arange(NB) * SB_BLOCK
    out = lax.map(block, (q_blocks, starts))
    return out.transpose(1, 0, 3, 2, 4).reshape(B, S, H, D)

def peer(h, w_query, sub_keys, expert_down, expert_up):
    B, S, Dm = h.shape
    T = B * S
    K = PEER_TOPK
    ht = h.reshape(T, Dm)
    qry = (ht @ w_query).reshape(T, PEER_HEADS, 2, PEER_HALF)
    sub_scores = jnp.einsum('thpc,hpkc->thpk', qry, sub_keys).astype(jnp.float32)
    top_s, top_i = lax.top_k(sub_scores, K)
    cand_s = top_s[:, :, 0, :, None] + top_s[:, :, 1, None, :]
    cand_id = top_i[:, :, 0, :, None] * N_KEYS + top_i[:, :, 1, None, :]
    best_s, best_c = lax.top_k(cand_s.reshape(T, PEER_HEADS, K * K), K)
    expert_id = jnp.take_along_axis(cand_id.reshape(T, PEER_HEADS, K * K), best_c, axis=-1)
    gate = jax.nn.softmax(best_s, axis=-1)
    NBK = T // PEER_BLOCK
    ids = expert_id.reshape(NBK, PEER_BLOCK, PEER_HEADS * K)
    gates = gate.reshape(NBK, PEER_BLOCK, PEER_HEADS * K)
    xs = ht.reshape(NBK, PEER_BLOCK, Dm)

    def block(args):
        xb, ib, gb = args
        u = expert_down[ib]
        a = jnp.einsum('pd,ped->pe', xb, u).astype(jnp.float32)
        act = jax.nn.gelu(a, approximate=False) * gb
        v = expert_up[ib]
        return jnp.einsum('pe,ped->pd', act.astype(xb.dtype), v)

    y = lax.map(block, (xs, ids, gates))
    return y.reshape(B, S, Dm)

def first_inputs(seed: int = 0) -> dict:
    key = jax.random.key(seed)
    ks = jax.random.split(key, 16)
    f32 = jnp.float32
    nrm = lambda k, shape, s: jax.random.normal(k, shape, f32) * s
    return {
        "x": nrm(ks[0], (BATCH, SEQ, D_MODEL), 1.0),
        "c": nrm(ks[1], (BATCH, D_MODEL), 1.0),
        "positions": jnp.broadcast_to(jnp.arange(SEQ, dtype=jnp.int32)[None, :], (BATCH, SEQ)),
        "ada_w": nrm(ks[2], (DEPTH, D_MODEL, 6 * D_MODEL), D_MODEL ** -0.5),
        "ada_b": nrm(ks[3], (DEPTH, 6 * D_MODEL), 0.1),
        "norm1_gain": 1.0 + nrm(ks[4], (DEPTH, D_MODEL), 0.1),
        "norm2_gain": 1.0 + nrm(ks[5], (DEPTH, D_MODEL), 0.1),
        "w_in": nrm(ks[6], (DEPTH, D_MODEL, IN_COLS), D_MODEL ** -0.5),
        "ret_norm_gain": 1.0 + nrm(ks[7], (DEPTH, RET_WIDTH), 0.1),
        "sb_q_gain": 1.0 + nrm(ks[8], (DEPTH, HEAD_DIM), 0.1),
        "sb_k_gain": 1.0 + nrm(ks[9], (DEPTH, HEAD_DIM), 0.1),
        "sb_out_gain": 1.0 + nrm(ks[10], (DEPTH, HEAD_DIM), 0.1),
        "w_out": nrm(ks[11], (DEPTH, D_MIX, D_MODEL), D_MIX ** -0.5),
        "peer_w_query": nrm(ks[12], (DEPTH, D_MODEL, PEER_HEADS * PEER_QDIM), D_MODEL ** -0.5),
        "peer_sub_keys": nrm(ks[13], (DEPTH, PEER_HEADS, 2, N_KEYS, PEER_HALF), PEER_HALF ** -0.5),
        "peer_down": nrm(ks[14], (DEPTH, N_EXPERTS, D_MODEL), D_MODEL ** -0.5),
        "peer_up": nrm(ks[15], (DEPTH, N_EXPERTS, D_MODEL), PEER_HEADS ** -0.5),
    }

def first_block(x, c, positions, ada_w, ada_b, norm1_gain, norm2_gain, w_in, ret_norm_gain,
              sb_q_gain, sb_k_gain, sb_out_gain, w_out, peer_w_query, peer_sub_keys,
              peer_down, peer_up):
    B, S, _ = x.shape
    for layer in range(DEPTH):
        mod = jax.nn.silu(c) @ ada_w[layer] + ada_b[layer]
        shift1, scale1, gate1, shift2, scale2, gate2 = jnp.split(mod[:, None, :], 6, axis=-1)

        h = rms_norm(x, norm1_gain[layer]) * (1.0 + scale1) + shift1
        proj = h @ w_in[layer]
        r_q, r_k, r_v, r_g, s_q, s_k, s_v = jnp.split(
            proj, np.cumsum([RET_WIDTH] * 4 + [SB_WIDTH] * 2), axis=-1)
        heads_r = lambda t: t.reshape(B, S, N_RET_HEADS, HEAD_DIM)
        heads_s = lambda t: t.reshape(B, S, N_SB_HEADS, HEAD_DIM)

        y_ret = retention(heads_r(r_q), heads_r(r_k), heads_r(r_v), positions)
        y_ret = head_group_norm(y_ret, ret_norm_gain[layer]) * jax.nn.silu(r_g.astype(jnp.float32))

        q_sb = rms_norm(heads_s(s_q), sb_q_gain[layer])
        k_sb = rms_norm(heads_s(s_k), sb_k_gain[layer])
        y_sb = stick_breaking(q_sb, k_sb, heads_s(s_v))
        y_sb = rms_norm(y_sb, sb_out_gain[layer]).reshape(B, S, SB_WIDTH)

        mixed = jnp.concatenate([y_ret.astype(x.dtype), y_sb.astype(x.dtype)], axis=-1) @ w_out[layer]
        x = x + gate1 * mixed

        h2 = rms_norm(x, norm2_gain[layer]) * (1.0 + scale2) + shift2
        ffn = peer(h2, peer_w_query[layer], peer_sub_keys[layer], peer_down[layer], peer_up[layer])
        x = x + gate2 * ffn
    return x


N_ATTN_HEADS = 8
N_KV_GROUPS = 2
HEADS_PER_GROUP = N_ATTN_HEADS // N_KV_GROUPS
ATTN_WIDTH = N_ATTN_HEADS * HEAD_DIM
CONV_WIDTH = D_MODEL - ATTN_WIDTH
KV_WIDTH = N_KV_GROUPS * HEAD_DIM
N_BRANCH = 3
CMP_BLOCK = 32
CMP_STRIDE = 16
CMP_HIDDEN = 4 * HEAD_DIM
SEL_BLOCK = 64
SEL_TOPK = 16
WINDOW = 512
Q_BLOCK = 128
CONV_K = 3
D_FF = 4 * D_MODEL
IN_WIDTH = ATTN_WIDTH + 6 * KV_WIDTH + N_BRANCH * N_ATTN_HEADS + 3 * CONV_WIDTH
NEG = -1e30
FORCE_BONUS = 1e4


def rms_norm_2(x, g):
    xf = x.astype(jnp.float32)
    y = xf * lax.rsqrt(jnp.mean(xf * xf, axis=-1, keepdims=True) + EPS)
    return (y * g.astype(jnp.float32)).astype(x.dtype)

def alibi_slopes():
    h = np.arange(1, N_ATTN_HEADS + 1, dtype=np.float32)
    s = np.power(np.float32(2.0), -8.0 * h / N_ATTN_HEADS).astype(np.float32)
    return jnp.asarray(s, dtype=jnp.float32).reshape(N_KV_GROUPS, HEADS_PER_GROUP)

def masked_softmax(s, mask):
    s = jnp.where(mask, s, NEG)
    m = jnp.max(s, axis=-1, keepdims=True)
    p = jnp.where(mask, jnp.exp(s - m), 0.0)
    return p / jnp.maximum(jnp.sum(p, axis=-1, keepdims=True), 1e-30)

def cmp_to_sel_matrix(n_cmp, n_sel):
    s0 = jnp.arange(n_cmp)[:, None] * CMP_STRIDE
    s1 = jnp.arange(n_sel)[None, :] * SEL_BLOCK
    shared = jnp.clip(jnp.minimum(s0 + CMP_BLOCK, s1 + SEL_BLOCK) - jnp.maximum(s0, s1), 0, None)
    return shared.astype(jnp.float32) / CMP_BLOCK

def compress(k_raw, pe, w1, b1, w2, b2):
    B, T = k_raw.shape[0], k_raw.shape[1]
    ch = k_raw.reshape(B, T // CMP_STRIDE, CMP_STRIDE, N_KV_GROUPS, HEAD_DIM)
    blk = jnp.concatenate([ch[:, :-1], ch[:, 1:]], axis=2)
    blk = blk + pe[None, None, :, None, :]
    blk = blk.transpose(0, 3, 1, 2, 4).reshape(B, N_KV_GROUPS, -1, CMP_BLOCK * HEAD_DIM)
    hdn = jax.nn.gelu(blk @ w1 + b1)
    return hdn @ w2 + b2

def nsa_attention(q, k_cmp, v_cmp, k_slc, v_slc, k_win, v_win, gates):
    B, T = q.shape[0], q.shape[1]
    G, R, hd = N_KV_GROUPS, HEADS_PER_GROUP, HEAD_DIM
    f32 = jnp.float32
    n_cmp = k_cmp.shape[2]
    n_sel = T // SEL_BLOCK
    n_top = min(SEL_TOPK, n_sel)
    n_qb = T // Q_BLOCK
    slopes = alibi_slopes()[None, :, :, None, None]
    sel_map = cmp_to_sel_matrix(n_cmp, n_sel)
    cmp_end = jnp.arange(n_cmp, dtype=jnp.int32) * CMP_STRIDE + (CMP_BLOCK - 1)
    sel_id = jnp.arange(n_sel, dtype=jnp.int32)
    sel_off = jnp.arange(SEL_BLOCK, dtype=jnp.int32)
    win_off = jnp.arange(Q_BLOCK + WINDOW, dtype=jnp.int32) - WINDOW
    ks_blk = k_slc.reshape(B, n_sel, SEL_BLOCK, G, hd).transpose(0, 3, 1, 2, 4)
    vs_blk = v_slc.reshape(B, n_sel, SEL_BLOCK, G, hd).transpose(0, 3, 1, 2, 4)
    kw_pad = jnp.pad(k_win, ((0, 0), (WINDOW, 0), (0, 0), (0, 0)))
    vw_pad = jnp.pad(v_win, ((0, 0), (WINDOW, 0), (0, 0), (0, 0)))
    q_blocks = (q * (hd ** -0.5)).reshape(B, n_qb, Q_BLOCK, G, R, hd).transpose(1, 0, 3, 4, 2, 5)
    g_blocks = gates.reshape(B, n_qb, Q_BLOCK, G, R, N_BRANCH).transpose(1, 0, 3, 4, 2, 5)
    b_ix = jnp.arange(B)[:, None, None, None]
    g_ix = jnp.arange(G)[None, :, None, None]

    def one_block(args):
        c, qb, gb = args
        q0 = c * Q_BLOCK
        t = q0 + jnp.arange(Q_BLOCK, dtype=jnp.int32)
        s = jnp.einsum('bgrqd,bgid->bgrqi', qb, k_cmp).astype(f32)
        dist = (t[:, None] - cmp_end[None, :]).astype(f32)
        p_cmp = masked_softmax(s - slopes * dist, dist >= 0)
        o_cmp = jnp.einsum('bgrqi,bgid->bgrqd', p_cmp.astype(v_cmp.dtype), v_cmp)
        imp = jnp.einsum('bgrqi,ij->bgqj', p_cmp, sel_map)
        jt = (t // SEL_BLOCK)[:, None]
        forced = (sel_id == 0) | (sel_id == jt) | (sel_id == jt - 1)
        valid = sel_id * SEL_BLOCK <= t[:, None]
        imp = jnp.where(valid, jnp.where(forced, imp + FORCE_BONUS, imp), NEG)
        _, idx = lax.top_k(imp, n_top)
        kg = ks_blk[b_ix, g_ix, idx].reshape(B, G, Q_BLOCK, n_top * SEL_BLOCK, hd)
        vg = vs_blk[b_ix, g_ix, idx].reshape(B, G, Q_BLOCK, n_top * SEL_BLOCK, hd)
        pos = (idx[..., None] * SEL_BLOCK + sel_off).reshape(B, G, Q_BLOCK, n_top * SEL_BLOCK)
        dist = (t[None, None, :, None] - pos).astype(f32)[:, :, None]
        s = jnp.einsum('bgrqd,bgqmd->bgrqm', qb, kg).astype(f32)
        p_slc = masked_softmax(s - slopes * dist, dist >= 0)
        o_slc = jnp.einsum('bgrqm,bgqmd->bgrqd', p_slc.astype(vg.dtype), vg)
        kw = lax.dynamic_slice_in_dim(kw_pad, q0, Q_BLOCK + WINDOW, axis=1)
        vw = lax.dynamic_slice_in_dim(vw_pad, q0, Q_BLOCK + WINDOW, axis=1)
        spos = q0 + win_off
        dist_i = t[:, None] - spos[None, :]
        mask = (spos[None, :] >= 0) & (dist_i >= 0) & (dist_i < WINDOW)
        s = jnp.einsum('bgrqd,bsgd->bgrqs', qb, kw).astype(f32)
        p_win = masked_softmax(s - slopes * dist_i.astype(f32), mask)
        o_win = jnp.einsum('bgrqs,bsgd->bgrqd', p_win.astype(vw.dtype), vw)
        o = gb[..., 0:1] * o_cmp + gb[..., 1:2] * o_slc + gb[..., 2:3] * o_win
        return o.astype(q.dtype)

    out = lax.map(one_block, (jnp.arange(n_qb, dtype=jnp.int32), q_blocks, g_blocks))
    return out.transpose(1, 0, 4, 2, 3, 5).reshape(B, T, N_ATTN_HEADS * hd)

def short_conv_mixer(h, c_gate, b_gate, conv_w):
    u = c_gate * h
    v = lax.conv_general_dilated(u, conv_w[:, None, :], window_strides=(1,),
                                 padding=((CONV_K - 1, 0),),
                                 dimension_numbers=('NWC', 'WIO', 'NWC'),
                                 feature_group_count=CONV_WIDTH)
    return b_gate * v

def second_inputs(seed: int = 0) -> dict:
    key = jax.random.key(seed)
    ks = jax.random.split(key, 16)
    f32 = jnp.float32

    def nrm(k, shape, scale):
        return jax.random.normal(k, shape, f32) * scale

    return {
        'x': nrm(ks[0], (BATCH, SEQ, D_MODEL), 1.0),
        'g_mix_norm': 1.0 + nrm(ks[1], (DEPTH, D_MODEL), 0.02),
        'w_in': nrm(ks[2], (DEPTH, D_MODEL, IN_WIDTH), D_MODEL ** -0.5),
        'g_q': 1.0 + nrm(ks[3], (DEPTH, HEAD_DIM), 0.02),
        'g_k': 1.0 + nrm(ks[4], (DEPTH, N_BRANCH, HEAD_DIM), 0.02),
        'pe_cmp': nrm(ks[5], (DEPTH, 2, CMP_BLOCK, HEAD_DIM), 0.1),
        'w_cmp1': nrm(ks[6], (DEPTH, 2, CMP_BLOCK * HEAD_DIM, CMP_HIDDEN), (CMP_BLOCK * HEAD_DIM) ** -0.5),
        'b_cmp1': nrm(ks[7], (DEPTH, 2, CMP_HIDDEN), 0.01),
        'w_cmp2': nrm(ks[8], (DEPTH, 2, CMP_HIDDEN, HEAD_DIM), CMP_HIDDEN ** -0.5),
        'b_cmp2': nrm(ks[9], (DEPTH, 2, HEAD_DIM), 0.01),
        'conv_w': nrm(ks[10], (DEPTH, CONV_K, CONV_WIDTH), CONV_K ** -0.5),
        'g_out': 1.0 + nrm(ks[11], (DEPTH, D_MODEL), 0.02),
        'w_o': nrm(ks[12], (DEPTH, D_MODEL, D_MODEL), (2 * DEPTH * D_MODEL) ** -0.5),
        'g_ffn_norm': 1.0 + nrm(ks[13], (DEPTH, D_MODEL), 0.02),
        'w_up': nrm(ks[14], (DEPTH, D_MODEL, D_FF), D_MODEL ** -0.5),
        'w_down': nrm(ks[15], (DEPTH, D_FF, D_MODEL), (2 * DEPTH * D_FF) ** -0.5),
    }

def second_block(x, g_mix_norm, w_in, g_q, g_k, pe_cmp, w_cmp1, b_cmp1, w_cmp2, b_cmp2,
              conv_w, g_out, w_o, g_ffn_norm, w_up, w_down):
    B, T = x.shape[0], x.shape[1]
    sizes = [ATTN_WIDTH] + [KV_WIDTH] * 6 + [N_BRANCH * N_ATTN_HEADS] + [CONV_WIDTH] * 3
    offs = [int(o) for o in np.cumsum(sizes)[:-1]]
    kv_shape = (B, T, N_KV_GROUPS, HEAD_DIM)
    for l in range(DEPTH):
        h = rms_norm_2(x, g_mix_norm[l])
        z = h @ w_in[l]
        q, kc, vc, ks_, vs_, kw_, vw_, gl, hc, cg, bg = jnp.split(z, offs, axis=-1)
        q = rms_norm_2(q.reshape(B, T, N_ATTN_HEADS, HEAD_DIM), g_q[l])
        k_cmp = rms_norm_2(compress(kc.reshape(kv_shape), pe_cmp[l, 0], w_cmp1[l, 0], b_cmp1[l, 0],
                                  w_cmp2[l, 0], b_cmp2[l, 0]), g_k[l, 0])
        v_cmp = compress(vc.reshape(kv_shape), pe_cmp[l, 1], w_cmp1[l, 1], b_cmp1[l, 1],
                         w_cmp2[l, 1], b_cmp2[l, 1])
        k_slc = rms_norm_2(ks_.reshape(kv_shape), g_k[l, 1])
        k_win = rms_norm_2(kw_.reshape(kv_shape), g_k[l, 2])
        gates = jax.nn.sigmoid(gl).reshape(B, T, N_ATTN_HEADS, N_BRANCH)
        attn_out = nsa_attention(q, k_cmp, v_cmp, k_slc, vs_.reshape(kv_shape),
                                 k_win, vw_.reshape(kv_shape), gates)
        conv_out = short_conv_mixer(hc, cg, bg, conv_w[l])
        mixed = jnp.concatenate([rms_norm_2(attn_out, g_out[l, :ATTN_WIDTH]),
                                 rms_norm_2(conv_out, g_out[l, ATTN_WIDTH:])], axis=-1)
        x = x + mixed @ w_o[l]
        h = rms_norm_2(x, g_ffn_norm[l])
        x = x + jnp.square(jax.nn.relu(h @ w_up[l])) @ w_down[l]
    return x


def setup_inputs(seed=0):
    out = dict(first_inputs(seed))
    for name, value in second_inputs(seed + 1).items():
        if name != "x":
            out[name + "_2"] = value
    return out


def reference(
    x, c, positions, ada_w, ada_b, norm1_gain, norm2_gain, w_in, ret_norm_gain, sb_q_gain,
    sb_k_gain, sb_out_gain, w_out, peer_w_query, peer_sub_keys, peer_down, peer_up,
    g_mix_norm_2, w_in_2, g_q_2, g_k_2, pe_cmp_2, w_cmp1_2, b_cmp1_2, w_cmp2_2, b_cmp2_2,
    conv_w_2, g_out_2, w_o_2, g_ffn_norm_2, w_up_2, w_down_2,
):
    x = first_block(
        x, c, positions, ada_w, ada_b, norm1_gain, norm2_gain, w_in, ret_norm_gain, sb_q_gain,
        sb_k_gain, sb_out_gain, w_out, peer_w_query, peer_sub_keys, peer_down, peer_up,
    )
    return second_block(
        x, g_mix_norm_2, w_in_2, g_q_2, g_k_2, pe_cmp_2, w_cmp1_2, b_cmp1_2, w_cmp2_2, b_cmp2_2,
        conv_w_2, g_out_2, w_o_2, g_ffn_norm_2, w_up_2, w_down_2,
    )


_drawn_inputs = setup_inputs


def setup_inputs(seed=0):
    import zlib

    import numpy as np

    out = dict(_drawn_inputs(seed))
    spreads = {}
    factors = {'g_mix_norm_2': 3.368,
     'g_q_2': 8.0,
     'g_k_2': 8.0,
     'b_cmp1_2': 8.0,
     'b_cmp2_2': 38.911,
     'g_out_2': 4.856,
     'g_ffn_norm_2': 4.425}
    for name, (base, spread) in spreads.items():
        noise = np.random.default_rng([zlib.crc32(name.encode()), seed]).standard_normal(out[name].shape)
        drawn = base * np.exp(spread * noise) if base else spread * noise
        out[name] = __import__('jax').numpy.asarray(drawn.astype(out[name].dtype))
    for name, factor in factors.items():
        out[name] = (out[name] * factor).astype(out[name].dtype)
    return out
```

```python
from contextlib import ExitStack

import numpy as np

import concourse.bass as bass
from concourse import mybir

ALU = mybir.AluOpType
ACT = mybir.ActivationFunctionType
AX = mybir.AxisListType
F32 = mybir.dt.float32
U32 = mybir.dt.uint32
I32 = mybir.dt.int32

P = 128
NB = 2
T = NB * P
D = 1024
KC = D // P
HD = 64
NH = 8
HW = NH * HD
CHUNK = 512
SLOT = KC * CHUNK
RING = 3
EPS = 1e-6

PH = 8
PK = 16
NKEY = 128
GR = 8

NCMP = 15
CMPW = 32
CSTEP = 16
NPAIR = CMPW // 2
CF = 256
NG = 2
R = NH // NG
ZW = 2840
DFF = 4096

Z_Q, Z_KC, Z_VC, Z_KS, Z_VS, Z_KW, Z_VW, Z_G, Z_H, Z_C, Z_B = (
    0, 512, 640, 768, 896, 1024, 1152, 1280, 1304, 1816, 2328)

PAIRS = [(0, 0), (0, 1), (1, 1)]

TWO_PI = 2.0 * np.pi
MAGIC = 1.5 * 2.0 ** 23
C1 = 6.28125
C2 = float(np.float32(TWO_PI - C1))
C3 = float(np.float32(TWO_PI - C1 - np.float64(np.float32(TWO_PI - C1))))
FAR = -1e32

CONST = {}


def constants():
    i = np.arange(P)
    parts = {
        "ident": np.eye(P),
        "after": i[:, None] > i[None, :],
        "before": i[:, None] < i[None, :],
        "ones": np.ones((P, P)),
    }
    dist = np.empty((P, NB, T))
    cdist = np.empty((P, NB, CSTEP))
    for b in range(NB):
        t = b * P + i
        far = t[:, None] - np.arange(T)[None, :]
        dist[:, b] = np.where(far >= 0, -far, FAR)
        far = t[:, None] - (np.arange(CSTEP) * CSTEP + CMPW - 1)[None, :]
        cdist[:, b] = np.where(far >= 0, -far, FAR)
    parts["dist"] = dist
    parts["cdist"] = cdist
    parts["cmask"] = cdist > FAR
    half = HD // 2
    parts["freq"] = np.tile(np.float32(10000.0) ** (-np.arange(half, dtype=np.float32) / np.float32(half)), (P, 1))
    parts["iota"] = np.tile(np.arange(PK), (P, 1))
    for k in (1, 2):
        parts[f"shift{k}"] = i[:, None] == i[None, :] - k
        parts[f"carry{k}"] = i[:, None] == i[None, :] + P - k
    at, out = 0, []
    for name, a in parts.items():
        a = np.asarray(a, np.float32).reshape(P, -1)
        CONST[name] = (at, at + a.shape[1])
        at += a.shape[1]
        out.append(a)
    return np.ascontiguousarray(np.concatenate(out, 1))


def decay_table():
    i = np.arange(P, dtype=np.float64)
    log_g = np.log1p(-(2.0 ** (-5.0 - np.arange(NH))))
    rel = i[None, :] - i[:, None]
    table = np.empty((P, 2, NH, P))
    for h in range(NH):
        table[:, 0, h] = np.where(rel >= 0, np.exp(log_g[h] * np.maximum(rel, 0)), 0)
        table[:, 1, h] = np.exp(log_g[h] * (P + rel))
    return (table * HD ** -0.5).astype(np.float32).reshape(P, -1)


STREAM = (
    [("ada", j, "act") for j in range(4)] + [("win", j, "act") for j in range(7)]
    + [("ada", j, "act") for j in range(4, 10)] + [("wout", j, "dve") for j in range(2)]
    + [("ada", j, "act") for j in range(10, 12)] + [("wq", j, "act") for j in range(4)]
    + [("keys", 0, None)] + [("win2", j, "act") for j in range(6)]
    + [("cmp", j, None) for j in range(2)] + [("wo", j, "dve") for j in range(2)]
    + [("up", 0, "act")]
    + [x for j in range(1, 8) for x in (("up", j, "act"), ("down", j - 1, None))] + [("down", 7, None)]
)
NTH = {(k, j): n for n, (k, j, _) in enumerate(STREAM)}


def emptied():
    found, count, place = {}, {"act": 0, "dve": 0}, 0
    for n, (_, _, who) in enumerate(STREAM):
        if who:
            count[who] += 1
            found[n] = (place, who, count[who])
            place += 1
    return found


EMPTIED = emptied()
BY_PLACE = {p: (who, c) for p, who, c in EMPTIED.values()}


class Chain:

    def __init__(self, eng, sem):
        self.eng, self.sem, self.n = eng, sem, 0

    def __call__(self, ins):
        self.n += 1
        ins.then_inc(self.sem, 1)
        self.eng.wait_ge(self.sem, self.n)

    def restart(self):
        self.eng.sem_clear(self.sem)
        self.n = 0


def two_blocks(nc, a, out, stop=None):
    ctx = ExitStack()
    with ctx:
        def sb(name, shape, dt=F32):
            return ctx.enter_context(nc.sbuf_tensor(name, shape, dt))

        def sem(name):
            return ctx.enter_context(nc.semaphore(name))

        n_const = a["const"].shape[1]
        const = sb("const", [P, n_const])
        x_tok = sb("x_tok", [P, NB, D])
        h_tok = sb("h_tok", [P, NB, D])
        hT = sb("hT", [P, KC, T])
        mod = sb("mod", [P, 4, D])
        gain1 = sb("gain1", [P, 2, D])
        late = sb("late", [P, 4608])
        small = sb("small", [P, 7, HD])
        wring = sb("wring", [P, RING, SLOT])
        arena = sb("arena", [P, 18560])
        csilu = sb("csilu", [P, 2, KC])
        adab = sb("adab", [12, CHUNK])
        posi = sb("posi", [P, NB], I32)
        posf = sb("posf", [P, NB])
        st = sb("st", [P, 10, 16])
        cbias = sb("cbias", [P, 2, 2])
        w2 = sb("w2", [P, 2, 2, HD])
        b2 = sb("b2", [1, 2, HD])
        ps = ctx.enter_context(nc.psum_tensor("ps", [P, 8, 512], F32))
        psf = ps[:, :, :].rearrange("p b n -> p (b n)")

        def con(name, *dims):
            lo, hi = CONST[name]
            v = const[:, lo:hi]
            return v

        ident, ones = con("ident"), con("ones")
        SHIFT, SCALE, GATE1, GATE2 = (mod[:, k, :] for k in range(4))

        proj = arena[:, 0:NB * 3584].rearrange("p (b n) -> p b n", b=NB)
        qT = arena[:, 7168:8192].rearrange("p (c t) -> p c t", c=4)
        kT = arena[:, 8192:9216].rearrange("p (c t) -> p c t", c=4)
        tiles = arena[:, 9216:18432].rearrange("p (k n) -> p k n", k=6)
        trig = arena[:, 18432:18560].rearrange("p (f b n) -> p f b n", f=2, b=NB)
        ang = tiles[:, 0, 0:64].rearrange("p (b n) -> p b n", b=NB)
        turns = tiles[:, 0, 64:192].rearrange("p (f b n) -> p f b n", f=2, b=NB)
        ang2 = tiles[:, 0, 192:320].rearrange("p (f b n) -> p f b n", f=2, b=NB)
        decay = late[:, 0:2048].rearrange("p (k h i) -> p k h i", k=2, h=NH)
        rgain = late[:, 2048:2560]

        def heads(v):
            return v.rearrange("p b (h d) -> p b h d", d=HD)

        def every_other(v, par):
            return v.rearrange("p (h u d) -> p u h d", u=2, d=HD)[:, par, :, :]

        qryT = arena[:, 0:16 * T].rearrange("p (c t) -> p c t", c=16)
        downs = arena[:, 0:GR * D].rearrange("p (s n) -> p s n", s=GR)
        ups = arena[:, GR * D:2 * GR * D].rearrange("p (s n) -> p s n", s=GR)
        score = late[:, 0:17 * 256].rearrange("p (c n) -> p c n", n=256)
        sc2 = sb("sc2", [P, 256])
        top = sb("top", [P, 2, PK])
        topi = sb("topi", [P, 2, PK], U32)
        topf = sb("topf", [P, 2, PK])
        cand = sb("cand", [P, PK, PK])
        cand2 = sb("cand2", [P, PK * PK])
        best = sb("best", [P, PK])
        besti = sb("besti", [P, 3, PK], U32)
        bestf = sb("bestf", [P, 2, PK])
        pick = sc2[:, :].rearrange("p (i j) -> p i j", i=PK)
        picked = sb("picked", [P, 2, PK])
        ids = sb("ids", [P, 2, PK], U32)
        ex = sb("ex", [P, 2, PK])
        exs = sb("exs", [P, 2])
        dots = sb("dots", [P, 2, PK])
        actw = sb("actw", [P, 2, PK])
        diag = sb("diag", [P, 4, P])
        first = sb("first", [P, 1])

        z = arena[:, 0:NB * ZW].rearrange("p (b n) -> p b n", b=NB)
        o = NB * ZW
        qT2 = arena[:, o:o + 1024].rearrange("p (c t) -> p c t", c=4)
        kT2 = arena[:, o + 1024:o + 2048].rearrange("p (r g t) -> p r g t", r=2, g=NG)
        kvA = arena[:, o + 2048:o + 3072].rearrange("p (v g t) -> p v g t", v=2, g=NG)
        blkT = arena[:, o + 3072:o + 4032].rearrange("p (v m c) -> p v m c", v=2, m=NPAIR)
        hdnT = arena[:, o + 4032:o + 4160].rearrange("p (f c) -> p f c", f=2)
        o += 4288
        ptile = arena[:, o:o + 3072].rearrange("p (k n) -> p k n", k=2)
        pT = arena[:, o + 3072:o + 4608].rearrange("p (k r t) -> p k r t", k=3, r=R)
        kdup = arena[:, o:o + 1024].rearrange("p (b r g u d) -> p b r g u d", b=NB, r=2, g=NG, u=2)
        o += 4608
        sh1 = arena[:, o:o + 1024].rearrange("p (b n) -> p b n", b=NB)
        sh2 = arena[:, o + 1024:o + 2048].rearrange("p (b n) -> p b n", b=NB)
        tmp = arena[:, o + 2048:o + 3072].rearrange("p (b n) -> p b n", b=NB)
        kvdup = arena[:, o + 2048:o + 3072].rearrange("p (b v g u d) -> p b v g u d", b=NB, v=2, g=NG, u=2)
        hdnV = arena[:, o + 3072:o + 3584].rearrange("p (f g r n) -> p f g r n", f=2, g=NG, r=R)
        assert o + 3584 <= 18560
        gmix, gout, gffn = (late[:, k * D:(k + 1) * D] for k in range(3))
        convw = late[:, 3 * D:3 * D + 3 * HW].rearrange("p (k n) -> p k n", k=3)
        gatec = sb("gatec", [P, NB, NH, 3])
        mx = sb("mx", [P, 2, NB, R])
        sm = sb("sm", [P, 2, NB, R])
        kcn = sb("kcn", [64, 2, HD])
        kcq = sb("kcq", [64, HD])
        kcst = sb("kcst", [64, 4])
        kcmpT = sb("kcmpT", [P, 64])
        spare = gain1[:, :, :].rearrange("p k n -> p (k n)")
        vbd = spare[:, 0:512].rearrange("p (g r d) -> p g r d", g=NG, r=R)
        pcmp = spare[:, 512:1024].rearrange("p (b h n) -> p b h n", b=NB, h=NH)
        pcT = spare[:, 1024:1536].rearrange("p (b g t) -> p b g t", b=NB, g=NG)
        pcs = spare[:, 1536:1792].rearrange("p (c n) -> p c n", n=CSTEP)
        cst = spare[:, 1792:1840].rearrange("p (k c) -> p k c", k=3)
        peT = sb("peT", [P, 2, NPAIR])
        uT = arena[:, 0:3 * 1024].rearrange("p (s f t) -> p s f t", s=3, f=4)

        ld_const, ld_x, ld_c, ld_gain, ld_early, ld_late, ld_cmp = (
            sem(s) for s in ("ld_const", "ld_x", "ld_c", "ld_gain", "ld_early", "ld_late", "ld_cmp"))
        w_in_slot = [sem(f"w_in_slot{k}") for k in range(RING)]
        w_used = sem("w_used")
        emptied_by = {"act": sem("emptied_by_act"), "dve": sem("emptied_by_dve")}
        dve_own, act_own, pool_own = sem("dve_own"), sem("act_own"), sem("pool_own")
        names = """silu_c sumsq var std h_ready tr_done tr_copied_act tr_copied_dve angles trig_ready
        rot_ready ret_scores ret_decayed ret_y ret_y_out ret_gate var_s std_s sbq_ready sb_z sb_abs sb_exp sb_L sb_ls sb_cum
        sb_logw sb_w sb_y sb_y_out y_ready x1_ready qry_ready sub_done sub_out
        down_free up_free gelu_done actw_ready diag_ready ids_ready ids_used dmax exp_done peer_done x2_ready
        late_free ksum zrms zstd kv_ready kv_copied blk_ready hdn hdn_out kcmp kvar kstd kcn_ready vcmp_out kct_copied
        s_done s_max p_ready p_masked p_sum pt_done pt_out o_done o_out cs_done c_max c_exp c_ready c_tr c_out co_done co_out
        u_ready u_shifted u_copied conv_out fvar fstd relu_done u2_ready fin x_out stored gathers dve_step""".split()
        S = {n: sem(n) for n in names}
        ring_down = [sem(f"down_in_slot{k}") for k in range(GR)]
        ring_up = [sem(f"up_in_slot{k}") for k in range(GR)]

        block = ctx.enter_context(nc.Block())

        def emptied_count(kind, j):
            return EMPTIED[NTH[kind, j]][2]

        def pair(kind, j):
            return 2 * (EMPTIED[NTH[kind, j]][0] % 2)

        def through(kind, j):
            return NTH[kind, j] + 1

        @block.sync
        def _(sp):
            sp.dma_start(csilu[:, 0, :], a["c"]).then_inc(ld_c, 16)
            sp.dma_start(adab[:, :], a["ada_b"]).then_inc(ld_c, 16)
            sp.dma_start(const[:, :], a["const"]).then_inc(ld_const, 16)
            sp.dma_start(x_tok[:, :, :], a["x"].rearrange("(b p) n -> p b n", p=P)).then_inc(ld_x, 16)
            sp.dma_start(posi[:, :], a["positions"].rearrange("(b p) -> p b", p=P),
                         allow_slow_non_contiguous=True).then_inc(ld_x, 16)

            def weights(n):
                kind, j, _ = STREAM[n]
                slot = wring[:, n % RING, :]
                if n >= RING:
                    sp.wait_ge(w_used, n - RING + 1)
                cols = slice(j * CHUNK, (j + 1) * CHUNK)
                if kind == "keys":
                    src, dst = a["keys"], slot[:, 0:16 * P]
                elif kind == "cmp":
                    src = a["w_cmp1"][j].rearrange("(m p) n -> p m n", p=P)
                    dst = slot.rearrange("p (m n) -> p m n", n=CF)
                elif kind == "down":
                    src = a["w_down"][cols, :].rearrange("(f p) n -> p f n", p=P)
                    dst = slot.rearrange("p (f n) -> p f n", n=D)
                else:
                    w = a[{"ada": "ada_w", "win": "w_in", "wout": "w_out", "wq": "w_query", "win2": "w_in2",
                           "wo": "w_o", "up": "w_up"}[kind]]
                    last = min((j + 1) * CHUNK, w.shape[1])
                    src = w[:, j * CHUNK:last].rearrange("(k p) n -> p k n", p=P)
                    dst = slot.rearrange("p (k n) -> p k n", k=KC)[:, :, 0:last - j * CHUNK]
                sp.dma_start(dst, src).then_inc(w_in_slot[n % RING], 16)

            for n in range(RING):
                weights(n)
            sp.dma_start(gain1[:, 0, :], a["gain1"].partition_broadcast(P)).then_inc(ld_gain, 16)
            sp.dma_start(gain1[:, 1, :], a["gain2"].partition_broadcast(P)).then_inc(ld_gain, 16)
            sp.dma_start(late[:, 0:2048], a["decay"]).then_inc(ld_early, 16)
            sp.dma_start(rgain, a["ret_gain"].partition_broadcast(P)).then_inc(ld_early, 16)
            for k, name in enumerate(("sb_q", "sb_k", "sb_out", "g_q")):
                sp.dma_start(small[:, k, :], a[name].partition_broadcast(P)).then_inc(ld_early, 16)
            sp.dma_start(small[:, 4:7, :].rearrange("p k d -> p (k d)"),
                         a["g_k"].partition_broadcast(P)).then_inc(ld_early, 16)
            sp.dma_start(peT[:, :, :], a["pe"]).then_inc(ld_cmp, 16)
            sp.dma_start(cbias[:, :, :], a["b_cmp1"]).then_inc(ld_cmp, 16)
            sp.dma_start(w2[:, :, :, :], a["w_cmp2"].rearrange("v (f p) d -> p v f d", p=P)).then_inc(ld_cmp, 16)
            sp.dma_start(b2[:, :, :], a["b_cmp2"]).then_inc(ld_cmp, 16)
            first_late = NTH["win2", 0]
            for n in range(RING, first_late + RING):
                weights(n)
            sp.wait_ge(S["late_free"], 1)
            for k, name in enumerate(("g_mix", "g_out", "g_ffn")):
                sp.dma_start(late[:, k * D:(k + 1) * D], a[name].partition_broadcast(P)).then_inc(ld_late, 16)
            sp.dma_start(late[:, 3 * D:3 * D + 3 * HW], a["conv_w"].partition_broadcast(P)).then_inc(ld_late, 16)
            for n in range(first_late + RING, len(STREAM)):
                weights(n)
            for b in range(NB):
                sp.wait_ge(S["x_out"], b + 1)
                sp.dma_start(out[b * P:(b + 1) * P, :], x_tok[:, b, :]).then_inc(S["stored"], 16)
            sp.wait_ge(S["stored"], 16 * NB)

        @block.tensor
        def _(pe):
            def slot(n, inner):
                pe.wait_ge(w_in_slot[n % RING], 16 * (n // RING + 1))
                return wring[:, n % RING, :].rearrange("p (k n) -> p k n", n=inner)

            def free_banks(n):
                place = EMPTIED[n][0]
                if place >= 2:
                    who, count = BY_PLACE[place - 2]
                    pe.wait_ge(emptied_by[who], count)
                return 2 * (place % 2)

            def ada(j):
                n = NTH["ada", j]
                w, bank = slot(n, CHUNK), free_banks(n)
                for k in range(KC):
                    pe.matmul(ps[:, bank, :], csilu[:, 1, k:k + 1].to_broadcast([P, P]), w[:, k, :],
                              start=(k == 0), stop=False)
                pe.matmul(ps[:, bank, :], ident[0:12, j:j + 1].to_broadcast([12, P]), adab[:, :],
                          start=False, stop=True).then_inc(w_used, 1)

            def by_tokens(kind, j, cols=CHUNK):
                n = NTH[kind, j]
                w, bank = slot(n, CHUNK), free_banks(n)
                for b in range(NB):
                    for k in range(KC):
                        mm = pe.matmul(ps[:, bank + b, 0:cols], hT[:, k, b * P:(b + 1) * P], w[:, k, 0:cols],
                                       start=(k == 0), stop=(k == KC - 1))
                mm.then_inc(w_used, 1)

            def by_columns(kind, j):
                n = NTH[kind, j]
                w, bank = slot(n, CHUNK), free_banks(n)
                for f in range(4):
                    at = bank * 512 + f * T
                    for k in range(KC):
                        mm = pe.matmul(psf[:, at:at + T], w[:, k, f * P:(f + 1) * P], hT[:, k, :],
                                       start=(k == 0), stop=(k == KC - 1))
                mm.then_inc(w_used, 1)

            def turn_round(src, what):
                for k in range(what):
                    for b in range(NB):
                        at = 4 * 512 + k * T + b * P
                        mm = pe.transpose(psf[:, at:at + P], src(k, b), ident)
                mm.then_inc(S["tr_done"], 1)

            def copied(r):
                pe.wait_ge(S["tr_copied_act"], r)
                pe.wait_ge(S["tr_copied_dve"], r)

            def head_scores(bank, b4):
                for n, (jb, ib) in enumerate(PAIRS):
                    for c in range(4):
                        lo = HD * b4
                        mm = pe.matmul(ps[:, bank + n, c * P:(c + 1) * P], kT[lo:lo + HD, c, jb * P:(jb + 1) * P],
                                       qT[lo:lo + HD, c, ib * P:(ib + 1) * P], start=True, stop=True)
                return mm

            def head_values(bank, tile, v, b4):
                for hh in range(4):
                    col = (2 * hh + b4) * HD
                    w = [tile[:, n * 512 + hh * P:n * 512 + (hh + 1) * P] for n in range(3)]
                    pe.matmul(ps[:, bank, hh * HD:(hh + 1) * HD], w[0], v[:, 0, col:col + HD], start=True, stop=True)
                    at = 4 * HD + hh * HD
                    pe.matmul(ps[:, bank, at:at + HD], w[1], v[:, 0, col:col + HD], start=True, stop=False)
                    mm = pe.matmul(ps[:, bank, at:at + HD], w[2], v[:, 1, col:col + HD], start=False, stop=True)
                return mm

            pe.wait_ge(ld_const, 16)
            pe.wait_ge(ld_c, 32)
            pe.wait_ge(S["silu_c"], 1)
            for j in range(4):
                ada(j)
            pe.wait_ge(S["h_ready"], 2)
            turn_round(lambda k, b: h_tok[:, b, k * P:(k + 1) * P], KC)
            copied(1)
            for j in range(7):
                by_tokens("win", j)
            ada(4)

            pe.wait_ge(S["rot_ready"], 2)
            turn_round(lambda k, b: h_tok[:, b, k * P:(k + 1) * P], KC)
            ada(5)
            copied(2)
            head_scores(4, 0).then_inc(S["ret_scores"], 1)
            ada(6)
            pe.wait_ge(S["ret_decayed"], 1)
            head_scores(4, 1).then_inc(S["ret_scores"], 1)
            pe.wait_ge(emptied_by["act"], emptied_count("win", 2))
            head_values(7, tiles[:, 0, :], proj[:, :, 2 * HW:3 * HW], 0).then_inc(S["ret_y"], 1)
            ada(7)
            pe.wait_ge(S["ret_decayed"], 2)
            pe.wait_ge(S["ret_y_out"], 1)
            head_values(7, tiles[:, 1, :], proj[:, :, 2 * HW:3 * HW], 1).then_inc(S["ret_y"], 1)
            ada(8)

            pe.wait_ge(S["sbq_ready"], 2)
            pe.wait_ge(S["ret_y_out"], 2)
            turn_round(lambda k, b: proj[:, b, (4 * HW + k * P):(4 * HW + (k + 1) * P)], KC)
            ada(9)
            copied(3)
            pe.wait_ge(emptied_by["act"], emptied_count("ada", 9))
            for b4 in range(2):
                head_scores(4 - 4 * b4, b4).then_inc(S["sb_z"], 1)
            for b4 in range(2):
                bank, ls = 4 - 4 * b4, tiles[:, 3 * b4 + 2, :].rearrange("p (k n) -> p k n", k=3)
                pe.wait_ge(S["sb_ls"], b4 + 1)
                pe.matmul(ps[:, bank, :], con("after"), ls[:, 0, :], start=True, stop=True)
                pe.matmul(ps[:, bank + 1, :], con("after"), ls[:, 1, :], start=True, stop=False)
                pe.matmul(ps[:, bank + 1, :], ones, ls[:, 2, :], start=False, stop=True)
                pe.matmul(ps[:, bank + 2, :], con("after"), ls[:, 2, :], start=True, stop=True)\
                    .then_inc(S["sb_cum"], 1)
            for b4 in range(2):
                pe.wait_ge(S["sb_w"], b4 + 1)
                head_values(7 - 4 * b4, tiles[:, 3 * b4 + 1, :], proj[:, :, 6 * HW:7 * HW], b4)\
                    .then_inc(S["sb_y"], 1)
            pe.wait_ge(S["y_ready"], 2)
            turn_round(lambda k, b: proj[:, b, k * P:(k + 1) * P], KC)
            copied(4)
            for j in range(2):
                by_tokens("wout", j)
            for j in (10, 11):
                ada(j)

            pe.wait_ge(S["h_ready"], 4)
            turn_round(lambda k, b: h_tok[:, b, k * P:(k + 1) * P], KC)
            copied(5)
            for j in range(4):
                by_columns("wq", j)
            n = NTH["keys", 0]
            keys = slot(n, NKEY)
            pe.wait_ge(emptied_by["act"], emptied_count("wq", 3))
            for b in range(NB):
                for c in range(16):
                    at = (4 - 4 * b) * 512 + c * NKEY
                    mm = pe.matmul(psf[:, at:at + NKEY], qryT[:, c, b * P:(b + 1) * P], keys[:, c, :],
                                   start=True, stop=True)
                mm.then_inc(S["sub_done"], 1)
            pe.wait_ge(S["sub_out"], 2)
            pe.sem_inc(w_used, 1)

            zeros = score[0:1, 2 * PH, :]
            for bank in range(4):
                pe.matmul(ps[:, bank, 0:256], ones[0:1, :], zeros, start=True, stop=False, skip_group_check=True)
            for b in range(NB):
                with pe.Fori(0, PH // 2) as turn:
                    for par in range(2):
                        head = turn * 2 + (PH * b + par)
                        for k in range(PK):
                            pe.wait_ge(S["diag_ready"], head * PK + (k + 1))
                            pe.wait_ge(ring_up[k % GR], head * 32 + 16 * (k // GR + 1))
                            for half in range(2):
                                mm = pe.matmul(ps[:, 2 * b + half, :], diag[:, k % 4, :],
                                               ups[:, k % GR, half * 512:(half + 1) * 512],
                                               start=False, stop=False, skip_group_check=True)
                            mm.then_inc(S["up_free"], 1)

            pe.wait_ge(S["h_ready"], 6)
            turn_round(lambda k, b: h_tok[:, b, k * P:(k + 1) * P], KC)
            copied(6)
            pe.wait_ge(S["peer_done"], 2)
            for j in range(6):
                by_tokens("win2", j, min(CHUNK, ZW - j * CHUNK))

            pe.wait_ge(S["kv_ready"], 1)
            turn_round(lambda k, b: z[:, b, k * P:(k + 1) * P] if k < 4 else
                       kdup[:, b, (k - 4) // 2, (k - 4) % 2, :, :].rearrange("p u d -> p (u d)"), KC)
            copied(7)

            def scores(i):
                br, lo = i // 2, HD * (i % 2)
                for r in range(R):
                    for b in range(NB):
                        at = 4 * 512 + (r * P if b == 0 else 512 + r * T)
                        mm = pe.matmul(psf[:, at:at + (b + 1) * P], qT2[lo:lo + HD, r, b * P:(b + 1) * P],
                                       kT2[lo:lo + HD, br, r // 2, 0:(b + 1) * P], start=True, stop=True)
                mm.then_inc(S["s_done"], 1)

            def weigh(i):
                br, pt = i // 2, ptile[:, i % 2, :]
                pe.wait_ge(S["p_ready"], i + 1)
                for n, (jb, ib) in enumerate(PAIRS):
                    for r in range(R):
                        lo = r * P if ib == 0 else 512 + r * T + jb * P
                        at = (4 + n) * 512 + r * P
                        mm = pe.transpose(psf[:, at:at + P], pt[:, lo:lo + P], ident)
                mm.then_inc(S["pt_done"], 1)
                pe.wait_ge(S["pt_out"], i + 1)
                if i >= 1:
                    pe.wait_ge(S["o_out"], i)
                for r in range(R):
                    col = (Z_VS, Z_VW)[br] + (r // 2) * HD
                    v = [z[:, b, col:col + HD] for b in range(NB)]
                    pe.matmul(ps[:, 7, r * HD:(r + 1) * HD], pT[:, 0, r, :], v[0], start=True, stop=True)
                    at = (R + r) * HD
                    pe.matmul(ps[:, 7, at:at + HD], pT[:, 1, r, :], v[0], start=True, stop=False)
                    mm = pe.matmul(ps[:, 7, at:at + HD], pT[:, 2, r, :], v[1], start=False, stop=True)
                mm.then_inc(S["o_done"], 1)

            scores(0)
            pe.wait_ge(S["u_ready"], 1)
            pe.wait_ge(emptied_by["act"], emptied_count("win2", 5))
            for k in (1, 2):
                for b in range(NB):
                    bank = 2 * (k - 1) + b
                    mm = pe.matmul(ps[:, bank, :], con(f"shift{k}"), z[:, b, Z_H:Z_H + HW], start=True, stop=(b == 0))
                    if b:
                        mm = pe.matmul(ps[:, bank, :], con(f"carry{k}"), z[:, 0, Z_H:Z_H + HW], start=False, stop=True)
            mm.then_inc(S["u_shifted"], 1)
            weigh(0)
            pe.wait_ge(S["pt_out"], 1)
            scores(1)

            pe.wait_ge(S["kv_ready"], 2)
            pe.wait_ge(S["u_copied"], 1)
            for v in range(2):
                for g in range(NG):
                    for b in range(NB):
                        at = (v * NG + g) * T + b * P
                        mm = pe.transpose(psf[:, at:at + P],
                                          kvdup[:, b, v, g, :, :].rearrange("p u d -> p (u d)"), ident)
            mm.then_inc(S["c_tr"], 1)
            pe.wait_ge(S["blk_ready"], 1)
            for v in range(2):
                w = slot(NTH["cmp", v], CF)
                for f in range(2):
                    at = 2 * 512 + (2 * v + f) * 32
                    for m in range(NPAIR):
                        mm = pe.matmul(psf[:, at:at + 2 * NCMP], w[:, m, f * P:(f + 1) * P], blkT[:, v, m, :],
                                       start=(m == 0), stop=(m == NPAIR - 1))
                mm.then_inc(w_used, 1)
            weigh(1)
            pe.wait_ge(S["pt_out"], 2)
            scores(2)
            pe.wait_ge(S["hdn_out"], 1)
            pe.wait_ge(ld_cmp, 64)
            for f in range(2):
                pe.matmul(ps[0:64, 3, 0:HD], hdnT[:, f, :], w2[:, 0, f, :], start=(f == 0), stop=False)
            pe.matmul(ps[0:64, 3, 0:HD], ones[0:1, 0:64], b2[:, 0, :], start=False, stop=True).then_inc(S["kcmp"], 1)
            for g in range(NG):
                for f in range(2):
                    pe.matmul(ps[:, 0, g * HD:(g + 1) * HD],
                              hdnV[:, f, g, :, :].rearrange("p r n -> p (r n)"),
                              w2[:, 1, f, :], start=(f == 0), stop=False)
                mm = pe.matmul(ps[:, 0, g * HD:(g + 1) * HD], ones[0:1, :], b2[:, 1, :], start=False, stop=True)
            mm.then_inc(S["kcmp"], 1)
            pe.wait_ge(S["kcn_ready"], 1)
            pe.transpose(ps[:, 3, 128:192], kcn[:, :, :].rearrange("p u d -> p (u d)"), ident[0:64, 0:64])\
                .then_inc(S["c_tr"], 1)
            weigh(2)
            pe.wait_ge(S["pt_out"], 3)
            scores(3)
            pe.wait_ge(S["kct_copied"], 1)
            for b in range(NB):
                for h in range(NH):
                    lo, g = HD * (h % 2), h // R
                    at = (2 - h % 2) * 512 + (b * R + h // 2) * CSTEP
                    mm = pe.matmul(psf[:, at:at + CSTEP], qT2[lo:lo + HD, h // 2, b * P:(b + 1) * P],
                                   kcmpT[lo:lo + HD, g * 32:g * 32 + CSTEP], start=True, stop=True)
            mm.then_inc(S["cs_done"], 1)
            weigh(3)
            pe.wait_ge(S["c_ready"], 1)
            for b in range(NB):
                for g in range(NG):
                    at = 3 * 512 + (b * NG + g) * P
                    mm = pe.transpose(psf[:, at:at + P],
                                      pcmp[:, b, g * R:(g + 1) * R, :].rearrange("p r n -> p (r n)"), ident)
            mm.then_inc(S["c_tr"], 1)
            pe.wait_ge(S["c_out"], 1)
            pe.wait_ge(S["vcmp_out"], 1)
            for b in range(NB):
                for g in range(NG):
                    at = b * 512 + g * 256
                    mm = pe.matmul(psf[:, at:at + 256], pcT[:, b, g, :],
                                   vbd[:, g, :, :].rearrange("p r d -> p (r d)"), start=True, stop=True)
            mm.then_inc(S["co_done"], 1)

            pe.wait_ge(S["h_ready"], 8)
            turn_round(lambda k, b: h_tok[:, b, k * P:(k + 1) * P], KC)
            copied(8)
            for j in range(2):
                by_tokens("wo", j)

            pe.wait_ge(S["h_ready"], 10)
            turn_round(lambda k, b: h_tok[:, b, k * P:(k + 1) * P], KC)
            copied(9)
            last = DFF // CHUNK - 1
            for j in range(last + 2):
                if j <= last:
                    by_columns("up", j)
                if j >= 1:
                    w = slot(NTH["down", j - 1], D)
                    pe.wait_ge(S["u2_ready"], j)
                    for b in range(NB):
                        for half in range(2):
                            for f in range(4):
                                mm = pe.matmul(ps[:, 4 + 2 * b + half, :], uT[:, (j - 1) % 3, f, b * P:(b + 1) * P],
                                               w[:, f, half * 512:(half + 1) * 512],
                                               start=(j == 1 and f == 0), stop=(j == last + 1 and f == 3))
                    mm.then_inc(w_used, 1)

        @block.scalar
        def _(act):
            own = Chain(act, act_own)

            def squares(b0, width, view, row):
                for b in range(NB):
                    act.activation(view(b)[1], view(b)[0], ACT.Square,
                                   accum_out=st[:, row, b0 + b:b0 + b + 1]).then_inc(S["sumsq"], 1)

            def root(cols, src, dst, wait, count, done):
                act.wait_ge(S[wait], count)
                rows = (cols + 15) // 16
                cols = min(cols, 16)
                act.activation(st[:, dst:dst + rows, 0:cols], st[:, src:src + rows, 0:cols], ACT.Sqrt)\
                    .then_inc(S[done], 1)

            def copy_round(r, dst):
                act.wait_ge(S["tr_done"], r)
                act.copy(dst, psf[:, 4 * 512:6 * 512]).then_inc(S["tr_copied_act"], 1)

            def empty(kind, j, dst, src, func=ACT.Copy, bias=0.0):
                act.wait_ge(w_used, through(kind, j))
                act.activation(dst, src, func, bias=bias).then_inc(emptied_by["act"], 1)

            def empty_ada(j):
                cols = slice((j % 2) * CHUNK, (j % 2 + 1) * CHUNK)
                which = (0, 1, 2, 0, 1, 3)[j // 2]
                if j == 6:
                    act.wait_ge(S["h_ready"], 2)
                empty("ada", j, mod[:, which, cols], ps[:, pair("ada", j), :], ACT.Copy, 1.0 if which == 1 else 0.0)

            def first_half(v):
                return v[:, 0:KC // 2, :].rearrange("p k t -> p (k t)")

            act.wait_ge(ld_c, 32)
            act.activation(csilu[:, 1, :], csilu[:, 0, :], ACT.Silu).then_inc(S["silu_c"], 1)
            act.wait_ge(ld_x, 32)
            squares(0, D, lambda b: (x_tok[:, b, :], tiles[:, 4 + b, 0:D]), 0)
            act.wait_ge(S["angles"], 1)
            act.activation(trig[:, :, :, :], turns, ACT.Sin).then_inc(S["trig_ready"], 1)
            for j in range(4):
                empty_ada(j)
            root(NB, 1, 2, "var", 1, "std")
            copy_round(1, first_half(hT))
            for j in range(7):
                b0 = pair("win", j)
                empty("win", j, proj[:, :, j * HW:(j + 1) * HW], ps[:, b0:b0 + 2, :])
                if j == 3:
                    act.wait_ge(emptied_by["act"], emptied_count("win", 3))
                    act.activation(proj[:, :, 3 * HW:4 * HW], proj[:, :, 3 * HW:4 * HW], ACT.Silu)\
                        .then_inc(S["ret_gate"], 1)
            empty_ada(4)
            copy_round(2, qT.rearrange("p c t -> p (c t)"))
            empty_ada(5)
            empty_ada(6)
            root(32, 4, 6, "var_s", 1, "std_s")
            empty_ada(7)
            empty_ada(8)
            copy_round(3, qT.rearrange("p c t -> p (c t)"))
            empty_ada(9)
            act.wait_ge(S["ret_y"], 2)
            for b4 in range(2):
                bank, t = 4 - 4 * b4, tiles[:, 3 * b4, :]
                act.wait_ge(S["sb_z"], b4 + 1)
                own(act.activation(t, psf[:, bank * 512:(bank + 3) * 512], ACT.Abs))
                own(act.activation(t, t, ACT.Exp, scale=-1.0))
                act.activation(t, t, ACT.Ln, bias=1.0).then_inc(S["sb_L"], 1)
            root(16, 4, 6, "var_s", 2, "std_s")
            for b4 in range(2):
                t = tiles[:, 3 * b4 + 1, :]
                act.wait_ge(S["sb_logw"], b4 + 1)
                act.activation(t, t, ACT.Exp).then_inc(S["sb_exp"], 1)
            root(16, 5, 7, "var_s", 3, "std_s")
            copy_round(4, first_half(hT))
            act.wait_ge(S["x1_ready"], 2)
            squares(0, D, lambda b: (x_tok[:, b, :], tiles[:, 4 + b, 0:D]), 0)
            for j in (10, 11):
                empty_ada(j)
            root(NB, 1, 2, "var", 2, "std")
            copy_round(5, first_half(hT))
            for j in range(4):
                b0 = pair("wq", j)
                empty("wq", j, qryT[:, 4 * j:4 * j + 4, :].rearrange("p c t -> p (c t)"),
                      psf[:, b0 * 512:b0 * 512 + 1024])
            act.wait_ge(S["sub_done"], 1)
            act.copy(score[:, 0:PH, :].rearrange("p h n -> p (h n)"), psf[:, 4 * 512:8 * 512])\
                .then_inc(S["sub_out"], 1)

            def exps(head, n):
                act.wait_ge(S["dmax"], head + 1)
                act.activation(ex[:, n, :], best[:, :], ACT.Exp, accum_out=exs[:, n:n + 1])\
                    .then_inc(S["exp_done"], 1)

            exps(0, 0)
            for b in range(NB):
                with act.Fori(0, PH // 2) as turn:
                    for par in range(2):
                        head = turn * 2 + (PH * b + par)
                        act.wait_ge(S["down_free"], head * PK + (GR + PK))
                        act.activation(actw[:, par, :], dots[:, par, :], ACT.Gelu).then_inc(S["gelu_done"], 1)
                        act.wait_ge(S["actw_ready"], head + 1)
                        for k in range(PK):
                            act.wait_ge(S["up_free"], head * PK + (GR + k - 3))
                            act.activation(diag[:, k % 4, :], ident, ACT.Copy, scale=actw[:, par, k:k + 1])\
                                .then_inc(S["diag_ready"], 1)
                        exps(head + 1, 1 - par)

            act.wait_ge(S["x2_ready"], 2)
            squares(0, D, lambda b: (x_tok[:, b, :], ptile[:, b, 0:D]), 0)
            root(NB, 1, 2, "var", 3, "std")
            copy_round(6, first_half(hT))
            for j in range(6):
                b0, n = pair("win2", j), min(CHUNK, ZW - j * CHUNK)
                empty("win2", j, z[:, :, j * CHUNK:j * CHUNK + n], ps[:, b0:b0 + 2, 0:n])
                if j == 2:
                    root(32, 4, 6, "zrms", 1, "zstd")
            act.wait_ge(emptied_by["act"], emptied_count("win2", 2))
            act.activation(gatec[:, :, :, :].rearrange("p b h k -> p b (h k)"), z[:, :, Z_G:Z_H], ACT.Sigmoid)\
                .then_inc(S["ret_gate"], 1)
            copy_round(7, qT2.rearrange("p c t -> p (c t)"))

            def exp_batch(i):
                act.wait_ge(S["s_max"], i + 1)
                for b in range(NB):
                    for r in range(R):
                        lo, n = (r * P, P) if b == 0 else (512 + r * T, T)
                        t = ptile[:, i % 2, lo:lo + n]
                        ins = act.activation(t, t, ACT.Exp, bias=mx[:, i % 2, b, r:r + 1],
                                             accum_out=sm[:, i % 2, b, r:r + 1])
                ins.then_inc(S["p_ready"], 1)

            exp_batch(0)
            act.wait_ge(S["u_shifted"], 1)
            act.copy(sh1[:, :, :], ps[:, 0:2, :])
            act.copy(sh2[:, :, :], ps[:, 2:4, :]).then_inc(S["u_copied"], 1)
            act.wait_ge(S["c_tr"], 1)
            kv = psf[:, 0:1024].rearrange("p (v g t) -> p v g t", v=2, g=NG)
            act.copy(kvA[0:64, :, :, :], kv[0:64, :, :, :])
            act.copy(kvA[64:P, :, :, 0:T - 1], kv[64:P, :, :, 1:T]).then_inc(S["kv_copied"], 1)
            exp_batch(1)
            act.wait_ge(ld_cmp, 64)
            act.wait_ge(S["blk_ready"], 1)
            act.wait_ge(w_used, through("cmp", 1))
            for v in range(2):
                for f in range(2):
                    at = 2 * 512 + (2 * v + f) * 32
                    src = psf[:, at:at + 2 * NCMP].rearrange("p (g n) -> p g n", g=NG)
                    dst = hdnT[:, f, :].rearrange("p (g n) -> p g n", g=NG)[:, :, 0:NCMP]
                    if v == 1:
                        src = src.unsqueeze(2).to_broadcast([P, NG, R, NCMP])
                        dst = hdnV[:, f, :, :, 0:NCMP]
                    ins = act.activation(dst, src, ACT.Gelu_apprx_tanh, bias=cbias[:, v, f:f + 1])
            ins.then_inc(S["hdn_out"], 1)
            act.wait_ge(S["kvar"], 1)
            act.activation(kcst[:, 2:3], kcst[:, 1:2], ACT.Sqrt).then_inc(S["kstd"], 1)
            act.wait_ge(S["kcmp"], 2)
            for g in range(NG):
                for r in range(R):
                    ins = act.copy(vbd[32 * r:32 * r + 32, g, r, :], ps[32 * r:32 * r + 32, 0, g * HD:(g + 1) * HD])
            ins.then_inc(S["vcmp_out"], 1)
            act.wait_ge(S["c_tr"], 2)
            act.copy(kcmpT[:, :], ps[:, 3, 128:192]).then_inc(S["kct_copied"], 1)
            exp_batch(2)
            act.wait_ge(S["c_max"], 1)
            act.activation(pcs, pcs, ACT.Exp).then_inc(S["c_exp"], 1)
            exp_batch(3)
            act.wait_ge(S["c_tr"], 3)
            act.copy(pcT.rearrange("p b g t -> p (b g t)"), ps[:, 3, :]).then_inc(S["c_out"], 1)
            act.wait_ge(S["conv_out"], 1)
            act.wait_ge(S["o_out"], 5)
            for b in range(NB):
                act.activation(tmp[:, b, :], h_tok[:, b, 0:HW], ACT.Square, accum_out=st[:, 0, b:b + 1])
                act.activation(sh1[:, b, :], z[:, b, Z_H:Z_H + HW], ACT.Square, accum_out=st[:, 0, 2 + b:3 + b])\
                    .then_inc(S["sumsq"], 1)
            root(4, 1, 2, "var", 4, "std")
            copy_round(8, first_half(hT))
            act.wait_ge(S["x1_ready"], 4)
            squares(0, D, lambda b: (x_tok[:, b, :], ptile[:, b, 0:D]), 0)
            root(NB, 1, 2, "var", 5, "std")
            copy_round(9, first_half(hT))
            for j in range(DFF // CHUNK):
                b0 = pair("up", j)
                if j >= 3:
                    act.wait_ge(w_used, through("down", j - 3))
                empty("up", j, uT[:, j % 3, :, :].rearrange("p f t -> p (f t)"),
                      psf[:, b0 * 512:b0 * 512 + 1024], ACT.Relu)

        @block.gpsimd
        def _(pool):
            own = Chain(pool, pool_own)
            for b in range(NB):
                with pool.Fori(0, PH // 2) as turn:
                    for par in range(2):
                        head = turn * 2 + (PH * b + par)
                        pool.wait_ge(S["ids_ready"], head + 1)
                        for table, ring, landed, free in ((a["peer_down"], downs, ring_down, "down_free"),
                                                          (a["peer_up"], ups, ring_up, "up_free")):
                            for k in range(PK):
                                pool.wait_ge(S[free], head * PK + (k + 1))
                                pool.sem_inc(S["gathers"], 1)
                                pool.indirect_dma_start(
                                    out=ring[:, k % GR, :], out_offset=None, in_=table,
                                    in_offset=bass.IndirectOffsetOnAxis(ap=ids[:, par, k:k + 1], axis=0))\
                                    .then_inc(landed[k % GR], 16)
            pool.wait_ge(emptied_by["act"], emptied_count("win2", 5))
            u = z[:, :, Z_H:Z_H + HW]
            pool.tensor_tensor(u, z[:, :, Z_C:Z_C + HW], u, ALU.mult).then_inc(S["u_ready"], 1)
            pool.wait_ge(ld_late, 64)
            pool.wait_ge(S["u_copied"], 1)

            def tap(k):
                return convw[:, k, :].unsqueeze(1).to_broadcast([P, NB, HW])

            own(pool.tensor_tensor(u, u, tap(2), ALU.mult))
            own(pool.tensor_tensor(sh1, sh1, tap(1), ALU.mult))
            own(pool.tensor_tensor(sh2, sh2, tap(0), ALU.mult))
            own(pool.tensor_tensor(sh1, sh1, sh2, ALU.add))
            own(pool.tensor_tensor(u, u, sh1, ALU.add))
            pool.tensor_tensor(u, u, z[:, :, Z_B:Z_B + HW], ALU.mult).then_inc(S["conv_out"], 1)

        @block.vector
        def _(dve):
            own = Chain(dve, dve_own)

            def mean_eps(n, width):
                dve.tensor_scalar(st[:, 1, 0:n], st[:, 0, 0:n], 1.0 / width, EPS, ALU.mult, ALU.add)\
                    .then_inc(S["var"], 1)

            def copy_round(r, dst):
                dve.wait_ge(S["tr_done"], r)
                dve.tensor_copy(dst, psf[:, 6 * 512:8 * 512]).then_inc(S["tr_copied_dve"], 1)

            def second_half(v):
                return v[:, KC // 2:KC, :].rearrange("p k t -> p (k t)")

            def over_heads(row, n=NH):
                v = st[:, row, 0:NB * n].rearrange("p (b h) -> p b h", b=NB)
                return v.unsqueeze(3).to_broadcast([P, NB, n, HD])

            def head_gain(k, n=NH):
                return small[:, k, :].unsqueeze(1).unsqueeze(1).to_broadcast([P, NB, n, HD])

            def head_sums(row, v, square, n=NH):
                own(dve.tensor_tensor(square, v, v, ALU.mult))
                own(dve.tensor_reduce(st[:, row, 0:NB * n].rearrange("p (b h) -> p b h", b=NB), square, AX.X, ALU.add))

            def norm_x(turn, sums, gain, shift=None):
                dve.wait_ge(S["sumsq"], sums)
                mean_eps(NB, D)
                dve.wait_ge(S["std"], turn)
                own(dve.reciprocal(st[:, 3, 0:NB], st[:, 2, 0:NB]))
                for b in range(NB):
                    ins = dve.scalar_tensor_tensor(h_tok[:, b, :], x_tok[:, b, :], st[:, 3, b:b + 1], gain,
                                                   ALU.mult, ALU.mult)
                    if shift is not None:
                        own(ins)
                        ins = dve.tensor_tensor(h_tok[:, b, :], h_tok[:, b, :], shift, ALU.add)
                    ins.then_inc(S["h_ready"], 1)

            dve.memset(dots[:, :, :], 0.0).then_inc(S["down_free"], GR)
            dve.memset(actw[:, :, :], 0.0).then_inc(S["up_free"], GR)
            dve.wait_ge(ld_x, 32)
            dve.wait_ge(ld_const, 16)
            own(dve.tensor_copy(posf[:, :], posi[:, :]))
            for b in range(NB):
                own(dve.tensor_scalar(ang[:, b, :], con("freq"), posf[:, b:b + 1], None, ALU.mult))
            for f, quarter in enumerate((0.0, 0.25)):
                t = turns[:, f, :, :]
                own(dve.tensor_scalar(t, ang, 1.0 / TWO_PI, quarter, ALU.mult, ALU.add))
                own(dve.tensor_scalar(t, t, MAGIC, None, ALU.add))
                own(dve.tensor_scalar(t, t, MAGIC, None, ALU.subtract))
                w = ang2[:, f, :, :]
                own(dve.scalar_tensor_tensor(w, t, -C1, ang, ALU.mult, ALU.add))
                own(dve.scalar_tensor_tensor(w, t, -C2, w, ALU.mult, ALU.add))
                own(dve.scalar_tensor_tensor(w, t, -C3, w, ALU.mult, ALU.add))
                own(dve.tensor_scalar(w, w, quarter * TWO_PI, np.pi, ALU.add, ALU.min))
                ins = dve.tensor_scalar(t, w, -np.pi, None, ALU.max)
                if f == 0:
                    own(ins)
            ins.then_inc(S["angles"], 1)

            dve.wait_ge(ld_gain, 32)
            dve.wait_ge(emptied_by["act"], emptied_count("ada", 3))
            own(dve.tensor_tensor(SCALE, SCALE, gain1[:, 0, :], ALU.mult))
            norm_x(1, 2, SCALE, SHIFT)
            copy_round(1, second_half(hT))

            dve.wait_ge(S["trig_ready"], 1)
            dve.wait_ge(emptied_by["act"], emptied_count("win", 1))
            for b in range(NB):
                src = proj[:, b, 0:2 * HW].rearrange("p (h f d) -> p h f d", f=2, d=HD // 2)
                dst = h_tok[:, b, :].rearrange("p (h f d) -> p h f d", f=2, d=HD // 2)
                sin, cos = (trig[:, f, b, :].unsqueeze(1).to_broadcast([P, 2 * NH, HD // 2]) for f in range(2))
                t = [tiles[:, 2 + k, 0:512].rearrange("p (h d) -> p h d", d=HD // 2) for k in range(2)]
                own(dve.tensor_tensor(dst[:, :, 0, :], src[:, :, 0, :], cos, ALU.mult))
                own(dve.tensor_tensor(t[0], src[:, :, 1, :], sin, ALU.mult))
                own(dve.tensor_tensor(dst[:, :, 0, :], dst[:, :, 0, :], t[0], ALU.subtract))
                own(dve.tensor_tensor(dst[:, :, 1, :], src[:, :, 1, :], cos, ALU.mult))
                own(dve.tensor_tensor(t[1], src[:, :, 0, :], sin, ALU.mult))
                dve.tensor_tensor(dst[:, :, 1, :], dst[:, :, 1, :], t[1], ALU.add).then_inc(S["rot_ready"], 1)

            dve.wait_ge(emptied_by["act"], emptied_count("win", 5))
            sq_, sk_ = (heads(proj[:, :, (4 + k) * HW:(5 + k) * HW]) for k in range(2))
            flat = tiles[:, 5, 0:1024].rearrange("p (b h d) -> p b h d", b=NB, d=HD)
            head_sums(4, sq_, flat)
            head_sums(5, sk_, flat)
            dve.tensor_scalar(st[:, 4:6, :], st[:, 4:6, :], 1.0 / HD, EPS, ALU.mult, ALU.add).then_inc(S["var_s"], 1)
            copy_round(2, kT.rearrange("p c t -> p (c t)"))
            dve.wait_ge(ld_early, 112)
            own(dve.tensor_scalar(small[:, 0, :], small[:, 0, :], HD ** -0.5, None, ALU.mult))
            own(dve.tensor_scalar(small[:, 3, :], small[:, 3, :], HD ** -0.5, None, ALU.mult))

            for b4 in range(2):
                dve.wait_ge(S["ret_scores"], b4 + 1)
                for n in range(3):
                    ins = dve.tensor_tensor(tiles[:, b4, n * 512:(n + 1) * 512].rearrange("p (h i) -> p h i", h=4),
                                            ps[:, 4 + n, :].rearrange("p (h i) -> p h i", h=4),
                                            decay[:, n % 2, b4::2, :], ALU.mult)
                ins.then_inc(S["ret_decayed"], 1)
                if b4 == 0:
                    dve.wait_ge(S["std_s"], 1)
                    own(dve.reciprocal(st[:, 8:10, :], st[:, 6:8, :]))
                    own(dve.tensor_tensor(sq_, sq_, over_heads(8), ALU.mult))
                    dve.tensor_tensor(sq_, sq_, head_gain(0), ALU.mult).then_inc(S["sbq_ready"], 1)
                    own(dve.tensor_tensor(sk_, sk_, over_heads(9), ALU.mult))
                    dve.tensor_tensor(sk_, sk_, head_gain(1), ALU.mult).then_inc(S["sbq_ready"], 1)
            for b4 in range(2):
                dve.wait_ge(S["ret_y"], b4 + 1)
                for b in range(NB):
                    ins = dve.tensor_copy(every_other(proj[:, b, 0:HW], b4),
                                          ps[:, 7, b * 256:(b + 1) * 256].rearrange("p (h d) -> p h d", d=HD))
                ins.then_inc(S["ret_y_out"], 1)
            copy_round(3, kT.rearrange("p c t -> p (c t)"))

            dve.wait_ge(S["ret_y_out"], 2)
            yr = heads(proj[:, :, 0:HW])
            ysum = st[:, 4, :].rearrange("p (b h) -> p b h", b=NB)
            own(dve.tensor_reduce(ysum, yr, AX.X, ALU.add))
            own(dve.tensor_scalar(st[:, 4, :], st[:, 4, :], 1.0 / HD, None, ALU.mult))
            own(dve.tensor_tensor(yr, yr, over_heads(4), ALU.subtract))

            def sb_logs(b4):
                bank, t = 4 - 4 * b4, [tiles[:, 3 * b4 + k, :] for k in range(3)]
                zed = psf[:, bank * 512:(bank + 3) * 512]
                dve.wait_ge(S["sb_L"], b4 + 1)
                own(dve.scalar_tensor_tensor(t[1], zed, 0.0, t[0], ALU.min, ALU.subtract))
                own(dve.tensor_tensor(t[2], t[1], zed, ALU.subtract))
                mask = con("before").unsqueeze(1).to_broadcast([P, 4, P])
                for n in (0, 2):
                    v = t[2][:, n * 512:(n + 1) * 512].rearrange("p (h i) -> p h i", h=4)
                    ins = dve.tensor_tensor(v, v, mask, ALU.mult)
                ins.then_inc(S["sb_ls"], 1)

            def sb_weights(b4):
                bank, t = 4 - 4 * b4, tiles[:, 3 * b4 + 1, :]
                dve.wait_ge(S["sb_cum"], b4 + 1)
                dve.tensor_tensor(t, t, psf[:, bank * 512:(bank + 3) * 512], ALU.add).then_inc(S["sb_logw"], 1)

            def sb_mask(b4):
                t = tiles[:, 3 * b4 + 1, :]
                mask = con("before").unsqueeze(1).to_broadcast([P, 4, P])
                dve.wait_ge(S["sb_exp"], b4 + 1)
                for n in (0, 2):
                    v = t[:, n * 512:(n + 1) * 512].rearrange("p (h i) -> p h i", h=4)
                    ins = dve.tensor_tensor(v, v, mask, ALU.mult)
                ins.then_inc(S["sb_w"], 1)

            sb_logs(0)
            sb_logs(1)
            sqr = tiles[:, 0, 0:1024].rearrange("p (b h d) -> p b h d", b=NB, d=HD)
            head_sums(4, yr, sqr)
            dve.tensor_scalar(st[:, 4, :], st[:, 4, :], 1.0 / HD, EPS, ALU.mult, ALU.add).then_inc(S["var_s"], 1)
            sb_weights(0)
            sb_weights(1)
            dve.wait_ge(S["std_s"], 2)
            own(dve.reciprocal(st[:, 8, :], st[:, 6, :]))
            own(dve.tensor_tensor(yr, yr, over_heads(8), ALU.mult))
            dve.wait_ge(S["ret_gate"], 1)
            yw = proj[:, :, 0:HW]
            own(dve.tensor_tensor(yw, yw, rgain.unsqueeze(1).to_broadcast([P, NB, HW]), ALU.mult))
            dve.tensor_tensor(yw, yw, proj[:, :, 3 * HW:4 * HW], ALU.mult).then_inc(S["y_ready"], 1)
            sb_mask(0)
            sb_mask(1)
            ys = heads(proj[:, :, HW:2 * HW])
            for b4 in range(2):
                dve.wait_ge(S["sb_y"], b4 + 1)
                for b in range(NB):
                    own(dve.tensor_copy(every_other(proj[:, b, HW:2 * HW], b4),
                                        ps[:, 7 - 4 * b4, b * 256:(b + 1) * 256].rearrange("p (h d) -> p h d", d=HD)))
            head_sums(5, ys, sqr)
            dve.tensor_scalar(st[:, 5, :], st[:, 5, :], 1.0 / HD, EPS, ALU.mult, ALU.add).then_inc(S["var_s"], 1)
            dve.wait_ge(S["std_s"], 3)
            own(dve.reciprocal(st[:, 9, :], st[:, 7, :]))
            own(dve.tensor_tensor(ys, ys, over_heads(9), ALU.mult))
            dve.tensor_tensor(ys, ys, head_gain(2), ALU.mult).then_inc(S["y_ready"], 1)
            copy_round(4, second_half(hT))

            for j in range(2):
                b0, cols = pair("wout", j), slice(j * CHUNK, (j + 1) * CHUNK)
                dve.wait_ge(w_used, through("wout", j))
                gated = tiles[:, 0, 0:1024].rearrange("p (b n) -> p b n", b=NB)
                own(dve.tensor_tensor(gated, ps[:, b0:b0 + 2, :],
                                      GATE1[:, cols].unsqueeze(1).to_broadcast([P, NB, CHUNK]), ALU.mult))
                own(dve.tensor_tensor(x_tok[:, :, cols], x_tok[:, :, cols], gated, ALU.add))
                dve.sem_inc(emptied_by["dve"], 1)
                dve.sem_inc(S["x1_ready"], 1)
            own(dve.tensor_tensor(SCALE, SCALE, gain1[:, 1, :], ALU.mult))
            norm_x(2, 4, SCALE, SHIFT)
            copy_round(5, second_half(hT))
            dve.memset(score[:, 2 * PH, :], 0.0)
            dve.wait_ge(S["sub_done"], 2)
            dve.tensor_copy(score[:, PH:2 * PH, :].rearrange("p h n -> p (h n)"), psf[:, 0:4 * 512])\
                .then_inc(S["sub_out"], 1)

            step = Chain(dve, S["dve_step"])

            def top16(vals, work, values, index, n):
                step(dve.max(values[:, 0:8], vals))
                step(dve.max_index(index[:, 0:8], values[:, 0:8], vals))
                step(dve.match_replace(work, values[:, 0:8], vals, -3.0e38))
                step(dve.max(values[:, 8:16], work))
                step(dve.max_index(index[:, 8:16], values[:, 8:16], work))

            def choose(head, n):
                row = score[:, head, :] if isinstance(head, int) else \
                    score[:, bass.ds(head, 1), :].rearrange("p c n -> p (c n)")
                step(dve.tensor_copy(sc2[:, :], row))
                for half in range(2):
                    top16(sc2[:, half * NKEY:(half + 1) * NKEY], cand2[:, 0:NKEY], top[:, half, :], topi[:, half, :], n)
                step(dve.tensor_copy(topf[:, :, :], topi[:, :, :]))
                step(dve.tensor_tensor(cand[:, :, :], top[:, 0, :].unsqueeze(2).to_broadcast([P, PK, PK]),
                                      top[:, 1, :].unsqueeze(1).to_broadcast([P, PK, PK]), ALU.add))
                if not isinstance(head, int):
                    dve.wait_ge(S["exp_done"], head)
                top16(cand[:, :, :].rearrange("p i j -> p (i j)"), cand2[:, :], best[:, :], besti[:, 0, :], n)
                step(dve.tensor_scalar(besti[:, 1, :], besti[:, 0, :], 4, None, ALU.logical_shift_right))
                step(dve.tensor_scalar(besti[:, 2, :], besti[:, 0, :], 15, None, ALU.bitwise_and))
                step(dve.tensor_copy(bestf[:, :, :], besti[:, 1:3, :]))
                for half in range(2):
                    step(dve.tensor_tensor(pick[:, :, :], bestf[:, half, :].unsqueeze(2).to_broadcast([P, PK, PK]),
                                          con("iota").unsqueeze(1).to_broadcast([P, PK, PK]), ALU.is_equal))
                    step(dve.tensor_tensor(pick[:, :, :], pick[:, :, :],
                                          topf[:, half, :].unsqueeze(1).to_broadcast([P, PK, PK]), ALU.mult))
                    step(dve.tensor_reduce(picked[:, half, :], pick[:, :, :], AX.X, ALU.add))
                step(dve.scalar_tensor_tensor(picked[:, 0, :], picked[:, 0, :], float(NKEY), picked[:, 1, :],
                                             ALU.mult, ALU.add))
                if not isinstance(head, int):
                    dve.wait_ge(S["up_free"], head * PK + (GR - PK))
                dve.tensor_copy(ids[:, n, :], picked[:, 0, :]).then_inc(S["ids_ready"], 1)
                step(dve.tensor_scalar(first[:, :], best[:, 0:1], 1.0, None, ALU.mult))
                dve.tensor_scalar(best[:, :], best[:, :], first[:, 0:1], None, ALU.subtract).then_inc(S["dmax"], 1)

            dve.wait_ge(S["sub_out"], 2)
            choose(0, 0)
            for b in range(NB):
                with dve.Fori(0, PH // 2) as turn:
                    for par in range(2):
                        head = turn * 2 + (PH * b + par)
                        step.restart()
                        for k in range(PK):
                            dve.wait_ge(ring_down[k % GR], head * 32 + 16 * (k // GR + 1))
                            d = downs[:, k % GR, :]
                            dve.tensor_tensor_reduce(d, d, h_tok[:, b, :], 1.0, 0.0, ALU.mult, ALU.add,
                                                     dots[:, par, k:k + 1]).then_inc(S["down_free"], 1)
                        dve.wait_ge(S["exp_done"], head + 1)
                        step(dve.reciprocal(exs[:, par:par + 1], exs[:, par:par + 1]))
                        step(dve.tensor_scalar(ex[:, par, :], ex[:, par, :], exs[:, par:par + 1], None, ALU.mult))
                        dve.wait_ge(S["gelu_done"], head + 1)
                        dve.tensor_tensor(actw[:, par, :], actw[:, par, :], ex[:, par, :], ALU.mult)\
                            .then_inc(S["actw_ready"], 1)
                        choose(head + 1, 1 - par)
                dve.wait_ge(S["up_free"], GR + PH * PK * (b + 1))
                own(dve.tensor_tensor(SHIFT, psf[:, 1024 * b:1024 * (b + 1)], GATE2, ALU.mult))
                dve.sem_inc(S["peer_done"], 1)
                dve.tensor_tensor(x_tok[:, b, :], x_tok[:, b, :], SHIFT, ALU.add).then_inc(S["x2_ready"], 1)
            dve.sem_inc(S["late_free"], 1)

            own(dve.memset(hdnT, 0.0))
            own(dve.memset(hdnV, 0.0))
            own(dve.memset(vbd, 0.0))
            own(dve.memset(pcmp, 0.0))
            dve.wait_ge(ld_late, 64)
            norm_x(3, 6, gmix)
            copy_round(6, second_half(hT))
            zq = heads(z[:, :, Z_Q:Z_Q + HW])
            dve.wait_ge(emptied_by["act"], emptied_count("win2", 0))
            head_sums(4, zq, tmp.rearrange("p b (h d) -> p b h d", d=HD))
            zk = [heads(z[:, :, c:c + NG * HD]) for c in (Z_KS, Z_KW)]
            tk = tmp[:, 0, 0:256].rearrange("p (b g d) -> p b g d", b=NB, g=NG)
            dve.wait_ge(emptied_by["act"], emptied_count("win2", 2))
            for r in range(2):
                own(dve.tensor_tensor(tk, zk[r], zk[r], ALU.mult))
                own(dve.tensor_reduce(st[:, 5, 4 * r:4 * r + 4].rearrange("p (b g) -> p b g", b=NB), tk, AX.X, ALU.add))
            dve.tensor_scalar(st[:, 4:6, :], st[:, 4:6, :], 1.0 / HD, EPS, ALU.mult, ALU.add).then_inc(S["zrms"], 1)
            dve.wait_ge(S["zstd"], 1)
            own(dve.reciprocal(st[:, 8:10, :], st[:, 6:8, :]))
            own(dve.tensor_tensor(zq, zq, over_heads(8), ALU.mult))
            own(dve.tensor_tensor(zq, zq, head_gain(3), ALU.mult))
            for r in range(2):
                spread = st[:, 9, 4 * r:4 * r + 4].rearrange("p (b g) -> p b g", b=NB)
                own(dve.tensor_tensor(zk[r], zk[r], spread.unsqueeze(3).to_broadcast([P, NB, NG, HD]), ALU.mult))
                for b in range(NB):
                    ins = dve.tensor_tensor(kdup[:, b, r, :, :, :],
                                            zk[r][:, b, :, :].unsqueeze(2).to_broadcast([P, NG, 2, HD]),
                                            small[:, 5 + r, :].unsqueeze(1).unsqueeze(1).to_broadcast([P, NG, 2, HD]),
                                            ALU.mult)
            ins.then_inc(S["kv_ready"], 1)
            for v, c in enumerate((Z_KC, Z_VC)):
                for b in range(NB):
                    src = z[:, b, c:c + NG * HD].rearrange("p (g d) -> p g d", g=NG)
                    ins = dve.tensor_copy(kvdup[:, b, v, :, :, :], src.unsqueeze(2).to_broadcast([P, NG, 2, HD]))
            ins.then_inc(S["kv_ready"], 1)
            copy_round(7, kT2.rearrange("p r g t -> p (r g t)"))

            def bias_batch(i):
                pt = ptile[:, i % 2, :]
                dve.wait_ge(S["s_done"], i + 1)
                if i >= 2:
                    dve.wait_ge(S["pt_done"], i - 1)
                lo, hi = CONST["dist"]
                dist = const[:, lo:hi].rearrange("p (b s) -> p b s", b=NB)
                for b in range(NB):
                    for r in range(R):
                        at, n = (r * P, P) if b == 0 else (512 + r * T, T)
                        slope = 2.0 ** -(2 * r + i % 2 + 1)
                        own(dve.scalar_tensor_tensor(pt[:, at:at + n], dist[:, b, 0:n], slope,
                                                     psf[:, 4 * 512 + at:4 * 512 + at + n], ALU.mult, ALU.add))
                dve.tensor_reduce(mx[:, i % 2, 0, :], pt[:, 0:512].rearrange("p (r s) -> p r s", r=R), AX.X, ALU.max,
                                  negate=True)
                dve.tensor_reduce(mx[:, i % 2, 1, :], pt[:, 512:1536].rearrange("p (r s) -> p r s", r=R), AX.X,
                                  ALU.max, negate=True).then_inc(S["s_max"], 1)

            def take_turned(i):
                dve.wait_ge(S["pt_done"], i + 1)
                dve.tensor_copy(pT.rearrange("p k r t -> p (k r t)"), psf[:, 4 * 512:7 * 512]).then_inc(S["pt_out"], 1)

            def add_branch(coef, src, dst, fresh):
                c = coef.unsqueeze(3).to_broadcast([P, NB, coef.shape[2], HD])
                if fresh:
                    return dve.tensor_tensor(dst, src, c, ALU.mult)
                t = tmp[:, :, 0:coef.shape[2] * HD].rearrange("p b (h d) -> p b h d", d=HD)
                own(dve.tensor_tensor(t, src, c, ALU.mult))
                return dve.tensor_tensor(dst, dst, t, ALU.add)

            oh = heads(h_tok[:, :, 0:HW])

            def take_out(i):
                br, par = i // 2, i % 2
                s = sm[:, i % 2, :, :]
                own(dve.tensor_scalar(s, s, 1e-30, None, ALU.max))
                own(dve.reciprocal(s, s))
                own(dve.tensor_tensor(s, s, gatec[:, :, par::2, br + 1], ALU.mult))
                dve.wait_ge(S["o_done"], i + 1)
                own(add_branch(s, ps[:, 7, :].rearrange("p (b r d) -> p b r d", b=NB, r=R),
                               oh[:, :, par::2, :], br == 0))
                dve.sem_inc(S["o_out"], 1)

            def compress_blocks():
                dve.wait_ge(S["kv_copied"], 1)
                dve.wait_ge(ld_cmp, 64)
                for v in range(2):
                    for hi in range(2):
                        win = kvA[:, v, :, :].rearrange("p g (n m two) -> p two m g n", two=2, m=8)
                        code = peT[:, v, 8 * hi:8 * hi + 8].unsqueeze(2).unsqueeze(2).to_broadcast([P, 8, NG, NCMP])
                        dst = blkT[:, v, 8 * hi:8 * hi + 8, :].rearrange("p m (g n) -> p m g n", g=NG)
                        ins = dve.tensor_tensor(dst, win[:, 0, :, :, hi:hi + NCMP], code, ALU.add)
                ins.then_inc(S["blk_ready"], 1)

            def compressed_norm():
                dve.wait_ge(S["kcmp"], 1)
                own(dve.tensor_copy(kcn[:, 0, :], ps[0:64, 3, 0:HD]))
                own(dve.tensor_tensor(kcq[:, :], kcn[:, 0, :], kcn[:, 0, :], ALU.mult))
                own(dve.tensor_reduce(kcst[:, 0:1], kcq[:, :], AX.X, ALU.add))
                dve.tensor_scalar(kcst[:, 1:2], kcst[:, 0:1], 1.0 / HD, EPS, ALU.mult, ALU.add).then_inc(S["kvar"], 1)
                dve.wait_ge(S["kstd"], 1)
                own(dve.reciprocal(kcst[:, 3:4], kcst[:, 2:3]))
                own(dve.scalar_tensor_tensor(kcn[:, 0, :], kcn[:, 0, :], kcst[:, 3:4], small[0:64, 4, :],
                                             ALU.mult, ALU.mult))
                dve.tensor_copy(kcn[:, 1, :], kcn[:, 0, :]).then_inc(S["kcn_ready"], 1)

            def by_head(v):
                return v.rearrange("p (b h) n -> p b h n", b=NB)

            def compressed_scores():
                dve.wait_ge(S["cs_done"], 1)
                lo, hi = CONST["cdist"]
                dist = const[:, lo:hi].rearrange("p (b n) -> p b n", b=NB)
                for h in range(NH):
                    raw = ps[:, 2 - h % 2, 0:NB * R * CSTEP].rearrange("p (b h n) -> p b h n", b=NB, n=CSTEP)
                    own(dve.scalar_tensor_tensor(by_head(pcs)[:, :, h, :], dist, 2.0 ** -(h + 1),
                                                 raw[:, :, h // 2, :], ALU.mult, ALU.add))
                own(dve.tensor_reduce(cst[:, 0, :], pcs, AX.X, ALU.max))
                dve.tensor_tensor(pcs, pcs, cst[:, 0, :].unsqueeze(2).to_broadcast([P, NB * NH, CSTEP]),
                                  ALU.subtract).then_inc(S["c_max"], 1)

            def compressed_weights():
                lo, hi = CONST["cmask"]
                mask = const[:, lo:hi].rearrange("p (b n) -> p b n", b=NB)
                dve.wait_ge(S["c_exp"], 1)
                dst = pcmp[:, :, :, 0:CSTEP]
                dve.tensor_tensor(dst, by_head(pcs), mask.unsqueeze(2).to_broadcast([P, NB, NH, CSTEP]), ALU.mult)\
                    .then_inc(S["c_ready"], 1)
                dve.wait_ge(S["c_ready"], 1)
                total, coef = (cst[:, k, :].rearrange("p (b h) -> p b h", b=NB) for k in (1, 2))
                own(dve.tensor_reduce(total, dst, AX.X, ALU.add))
                own(dve.tensor_scalar(total, total, 1e-30, None, ALU.max))
                own(dve.reciprocal(total, total))
                own(dve.tensor_tensor(coef, total, gatec[:, :, :, 0], ALU.mult))
                return coef

            bias_batch(0)
            take_turned(0)
            bias_batch(1)
            compress_blocks()
            dve.wait_ge(S["ret_gate"], 2)
            take_out(0)
            take_turned(1)
            bias_batch(2)
            compressed_norm()
            take_out(1)
            take_turned(2)
            bias_batch(3)
            compressed_scores()
            take_out(2)
            take_turned(3)
            coef = compressed_weights()
            take_out(3)
            dve.wait_ge(S["co_done"], 1)
            own(add_branch(coef, psf[:, 0:1024].rearrange("p (b h d) -> p b h d", b=NB, d=HD), oh, False))
            dve.sem_inc(S["o_out"], 1)

            dve.wait_ge(S["sumsq"], 8)
            mean_eps(4, HW)
            dve.wait_ge(S["std"], 4)
            own(dve.reciprocal(st[:, 3, 0:4], st[:, 2, 0:4]))
            for b in range(NB):
                dve.scalar_tensor_tensor(h_tok[:, b, 0:HW], h_tok[:, b, 0:HW], st[:, 3, b:b + 1], gout[:, 0:HW],
                                         ALU.mult, ALU.mult)
                dve.scalar_tensor_tensor(h_tok[:, b, HW:D], z[:, b, Z_H:Z_H + HW], st[:, 3, 2 + b:3 + b],
                                         gout[:, HW:D], ALU.mult, ALU.mult).then_inc(S["h_ready"], 1)
            copy_round(8, second_half(hT))
            for j in range(2):
                b0, cols = pair("wo", j), slice(j * CHUNK, (j + 1) * CHUNK)
                dve.wait_ge(w_used, through("wo", j))
                own(dve.tensor_tensor(x_tok[:, :, cols], x_tok[:, :, cols], ps[:, b0:b0 + 2, :], ALU.add))
                dve.sem_inc(emptied_by["dve"], 1)
                dve.sem_inc(S["x1_ready"], 1)
            norm_x(5, 10, gffn)
            copy_round(9, second_half(hT))
            for j in range(DFF // CHUNK):
                t = uT[:, j % 3, :, :].rearrange("p f t -> p (f t)")
                dve.wait_ge(emptied_by["act"], emptied_count("up", j))
                dve.tensor_tensor(t, t, t, ALU.mult).then_inc(S["u2_ready"], 1)
            dve.wait_ge(w_used, through("down", DFF // CHUNK - 1))
            for b in range(NB):
                dve.tensor_tensor(x_tok[:, b, :], x_tok[:, b, :], psf[:, (4 + 2 * b) * 512:(6 + 2 * b) * 512], ALU.add)\
                    .then_inc(S["x_out"], 1)


def kernel(**inputs):
    from concourse import bacc
    from concourse.bass_utils import run_bass_kernel_spmd

    def of(name):
        return np.asarray(inputs[name])

    def put(a):
        return np.ascontiguousarray(a)

    arrays = {
        "x": of("x")[0],
        "c": of("c").reshape(KC, P).T,
        "positions": of("positions")[0],
        "ada_w": of("ada_w")[0],
        "ada_b": of("ada_b").reshape(12, CHUNK),
        "gain1": of("norm1_gain")[0],
        "gain2": of("norm2_gain")[0],
        "w_in": of("w_in")[0],
        "ret_gain": of("ret_norm_gain")[0],
        "sb_q": of("sb_q_gain")[0],
        "sb_k": of("sb_k_gain")[0],
        "sb_out": of("sb_out_gain")[0],
        "w_out": of("w_out")[0],
        "w_query": of("peer_w_query")[0],
        "keys": of("peer_sub_keys")[0].transpose(3, 0, 1, 2).reshape(P, -1),
        "peer_down": of("peer_down")[0],
        "peer_up": of("peer_up")[0],
        "g_mix": of("g_mix_norm_2")[0],
        "w_in2": of("w_in_2")[0],
        "g_q": of("g_q_2")[0],
        "g_k": of("g_k_2").reshape(-1),
        "pe": of("pe_cmp_2")[0].reshape(2, NPAIR, 2, HD).transpose(2, 3, 0, 1).reshape(P, 2, NPAIR),
        "w_cmp1": of("w_cmp1_2")[0],
        "b_cmp1": of("b_cmp1_2")[0].reshape(2, 2, P).transpose(2, 0, 1),
        "w_cmp2": of("w_cmp2_2")[0],
        "b_cmp2": of("b_cmp2_2").reshape(1, 2, HD),
        "conv_w": of("conv_w_2").reshape(-1),
        "g_out": of("g_out_2")[0],
        "w_o": of("w_o_2")[0],
        "g_ffn": of("g_ffn_norm_2")[0],
        "w_up": of("w_up_2")[0],
        "w_down": of("w_down_2")[0],
        "const": constants(),
        "decay": decay_table(),
    }
    arrays = {name: put(a) for name, a in arrays.items()}
    nc = bacc.Bacc("TRN2", target_bir_lowering=False, num_devices=1)
    aps = {name: nc.dram_tensor("in_" + name, a.shape, mybir.dt.from_np(a.dtype), kind="ExternalInput").ap()
           for name, a in arrays.items()}
    out = nc.dram_tensor("out", (T, D), F32, kind="ExternalOutput").ap()
    two_blocks(nc, aps, out)
    result = run_bass_kernel_spmd(nc, [{"in_" + name: a for name, a in arrays.items()}], core_ids=[0])
    return result.results[0]["out"].reshape(1, T, D)
```

```python
from contextlib import ExitStack

import numpy as np

import concourse.bass as bass
from concourse import mybir

ALU = mybir.AluOpType
ACT = mybir.ActivationFunctionType
AX = mybir.AxisListType
F32 = mybir.dt.float32
F32R = mybir.dt.float32r
U32 = mybir.dt.uint32
I32 = mybir.dt.int32

P = 128
NB = 2
T = NB * P
D = 1024
KC = D // P
HD = 64
NH = 8
HW = NH * HD
CHUNK = 512
SLOT = KC * CHUNK
PARTS = 4
PART = SLOT // PARTS
RING = 2
EPS = 1e-6

PH = 8
PK = 16
NKEY = 128
NE = NKEY * NKEY
EF = CHUNK // NKEY
STEPS = NE // CHUNK
LEAD = 3
AR = LEAD + 1
TT = 8

NCMP = 15
CMPW = 32
CSTEP = 16
NPAIR = CMPW // 2
CF = 256
NG = 2
R = NH // NG
ZW = 2840
DFF = 4096

Z_Q, Z_KC, Z_VC, Z_KS, Z_VS, Z_KW, Z_VW, Z_G, Z_H, Z_C, Z_B = (
    0, 512, 640, 768, 896, 1024, 1152, 1280, 1304, 1816, 2328)

PAIRS = [(0, 0), (0, 1), (1, 1)]

TWO_PI = 2.0 * np.pi
MAGIC = 1.5 * 2.0 ** 23
C1 = 6.28125
C2 = float(np.float32(TWO_PI - C1))
C3 = float(np.float32(TWO_PI - C1 - np.float64(np.float32(TWO_PI - C1))))
FAR = -1e32

CONST = {}


def constants():
    i = np.arange(P)
    parts = {
        "ident": np.eye(P),
        "after": i[:, None] > i[None, :],
        "before": i[:, None] < i[None, :],
        "ones": np.ones((P, P)),
    }
    dist = np.empty((P, NB, T))
    cdist = np.empty((P, NB, CSTEP))
    for b in range(NB):
        t = b * P + i
        far = t[:, None] - np.arange(T)[None, :]
        dist[:, b] = np.where(far >= 0, -far, FAR)
        far = t[:, None] - (np.arange(CSTEP) * CSTEP + CMPW - 1)[None, :]
        cdist[:, b] = np.where(far >= 0, -far, FAR)
    parts["dist"] = dist
    parts["cdist"] = cdist
    parts["cmask"] = cdist > FAR
    half = HD // 2
    parts["freq"] = np.tile(np.float32(10000.0) ** (-np.arange(half, dtype=np.float32) / np.float32(half)), (P, 1))
    parts["iota"] = np.tile(np.arange(NKEY), (P, 1))
    at, out = 0, []
    for name, a in parts.items():
        a = np.asarray(a, np.float32).reshape(P, -1)
        CONST[name] = (at, at + a.shape[1])
        at += a.shape[1]
        out.append(a)
    return np.ascontiguousarray(np.concatenate(out, 1))


def decay_table():
    i = np.arange(P, dtype=np.float64)
    log_g = np.log1p(-(2.0 ** (-5.0 - np.arange(NH))))
    rel = i[None, :] - i[:, None]
    table = np.empty((P, 2, NH, P))
    for h in range(NH):
        table[:, 0, h] = np.where(rel >= 0, np.exp(log_g[h] * np.maximum(rel, 0)), 0)
        table[:, 1, h] = np.exp(log_g[h] * (P + rel))
    return (table * HD ** -0.5).astype(np.float32).reshape(P, -1)


STREAM = (
    [("ada", j, "act") for j in range(4)] + [("win", j, "act") for j in range(7)]
    + [("ada", j, "act") for j in range(4, 10)] + [("wout", j, "dve") for j in range(2)]
    + [("wq", j, "act") for j in range(4)] + [("dn", j, "act") for j in range(LEAD)]
    + [("ada", j, "act") for j in range(10, 12)]
    + [x for j in range(STEPS) for x in ([("dn", j + LEAD, "act")] if j + LEAD < STEPS else []) + [("ex", j, None)]]
    + [("win2", j, "act") for j in range(5)] + [("cmp", j, None) for j in range(2)] + [("win2", 5, "act")]
    + [("wo", j, "dve") for j in range(2)]
    + [("up", 0, "act")]
    + [x for j in range(1, 8) for x in (("up", j, "act"), ("down", j - 1, None))] + [("down", 7, None)]
)
NTH = {(k, j): n for n, (k, j, _) in enumerate(STREAM)}


def emptied():
    found, count, place = {}, {"act": 0, "dve": 0}, 0
    for n, (_, _, who) in enumerate(STREAM):
        if who:
            count[who] += 1
            found[n] = (place, who, count[who])
            place += 1
    return found


RAW = ("ada", "cmp")
SPLIT_BEFORE = [sum(k not in RAW for k, _, _ in STREAM[:n]) * PARTS for n in range(len(STREAM) + 1)]
RAW_BEFORE = [sum(k in RAW for k, _, _ in STREAM[:n]) for n in range(len(STREAM) + 1)]
BY_POOL = [NTH["wq", j] for j in range(2, 4)] + [NTH["dn", j] for j in range(LEAD)]
POOL0, POOL1 = SPLIT_BEFORE[BY_POOL[0]], SPLIT_BEFORE[BY_POOL[-1] + 1]
EMPTIED = emptied()
BY_PLACE = {p: (who, c) for p, who, c in EMPTIED.values()}


class Chain:

    def __init__(self, eng, sem):
        self.eng, self.sem, self.n = eng, sem, 0

    def __call__(self, ins):
        self.n += 1
        ins.then_inc(self.sem, 1)
        self.eng.wait_ge(self.sem, self.n)

    def restart(self):
        self.eng.sem_clear(self.sem)
        self.n = 0


def two_blocks(nc, a, out, stop=None):
    ctx = ExitStack()
    with ctx:
        def sb(name, shape, dt=F32):
            return ctx.enter_context(nc.sbuf_tensor(name, shape, dt))

        def sem(name):
            return ctx.enter_context(nc.semaphore(name))

        n_const = a["const"].shape[1]
        const = sb("const", [P, n_const])
        x_tok = sb("x_tok", [P, NB, D])
        h_tok = sb("h_tok", [P, NB, D])
        hT_hi = sb("hT_hi", [P, KC, T], F32R)
        hT_lo = sb("hT_lo", [P, KC, T], F32R)
        mod = sb("mod", [P, 4, D])
        gain1 = sb("gain1", [P, 2, D])
        late = sb("late", [P, 1536])
        small = sb("small", [P, 7, HD])
        wring = sb("wring", [P, RING, SLOT])
        w_hi = sb("w_hi", [P, PARTS, PART], F32R)
        w_lo = sb("w_lo", [P, PARTS, PART], F32R)
        csilu = sb("csilu", [P, 2, KC])
        adab = sb("adab", [12, CHUNK])
        posi = sb("posi", [P, NB], I32)
        posf = sb("posf", [P, NB])
        st = sb("st", [P, 10, 16])
        cbias = sb("cbias", [P, 2, 2])
        w2 = sb("w2", [P, 2, 2, HD])
        b2 = sb("b2", [1, 2, HD])
        topi = sb("topi", [P, NB, 2, PK], U32)
        besti1 = sb("besti1", [P, NB, PK], U32)
        besti = sb("besti", [P, NB, 2, PH, PK], U32)
        cur = sb("cur", [P, 2, 3, TT])
        gatec = sb("gatec", [P, NB, NH, 3])
        mx = sb("mx", [P, 2, NB, R])
        sm = sb("sm", [P, 2, NB, R])
        kcn = sb("kcn", [64, 2, HD])
        kcq = sb("kcq", [64, HD])
        kcst = sb("kcst", [64, 4])
        kcmpT = sb("kcmpT", [P, 64])
        peT = sb("peT", [P, 2, NPAIR])
        with ExitStack() as peer_only:
            a_hi = peer_only.enter_context(nc.sbuf_tensor("a_hi", [P, 4, T], F32R))
            a_lo = peer_only.enter_context(nc.sbuf_tensor("a_lo", [P, 4, T], F32R))
            peer_arena = peer_only.enter_context(nc.sbuf_tensor("peer_arena", [P, 14336], F32))
        arena = sb("arena", [P, 16384])
        ps = ctx.enter_context(nc.psum_tensor("ps", [P, 8, 512], F32))
        psf = ps[:, :, :].rearrange("p b n -> p (b n)")

        def con(name, *dims):
            lo, hi = CONST[name]
            v = const[:, lo:hi]
            return v

        ident, ones = con("ident"), con("ones")
        SHIFT, SCALE, GATE1, GATE2 = (mod[:, k, :] for k in range(4))

        proj = arena[:, 0:NB * 3584].rearrange("p (b n) -> p b n", b=NB)
        qT = arena[:, 7168:8192].rearrange("p (c t) -> p c t", c=4)
        kT = arena[:, 8192:9216].rearrange("p (c t) -> p c t", c=4)
        tiles = arena[:, 9216:15360].rearrange("p (k n) -> p k n", k=4)
        trig = arena[:, 15360:15488].rearrange("p (f b n) -> p f b n", f=2, b=NB)
        ang = tiles[:, 0, 0:64].rearrange("p (b n) -> p b n", b=NB)
        turns = tiles[:, 0, 64:192].rearrange("p (f b n) -> p f b n", f=2, b=NB)
        ang2 = tiles[:, 0, 192:320].rearrange("p (f b n) -> p f b n", f=2, b=NB)
        decay = arena[:, 13312:15360].rearrange("p (k h i) -> p k h i", k=2, h=NH)
        rgain = late[:, 0:HW]

        def heads(v):
            return v.rearrange("p b (h d) -> p b h d", d=HD)

        def every_other(v, par):
            return v.rearrange("p (h u d) -> p u h d", u=2, d=HD)[:, par, :, :]

        h_flat = h_tok[:, :, :].rearrange("p b n -> p (b n)")
        spare = gain1[:, :, :].rearrange("p k n -> p (k n)")
        qryT = peer_arena[:, 0:16 * T].rearrange("p (c t) -> p c t", c=16)
        onehot = peer_arena[:, 0:4096].rearrange("p (k s t n) -> p k s t n", k=2, s=2, t=TT)
        score = peer_arena[:, 4096:8192].rearrange("p (b h n) -> p b h n", b=NB, h=PH)
        gates_in = peer_arena[:, 4096:8192].rearrange("p (s g f t) -> p s g f t", s=2, g=T // 16, t=16)
        keys = peer_arena[:, 10240:12288].rearrange("p (c n) -> p c n", n=NKEY)
        acts = peer_arena[:, 8192:12288].rearrange("p (s f t) -> p s f t", s=AR, f=EF)
        spread = [v.rearrange("p (n t) -> p n t", t=16) for v in (peer_arena[:, 12288:14336], spare)]
        pick = peer_arena[:, 0:4096].rearrange("p (b h i j) -> p b h i j", b=NB, h=PH, j=PK)
        sc2, cand, cand2 = (h_flat[:, k * 512:(k + 1) * 512].rearrange("p (b n) -> p b n", b=NB) for k in range(3))
        best1 = h_flat[:, 1536:1568].rearrange("p (b n) -> p b n", b=NB)
        top = h_flat[:, 1568:1632].rearrange("p (b k n) -> p b k n", b=NB, k=2)
        best = h_flat[:, 1632:1888].rearrange("p (b h n) -> p b h n", b=NB, h=PH)
        gsum = h_flat[:, 1888:1904].rearrange("p (b h) -> p b h", b=NB)
        topf = spare[:, 0:512].rearrange("p (b h k n) -> p b h k n", b=NB, h=PH, k=2)
        bestf = spare[:, 512:1024].rearrange("p (b k h n) -> p b k h n", b=NB, k=2, h=PH)
        sel = late[:, 0:768].rearrange("p (b k n) -> p b k n", b=NB, k=3)
        selT = late[:, 768:1536].rearrange("p (k t) -> p k t", k=3)
        gates_dram = nc.dram_tensor("gates_by_expert", (T // 16, P, NKEY * 16), F32, kind="Internal").ap()

        z = arena[:, 0:NB * ZW].rearrange("p (b n) -> p b n", b=NB)
        o = NB * ZW
        qT2 = arena[:, o:o + 1024].rearrange("p (c t) -> p c t", c=4)
        kT2 = arena[:, o + 1024:o + 2048].rearrange("p (r g t) -> p r g t", r=2, g=NG)
        kvA = arena[:, o + 2048:o + 3072].rearrange("p (v g t) -> p v g t", v=2, g=NG)
        blkT = arena[:, o + 3072:o + 4032].rearrange("p (v m c) -> p v m c", v=2, m=NPAIR)
        hdnT = arena[:, o + 4032:o + 4160].rearrange("p (f c) -> p f c", f=2)
        o += 4288
        ptile = arena[:, o:o + 3072].rearrange("p (k n) -> p k n", k=2)
        pT = arena[:, o + 3072:o + 4608].rearrange("p (k r t) -> p k r t", k=3, r=R)
        kdup = arena[:, o:o + 1024].rearrange("p (b r g u d) -> p b r g u d", b=NB, r=2, g=NG, u=2)
        o += 4608
        tmp = arena[:, o:o + 1024].rearrange("p (b n) -> p b n", b=NB)
        sqq = ptile[:, 0, 0:1024].rearrange("p (b h d) -> p b h d", b=NB, d=HD)
        tmp_k = ptile[:, 1, 1024:1280].rearrange("p (b g d) -> p b g d", b=NB, g=NG)
        kvdup = arena[:, o:o + 1024].rearrange("p (b v g u d) -> p b v g u d", b=NB, v=2, g=NG, u=2)
        hdnV = arena[:, o + 1024:o + 1536].rearrange("p (f g r n) -> p f g r n", f=2, g=NG, r=R)
        assert o + 1536 <= 16384
        gmix, gout, gffn = SHIFT, SCALE, GATE1
        sh1 = h_tok[:, :, HW:D]
        sh2 = GATE2.rearrange("p (b n) -> p b n", b=NB)
        convw = late[:, 0:3 * HW].rearrange("p (k n) -> p k n", k=3)
        vbd = spare[:, 0:512].rearrange("p (g r d) -> p g r d", g=NG, r=R)
        pcmp = spare[:, 512:1024].rearrange("p (b h n) -> p b h n", b=NB, h=NH)
        pcT = spare[:, 1024:1536].rearrange("p (b g t) -> p b g t", b=NB, g=NG)
        pcs = spare[:, 1536:1792].rearrange("p (c n) -> p c n", n=CSTEP)
        cst = spare[:, 1792:1840].rearrange("p (k c) -> p k c", k=3)
        uT = arena[:, 4096:6144].rearrange("p (s f t) -> p s f t", s=2, f=4)

        ld_const, ld_x, ld_c, ld_gain, ld_early, ld_keys, ld_gates, ld_late, ld_cmp = (
            sem(s) for s in ("ld_const", "ld_x", "ld_c", "ld_gain", "ld_early", "ld_keys", "ld_gates", "ld_late", "ld_cmp"))
        w_in_slot = [sem(f"w_in_slot{k}") for k in range(RING)]
        w_used = sem("w_used")
        split_hi = sem("split_hi")
        split_lo = sem("split_lo")
        split_lo_pool = sem("split_lo_pool")
        parts_used = sem("parts_used")
        emptied_by = {"act": sem("emptied_by_act"), "dve": sem("emptied_by_dve")}
        dve_own, act_own, pool_own = sem("dve_own"), sem("act_own"), sem("pool_own")
        names = """silu_c sumsq var std h_ready tr_done tr_copied_act tr_copied_dve angles trig_ready
        rot_ready ret_scores ret_decayed ret_y ret_y_out ret_gate var_s std_s sbq_ready sb_z sb_abs sb_exp sb_L sb_ls sb_cum
        sb_logw sb_w sb_y sb_y_out y_ready x1_ready qry_ready sub_done sub_out
        tr_hi a_hi_ready a_lo_ready score_max exp_done sel_ready sel_turned cur_ready onehot_raw onehot_ready onehot_used spread_out weighed x2_ready
        late_free ksum zrms zstd kv_ready kv_copied blk_ready hdn hdn_out kcmp kvar kstd kcn_ready vcmp_out kct_copied
        s_done s_max p_ready p_masked p_sum pt_done pt_out o_done o_out cs_done c_max c_exp c_ready c_tr c_out co_done co_out
        u_ready u_shifted conv_out fvar fstd relu_done u2_ready fin x_out stored choose0 choose1""".split()
        S = {n: sem(n) for n in names}
        gates_stored = [sem(f"gates_stored{k}") for k in range(2)]
        gates_landed = [sem(f"gates_landed{k}") for k in range(2)]

        block = ctx.enter_context(nc.Block())

        def emptied_count(kind, j):
            return EMPTIED[NTH[kind, j]][2]

        def pair(kind, j):
            return 2 * (EMPTIED[NTH[kind, j]][0] % 2)

        def stands(eng, kind, j):
            n = NTH[kind, j]
            if kind in RAW:
                eng.wait_ge(w_used, RAW_BEFORE[n + 1])
            else:
                eng.wait_ge(parts_used, SPLIT_BEFORE[n + 1])

        def slot_left(eng, n):
            if STREAM[n][0] in RAW:
                eng.wait_ge(w_used, RAW_BEFORE[n + 1])
            elif n in BY_POOL:
                eng.wait_ge(split_lo_pool, SPLIT_BEFORE[n + 1] - POOL0)
            else:
                eng.wait_ge(split_lo, rests(SPLIT_BEFORE[n + 1]))

        def rests(parts):
            if isinstance(parts, int) and parts <= POOL0:
                return parts
            return parts - (POOL1 - POOL0)

        def part_of(kind, raw, u, cols=CHUNK):
            if kind in ("wq", "up"):
                return raw.rearrange("p (k n) -> p k n", n=CHUNK)[:, :, u * P:(u + 1) * P]
            part = raw[:, u * PART:(u + 1) * PART]
            return part.rearrange("p (k n) -> p k n", n=CHUNK)[:, :, 0:cols]

        def split_part(kind, v, u, cols=CHUNK):
            if kind in ("wq", "up"):
                return v[:, u, :].rearrange("p (k n) -> p k n", n=P)
            return v[:, u, :].rearrange("p (k n) -> p k n", n=CHUNK)[:, :, 0:cols]

        def bank_set(i):
            return 4 - 4 * (i % 2)

        def width(kind, j):
            return min(CHUNK, ZW - j * CHUNK) if kind == "win2" else CHUNK

        down0, down3, out3 = NTH["dn", 0], NTH["dn", LEAD], EMPTIED[NTH["dn", LEAD]][2]
        TURNS = (STEPS - LEAD) // AR

        def part0(i):
            return i * (2 * PARTS) + SPLIT_BEFORE[down3]

        def slot_parts(i):
            if has_down(i):
                return part0(i), part0(i) + PARTS
            return None, SPLIT_BEFORE[NTH["ex", i]]

        def ring_turn(i, up):
            if not isinstance(i, int):
                n = down3 + up
                return n % RING, i * 16 + 16 * (n // RING + 1)
            n = NTH["ex", i] if up else NTH["dn", i + LEAD]
            return n % RING, 16 * (n // RING + 1)

        def expert_steps(fori, body):
            with fori(0, TURNS) as turn:
                for k in range(AR):
                    body(turn * AR + k, k)
            for i in range(TURNS * AR, STEPS):
                body(i, i % AR)

        def has_down(i):
            return not isinstance(i, int) or i + LEAD < STEPS

        @block.sync
        def _(sp):
            sp.dma_start(csilu[:, 0, :], a["c"]).then_inc(ld_c, 16)
            sp.dma_start(adab[:, :], a["ada_b"]).then_inc(ld_c, 16)
            sp.dma_start(const[:, :], a["const"]).then_inc(ld_const, 16)
            sp.dma_start(x_tok[:, :, :], a["x"].rearrange("(b p) n -> p b n", p=P)).then_inc(ld_x, 16)
            sp.dma_start(posi[:, :], a["positions"].rearrange("(b p) -> p b", p=P),
                         allow_slow_non_contiguous=True).then_inc(ld_x, 16)

            def weights(n):
                kind, j, _ = STREAM[n]
                slot = wring[:, n % RING, :]
                if n >= RING:
                    slot_left(sp, n - RING)
                cols = slice(j * CHUNK, (j + 1) * CHUNK)
                if kind == "dn":
                    src, dst = a["peer_down"][j * P:(j + 1) * P, :], slot
                elif kind == "cmp":
                    src = a["w_cmp1"][j].rearrange("(m p) n -> p m n", p=P)
                    dst = slot.rearrange("p (m n) -> p m n", n=CF)
                elif kind == "down":
                    src = a["w_down"][cols, :].rearrange("(f p) n -> p f n", p=P)
                    dst = slot.rearrange("p (f n) -> p f n", n=D)
                else:
                    w = a[{"ada": "ada_w", "win": "w_in", "wout": "w_out", "wq": "w_query", "win2": "w_in2",
                           "wo": "w_o", "up": "w_up"}[kind]]
                    last = min((j + 1) * CHUNK, w.shape[1])
                    src = w[:, j * CHUNK:last].rearrange("(k p) n -> p k n", p=P)
                    dst = slot.rearrange("p (k n) -> p k n", k=KC)[:, :, 0:last - j * CHUNK]
                sp.dma_start(dst, src).then_inc(w_in_slot[n % RING], 16)

            for n in range(RING):
                weights(n)
            sp.dma_start(gain1[:, 0, :], a["gain1"].partition_broadcast(P)).then_inc(ld_gain, 16)
            sp.dma_start(gain1[:, 1, :], a["gain2"].partition_broadcast(P)).then_inc(ld_gain, 16)
            sp.dma_start(arena[:, 13312:15360], a["decay"]).then_inc(ld_early, 16)
            sp.dma_start(rgain, a["ret_gain"].partition_broadcast(P)).then_inc(ld_early, 16)
            for k, name in enumerate(("sb_q", "sb_k", "sb_out", "g_q")):
                sp.dma_start(small[:, k, :], a[name].partition_broadcast(P)).then_inc(ld_early, 16)
            sp.dma_start(small[:, 4:7, :].rearrange("p k d -> p (k d)"),
                         a["g_k"].partition_broadcast(P)).then_inc(ld_early, 16)
            sp.dma_start(peT[:, :, :], a["pe"]).then_inc(ld_cmp, 16)
            sp.dma_start(cbias[:, :, :], a["b_cmp1"]).then_inc(ld_cmp, 16)
            sp.dma_start(w2[:, :, :, :], a["w_cmp2"].rearrange("v (f p) d -> p v f d", p=P)).then_inc(ld_cmp, 16)
            sp.dma_start(b2[:, :, :], a["b_cmp2"]).then_inc(ld_cmp, 16)
            for n in range(RING, NTH["wq", RING]):
                weights(n)
            sp.wait_ge(S["h_ready"], 4)
            sp.dma_start(keys.rearrange("p c n -> p (c n)"), a["keys"]).then_inc(ld_keys, 16)
            for n in range(NTH["wq", RING], down3):
                weights(n)

            def expert_slots(i, k):
                down, up = slot_parts(i)
                if has_down(i):
                    par, _ = ring_turn(i, 0)
                    if isinstance(i, int):
                        slot_left(sp, NTH["dn", i + LEAD] - RING)
                    elif k == 0:
                        slot_left(sp, down3 - RING)
                        sp.wait_ge(split_lo, rests(down - PARTS))
                    else:
                        sp.wait_ge(split_lo, rests(down - PARTS))
                    sp.dma_start(wring[:, par, :], a["peer_down"][bass.ds(i * P + LEAD * P, P), :])\
                        .then_inc(w_in_slot[par], 16)
                par, _ = ring_turn(i, 1)
                if k == 0 and not isinstance(i, int):
                    slot_left(sp, down3 + 1 - RING)
                sp.wait_ge(split_lo, rests(up - PARTS))
                sp.dma_start(wring[:, par, :].rearrange("p (f n) -> p f n", n=D),
                             a["peer_up"][bass.ds(i * CHUNK, CHUNK), :].rearrange("(f p) n -> p f n", p=P))\
                    .then_inc(w_in_slot[par], 16)

            for v, name in ((gmix, "g_mix"), (gout, "g_out"), (gffn, "g_ffn")):
                sp.dma_start(v, a[name].partition_broadcast(P)).then_inc(ld_late, 16)
            expert_steps(sp.Fori, expert_slots)
            first_late = NTH["win2", 0]
            for n in range(first_late, first_late + RING):
                weights(n)
            sp.wait_ge(S["late_free"], 1)
            sp.dma_start(late[:, 0:3 * HW], a["conv_w"].partition_broadcast(P)).then_inc(ld_late, 16)
            for n in range(first_late + RING, len(STREAM)):
                weights(n)
            for b in range(NB):
                sp.wait_ge(S["x_out"], b + 1)
                sp.dma_start(out[b * P:(b + 1) * P, :], x_tok[:, b, :]).then_inc(S["stored"], 16)
            sp.wait_ge(S["stored"], 16 * NB)

        @block.tensor
        def _(pe):
            def slot(n, inner):
                pe.wait_ge(w_in_slot[n % RING], 16 * (n // RING + 1))
                return wring[:, n % RING, :].rearrange("p (k n) -> p k n", n=inner)

            def free_banks(n):
                place = EMPTIED[n][0]
                if place >= 2:
                    who, count = BY_PLACE[place - 2]
                    pe.wait_ge(emptied_by[who], count)
                return 2 * (place % 2)

            def ada(j):
                n = NTH["ada", j]
                w, bank = slot(n, CHUNK), free_banks(n)
                for k in range(KC):
                    pe.matmul(ps[:, bank, :], csilu[:, 1, k:k + 1].to_broadcast([P, P]), w[:, k, :],
                              start=(k == 0), stop=False)
                pe.matmul(ps[:, bank, :], ident[0:12, j:j + 1].to_broadcast([12, P]), adab[:, :],
                          start=False, stop=True).then_inc(w_used, 1)

            def split_landed(n, u):
                if n in BY_POOL:
                    pe.wait_ge(split_lo_pool, SPLIT_BEFORE[n] - POOL0 + u + 1)
                else:
                    pe.wait_ge(split_lo, rests(SPLIT_BEFORE[n] + u + 1))

            def token_part(kind, u, bank, cols):
                hi, lo = (split_part(kind, v, u, cols) for v in (w_hi, w_lo))
                for kk in range(2):
                    k = 2 * u + kk
                    for b in range(NB):
                        t = slice(b * P, (b + 1) * P)
                        o = ps[:, bank + b, 0:cols]
                        pe.matmul(o, hT_hi[:, k, t], hi[:, kk, :], start=(k == 0), stop=False)
                        pe.matmul(o, hT_hi[:, k, t], lo[:, kk, :], start=False, stop=False)
                        mm = pe.matmul(o, hT_lo[:, k, t], hi[:, kk, :], start=False, stop=(k == KC - 1))
                mm.then_inc(parts_used, 1)

            def column_part(bank, u):
                hi, lo = (v[:, u, :].rearrange("p (k n) -> p k n", n=P) for v in (w_hi, w_lo))
                o = psf[:, bank * 512 + u * T:bank * 512 + (u + 1) * T]
                for k in range(KC):
                    pe.matmul(o, hi[:, k, :], hT_hi[:, k, :], start=(k == 0), stop=False)
                    pe.matmul(o, hi[:, k, :], hT_lo[:, k, :], start=False, stop=False)
                    mm = pe.matmul(o, lo[:, k, :], hT_hi[:, k, :], start=False, stop=(k == KC - 1))
                mm.then_inc(parts_used, 1)

            def row_part(u, first, last):
                hi, lo = (v[:, u, :].rearrange("p (s n) -> p s n", n=512) for v in (w_hi, w_lo))
                for b in range(NB):
                    t = slice(b * P, (b + 1) * P)
                    for half in range(2):
                        o = ps[:, 4 + 2 * b + half, :]
                        pe.matmul(o, a_hi[:, u, t], hi[:, half, :], start=first, stop=False, skip_group_check=True)
                        pe.matmul(o, a_hi[:, u, t], lo[:, half, :], start=False, stop=False, skip_group_check=True)
                        mm = pe.matmul(o, a_lo[:, u, t], hi[:, half, :], start=False, stop=last, skip_group_check=True)
                mm.then_inc(parts_used, 1)

            def by_tokens(kind, j):
                n = NTH[kind, j]
                bank = free_banks(n)
                for u in range(PARTS):
                    split_landed(n, u)
                    token_part(kind, u, bank, width(kind, j))

            def by_columns(kind, j):
                n = NTH[kind, j]
                bank = free_banks(n)
                for u in range(PARTS):
                    split_landed(n, u)
                    column_part(bank, u)

            def turn_round(src, what):
                for k in range(what):
                    for b in range(NB):
                        at = 4 * 512 + k * T + b * P
                        mm = pe.transpose(psf[:, at:at + P], src(k, b), ident)
                mm.then_inc(S["tr_done"], 1)

            def copied(r):
                pe.wait_ge(S["tr_copied_act"], r)
                pe.wait_ge(S["tr_copied_dve"], r)

            def head_scores(bank, b4):
                for n, (jb, ib) in enumerate(PAIRS):
                    for c in range(4):
                        lo = HD * b4
                        mm = pe.matmul(ps[:, bank + n, c * P:(c + 1) * P], kT[lo:lo + HD, c, jb * P:(jb + 1) * P],
                                       qT[lo:lo + HD, c, ib * P:(ib + 1) * P], start=True, stop=True)
                return mm

            def head_values(bank, tile, v, b4):
                for hh in range(4):
                    col = (2 * hh + b4) * HD
                    w = [tile[:, n * 512 + hh * P:n * 512 + (hh + 1) * P] for n in range(3)]
                    pe.matmul(ps[:, bank, hh * HD:(hh + 1) * HD], w[0], v[:, 0, col:col + HD], start=True, stop=True)
                    at = 4 * HD + hh * HD
                    pe.matmul(ps[:, bank, at:at + HD], w[1], v[:, 0, col:col + HD], start=True, stop=False)
                    mm = pe.matmul(ps[:, bank, at:at + HD], w[2], v[:, 1, col:col + HD], start=False, stop=True)
                return mm

            pe.wait_ge(ld_const, 16)
            pe.wait_ge(ld_c, 32)
            pe.wait_ge(S["silu_c"], 1)
            for j in range(4):
                ada(j)
            pe.wait_ge(S["h_ready"], 2)
            turn_round(lambda k, b: h_tok[:, b, k * P:(k + 1) * P], KC)
            copied(1)
            for j in range(7):
                by_tokens("win", j)
            ada(4)

            pe.wait_ge(S["rot_ready"], 2)
            turn_round(lambda k, b: h_tok[:, b, k * P:(k + 1) * P], KC)
            ada(5)
            copied(2)
            head_scores(4, 0).then_inc(S["ret_scores"], 1)
            ada(6)
            pe.wait_ge(S["ret_decayed"], 1)
            head_scores(4, 1).then_inc(S["ret_scores"], 1)
            pe.wait_ge(emptied_by["act"], emptied_count("win", 2))
            head_values(7, tiles[:, 0, :], proj[:, :, 2 * HW:3 * HW], 0).then_inc(S["ret_y"], 1)
            ada(7)
            pe.wait_ge(S["ret_decayed"], 2)
            pe.wait_ge(S["ret_y_out"], 1)
            head_values(7, tiles[:, 1, :], proj[:, :, 2 * HW:3 * HW], 1).then_inc(S["ret_y"], 1)
            ada(8)

            pe.wait_ge(S["sbq_ready"], 2)
            pe.wait_ge(S["ret_y_out"], 2)
            turn_round(lambda k, b: proj[:, b, (4 * HW + k * P):(4 * HW + (k + 1) * P)], KC)
            ada(9)
            copied(3)
            pe.wait_ge(emptied_by["act"], emptied_count("ada", 9))
            for b4 in range(2):
                head_scores(4 - 4 * b4, b4).then_inc(S["sb_z"], 1)
            for b4 in range(2):
                bank, ls = 4 - 4 * b4, tiles[:, 2 * b4 + 1, :].rearrange("p (k n) -> p k n", k=3)
                pe.wait_ge(S["sb_ls"], b4 + 1)
                pe.matmul(ps[:, bank, :], con("after"), ls[:, 0, :], start=True, stop=True)
                pe.matmul(ps[:, bank + 1, :], con("after"), ls[:, 1, :], start=True, stop=False)
                pe.matmul(ps[:, bank + 1, :], ones, ls[:, 2, :], start=False, stop=True)
                pe.matmul(ps[:, bank + 2, :], con("after"), ls[:, 2, :], start=True, stop=True)\
                    .then_inc(S["sb_cum"], 1)
            for b4 in range(2):
                pe.wait_ge(S["sb_w"], b4 + 1)
                head_values(7 - 4 * b4, tiles[:, 2 * b4, :], proj[:, :, 6 * HW:7 * HW], b4)\
                    .then_inc(S["sb_y"], 1)
            pe.wait_ge(S["y_ready"], 2)
            turn_round(lambda k, b: proj[:, b, k * P:(k + 1) * P], KC)
            copied(4)
            for j in range(2):
                by_tokens("wout", j)
            pe.wait_ge(S["h_ready"], 4)
            turn_round(lambda k, b: h_tok[:, b, k * P:(k + 1) * P], KC)
            copied(5)
            def key_scores(j):
                pe.wait_ge(emptied_by["act"], emptied_count("wq", j))
                if j >= 2:
                    pe.wait_ge(S["sub_out"], j - 1)
                for b in range(NB):
                    for i in range(4):
                        mm = pe.matmul(ps[:, 4 + 2 * (j % 2) + b, i * NKEY:(i + 1) * NKEY],
                                       qryT[:, 4 * j + i, b * P:(b + 1) * P], keys[:, 4 * j + i, :], start=True, stop=True)
                mm.then_inc(S["sub_done"], 1)

            by_columns("wq", 0)
            pe.wait_ge(ld_keys, 16)
            for j in range(1, 4):
                by_columns("wq", j)
                key_scores(j - 1)
            by_columns("dn", 0)
            key_scores(3)
            for j in range(1, LEAD):
                by_columns("dn", j)
            for j in (10, 11):
                ada(j)
            pe.wait_ge(S["sel_ready"], NB)
            for b in range(NB):
                for k in range(3):
                    mm = pe.transpose(ps[:, 4 + b, k * P:(k + 1) * P], sel[:, b, k, :], ident)
            mm.then_inc(S["sel_turned"], 1)
            with pe.Fori(0, T // (4 * TT)) as turn:
                for q in range(4):
                    group, e = turn * 4 + q, q % 2
                    pe.wait_ge(S["onehot_ready"], group + 1)
                    pe.wait_ge(S["spread_out"], group + 1)
                    for t in range(TT):
                        at = (4 + 2 * e) * 512 + t * NKEY
                        mm = pe.matmul(psf[:, at:at + NKEY], onehot[:, 1, e, t, :], onehot[:, 0, e, t, :],
                                       start=True, stop=True)
                    mm.then_inc(S["onehot_used"], 1)

            pe.wait_ge(S["spread_out"], 2 + T // TT)
            for bank in range(4, 8):
                pe.matmul(ps[:, bank, 0:P], ones[0:1, :], con("after")[0:1, :], start=True, stop=False,
                          skip_group_check=True)

            def expert_products(i, k):
                down, up = slot_parts(i)
                if has_down(i):
                    pe.wait_ge(emptied_by["act"], i + (out3 - 2))
                    for u in range(PARTS):
                        pe.wait_ge(split_lo, rests(down + (u + 1)))
                        column_part(2 * ((EMPTIED[down0][0] + k + LEAD) % 2), u)
                for u in range(PARTS):
                    pe.wait_ge(S["a_lo_ready"], i * PARTS + (u + 1))
                    pe.wait_ge(split_lo, rests(up + (u + 1)))
                    row_part(u, False, False)

            expert_steps(pe.Fori, expert_products)

            pe.wait_ge(S["h_ready"], 6)
            turn_round(lambda k, b: h_tok[:, b, k * P:(k + 1) * P], KC)
            copied(6)
            for j in range(3):
                by_tokens("win2", j)
            pe.wait_ge(S["kv_ready"], 1)
            for v in range(2):
                for g in range(NG):
                    for b in range(NB):
                        at = 4 * 512 + (v * NG + g) * T + b * P
                        mm = pe.transpose(psf[:, at:at + P],
                                          kvdup[:, b, v, g, :, :].rearrange("p u d -> p (u d)"), ident)
            mm.then_inc(S["c_tr"], 1)
            for j in (3, 4):
                by_tokens("win2", j)
            pe.wait_ge(S["blk_ready"], 1)
            for v in range(2):
                w = slot(NTH["cmp", v], CF)
                for f in range(2):
                    at = 6 * 512 + (2 * v + f) * 32
                    for m in range(NPAIR):
                        mm = pe.matmul(psf[:, at:at + 2 * NCMP], w[:, m, f * P:(f + 1) * P], blkT[:, v, m, :],
                                       start=(m == 0), stop=(m == NPAIR - 1))
                mm.then_inc(w_used, 1)
            by_tokens("win2", 5)

            pe.wait_ge(S["kv_ready"], 2)
            pe.wait_ge(S["kv_copied"], 1)
            pe.wait_ge(S["hdn_out"], 1)
            turn_round(lambda k, b: z[:, b, k * P:(k + 1) * P] if k < 4 else
                       kdup[:, b, (k - 4) // 2, (k - 4) % 2, :, :].rearrange("p u d -> p (u d)"), KC)
            pe.wait_ge(emptied_by["act"], emptied_count("win2", 5))
            pe.wait_ge(ld_cmp, 64)
            for f in range(2):
                pe.matmul(ps[0:64, 3, 0:HD], hdnT[:, f, :], w2[:, 0, f, :], start=(f == 0), stop=False)
            pe.matmul(ps[0:64, 3, 0:HD], ones[0:1, 0:64], b2[:, 0, :], start=False, stop=True).then_inc(S["kcmp"], 1)
            for g in range(NG):
                for f in range(2):
                    pe.matmul(ps[:, 0, g * HD:(g + 1) * HD],
                              hdnV[:, f, g, :, :].rearrange("p r n -> p (r n)"),
                              w2[:, 1, f, :], start=(f == 0), stop=False)
                mm = pe.matmul(ps[:, 0, g * HD:(g + 1) * HD], ones[0:1, :], b2[:, 1, :], start=False, stop=True)
            mm.then_inc(S["kcmp"], 1)
            copied(7)

            def scores(i):
                br, lo = i // 2, HD * (i % 2)
                for r in range(R):
                    for b in range(NB):
                        at = bank_set(i) * 512 + (r * P if b == 0 else 512 + r * T)
                        mm = pe.matmul(psf[:, at:at + (b + 1) * P], qT2[lo:lo + HD, r, b * P:(b + 1) * P],
                                       kT2[lo:lo + HD, br, r // 2, 0:(b + 1) * P], start=True, stop=True)
                mm.then_inc(S["s_done"], 1)

            def weigh(i):
                br, pt, bank = i // 2, ptile[:, i % 2, :], bank_set(i)
                pe.wait_ge(S["p_ready"], i + 1)
                for n, (jb, ib) in enumerate(PAIRS):
                    for r in range(R):
                        lo = r * P if ib == 0 else 512 + r * T + jb * P
                        at = (bank + n) * 512 + r * P
                        mm = pe.transpose(psf[:, at:at + P], pt[:, lo:lo + P], ident)
                mm.then_inc(S["pt_done"], 1)
                pe.wait_ge(S["pt_out"], i + 1)
                if i >= 2:
                    pe.wait_ge(S["o_out"], i - 1)
                for r in range(R):
                    col = (Z_VS, Z_VW)[br] + (r // 2) * HD
                    v = [z[:, b, col:col + HD] for b in range(NB)]
                    o = ps[:, bank + 3, :]
                    pe.matmul(o[:, r * HD:(r + 1) * HD], pT[:, 0, r, :], v[0], start=True, stop=True)
                    at = (R + r) * HD
                    pe.matmul(o[:, at:at + HD], pT[:, 1, r, :], v[0], start=True, stop=False)
                    mm = pe.matmul(o[:, at:at + HD], pT[:, 2, r, :], v[1], start=False, stop=True)
                mm.then_inc(S["o_done"], 1)

            scores(0)
            pe.wait_ge(S["kcn_ready"], 1)
            pe.transpose(ps[:, 3, 128:192], kcn[:, :, :].rearrange("p u d -> p (u d)"), ident[0:64, 0:64])\
                .then_inc(S["c_tr"], 1)
            pe.wait_ge(S["kct_copied"], 1)
            for b in range(NB):
                for h in range(NH):
                    lo, g = HD * (h % 2), h // R
                    at = (3 + 4 * (h % 2)) * 512 + (b * R + h // 2) * CSTEP
                    mm = pe.matmul(psf[:, at:at + CSTEP], qT2[lo:lo + HD, h // 2, b * P:(b + 1) * P],
                                   kcmpT[lo:lo + HD, g * 32:g * 32 + CSTEP], start=True, stop=True)
            mm.then_inc(S["cs_done"], 1)
            pe.wait_ge(S["vcmp_out"], 1)
            scores(1)
            pe.wait_ge(S["c_max"], 1)
            weigh(0)
            scores(2)
            weigh(1)
            scores(3)
            weigh(2)
            pe.wait_ge(S["c_ready"], 1)
            for b in range(NB):
                for g in range(NG):
                    at = 4 * 512 + (b * NG + g) * P
                    mm = pe.transpose(psf[:, at:at + P],
                                      pcmp[:, b, g * R:(g + 1) * R, :].rearrange("p r n -> p (r n)"), ident)
            mm.then_inc(S["c_tr"], 1)
            weigh(3)
            pe.wait_ge(S["c_out"], 1)
            for b in range(NB):
                for g in range(NG):
                    at = (5 + b) * 512 + g * 256
                    mm = pe.matmul(psf[:, at:at + 256], pcT[:, b, g, :],
                                   vbd[:, g, :, :].rearrange("p r d -> p (r d)"), start=True, stop=True)
            mm.then_inc(S["co_done"], 1)

            pe.wait_ge(S["h_ready"], 8)
            turn_round(lambda k, b: h_tok[:, b, k * P:(k + 1) * P], KC)
            copied(8)
            for j in range(2):
                by_tokens("wo", j)

            pe.wait_ge(S["h_ready"], 10)
            turn_round(lambda k, b: h_tok[:, b, k * P:(k + 1) * P], KC)
            copied(9)
            last = DFF // CHUNK - 1
            for j in range(last + 2):
                if j <= last:
                    by_columns("up", j)
                if j >= 1:
                    for u in range(PARTS):
                        pe.wait_ge(S["a_lo_ready"], (STEPS + j - 1) * PARTS + u + 1)
                        split_landed(NTH["down", j - 1], u)
                        row_part(u, j == 1 and u == 0, j == last + 1 and u == PARTS - 1)

        @block.scalar
        def _(act):
            own = Chain(act, act_own)

            def squares(b0, width, view, row):
                for b in range(NB):
                    act.activation(view(b)[1], view(b)[0], ACT.Square,
                                   accum_out=st[:, row, b0 + b:b0 + b + 1]).then_inc(S["sumsq"], 1)

            def root(cols, src, dst, wait, count, done):
                act.wait_ge(S[wait], count)
                rows = (cols + 15) // 16
                cols = min(cols, 16)
                act.activation(st[:, dst:dst + rows, 0:cols], st[:, src:src + rows, 0:cols], ACT.Sqrt)\
                    .then_inc(S[done], 1)

            def split(kind, j, acts=None, last=None):
                n = NTH[kind, j]
                act.wait_ge(w_in_slot[n % RING], 16 * (n // RING + 1))
                for u in range(PARTS):
                    if acts is not None:
                        if last is not None:
                            act.wait_ge(parts_used, SPLIT_BEFORE[last] + u + 1)
                        act.copy(a_hi[:, u, :], acts[:, u, :]).then_inc(S["a_hi_ready"], 1)
                    if SPLIT_BEFORE[n]:
                        act.wait_ge(parts_used, SPLIT_BEFORE[n] + u + 1 - PARTS)
                    act.copy(split_part(kind, w_hi, u, width(kind, j)),
                             part_of(kind, wring[:, n % RING, :], u, width(kind, j))).then_inc(split_hi, 1)

            def h_round(r):
                act.wait_ge(S["tr_done"], r)
                for half in range(2):
                    act.copy(hT_hi[:, half * 4:half * 4 + 4, :].rearrange("p k t -> p (k t)"),
                             psf[:, (4 + 2 * half) * 512:(6 + 2 * half) * 512]).then_inc(S["tr_hi"], 1)
                act.sem_inc(S["tr_copied_act"], 1)

            def copy_round(r, dst):
                act.wait_ge(S["tr_done"], r)
                act.copy(dst, psf[:, 4 * 512:6 * 512]).then_inc(S["tr_copied_act"], 1)

            def empty(kind, j, dst, src, func=ACT.Copy, bias=0.0):
                stands(act, kind, j)
                act.activation(dst, src, func, bias=bias).then_inc(emptied_by["act"], 1)

            def empty_ada(j):
                cols = slice((j % 2) * CHUNK, (j % 2 + 1) * CHUNK)
                which = (0, 1, 2, 0, 1, 3)[j // 2]
                if j == 6:
                    act.wait_ge(S["h_ready"], 2)
                empty("ada", j, mod[:, which, cols], ps[:, pair("ada", j), :], ACT.Copy, 1.0 if which == 1 else 0.0)

            act.wait_ge(ld_c, 32)
            act.activation(csilu[:, 1, :], csilu[:, 0, :], ACT.Silu).then_inc(S["silu_c"], 1)
            act.wait_ge(ld_x, 32)
            squares(0, D, lambda b: (x_tok[:, b, :], tiles[:, 1 + b, 0:D]), 0)
            act.wait_ge(S["angles"], 1)
            act.activation(trig[:, :, :, :], turns, ACT.Sin).then_inc(S["trig_ready"], 1)
            for j in range(4):
                empty_ada(j)
            root(NB, 1, 2, "var", 1, "std")
            split("win", 0)
            h_round(1)
            for j in range(7):
                if j < 6:
                    split("win", j + 1)
                b0 = pair("win", j)
                empty("win", j, proj[:, :, j * HW:(j + 1) * HW], ps[:, b0:b0 + 2, :])
                if j == 3:
                    act.wait_ge(emptied_by["act"], emptied_count("win", 3))
                    act.activation(proj[:, :, 3 * HW:4 * HW], proj[:, :, 3 * HW:4 * HW], ACT.Silu)\
                        .then_inc(S["ret_gate"], 1)
            empty_ada(4)
            copy_round(2, qT.rearrange("p c t -> p (c t)"))
            empty_ada(5)
            empty_ada(6)
            root(32, 4, 6, "var_s", 1, "std_s")
            empty_ada(7)
            empty_ada(8)
            copy_round(3, qT.rearrange("p c t -> p (c t)"))
            empty_ada(9)
            act.wait_ge(S["ret_y"], 2)
            for b4 in range(2):
                bank, t = 4 - 4 * b4, tiles[:, 2 * b4, :]
                act.wait_ge(S["sb_z"], b4 + 1)
                own(act.activation(t, psf[:, bank * 512:(bank + 3) * 512], ACT.Abs))
                own(act.activation(t, t, ACT.Exp, scale=-1.0))
                act.activation(t, t, ACT.Ln, bias=1.0).then_inc(S["sb_L"], 1)
            root(16, 4, 6, "var_s", 2, "std_s")
            for b4 in range(2):
                t = tiles[:, 2 * b4, :]
                act.wait_ge(S["sb_logw"], b4 + 1)
                act.activation(t, t, ACT.Exp).then_inc(S["sb_exp"], 1)
            root(16, 5, 7, "var_s", 3, "std_s")
            split("wout", 0)
            h_round(4)
            split("wout", 1)
            act.wait_ge(S["x1_ready"], 2)
            squares(0, D, lambda b: (x_tok[:, b, :], tiles[:, 2 + b, 0:D]), 0)
            root(NB, 1, 2, "var", 2, "std")
            split("wq", 0)
            h_round(5)

            def take_scores(j):
                bank = 4 + 2 * (j % 2)
                act.wait_ge(S["sub_done"], j + 1)
                act.copy(score[:, :, 2 * j:2 * j + 2, :].rearrange("p b h n -> p b (h n)"), ps[:, bank:bank + 2, :])\
                    .then_inc(S["sub_out"], 1)

            for j in range(4):
                split(*(("wq", j + 1) if j < 3 else ("dn", 0)))
                b0 = pair("wq", j)
                empty("wq", j, qryT[:, 4 * j:4 * j + 4, :].rearrange("p c t -> p (c t)"),
                      psf[:, b0 * 512:b0 * 512 + 1024])
                if j >= 1:
                    take_scores(j - 1)

            def down_gelu(k):
                b0 = 2 * ((EMPTIED[down0][0] + k) % 2)
                act.activation(acts[:, k % AR, :, :].rearrange("p f t -> p (f t)"), psf[:, b0 * 512:b0 * 512 + 1024],
                               ACT.Gelu).then_inc(emptied_by["act"], 1)

            split("dn", 1)
            stands(act, "dn", 0)
            down_gelu(0)
            take_scores(3)
            for j in range(1, LEAD):
                if j + 1 < LEAD:
                    split("dn", j + 1)
                stands(act, "dn", j)
                down_gelu(j)
            for j in (10, 11):
                empty_ada(j)
            act.wait_ge(S["score_max"], NB)
            act.activation(sel[:, :, 2, :], sel[:, :, 2, :], ACT.Exp).then_inc(S["exp_done"], 1)
            act.sem_inc(S["spread_out"], 2)
            for u in range(2):
                act.sem_inc(gates_stored[u], 16)
            act.sem_inc(gates_landed[0], 16)
            with act.Fori(0, T // (4 * TT)) as turn:
                for q in range(4):
                    group, e, u = turn * 4 + q, q % 2, q // 2
                    if e == 0:
                        act.wait_ge(gates_stored[u], turn * 16 + 16)
                    act.wait_ge(S["onehot_used"], group + 3)
                    at = (4 + 2 * e) * 512
                    act.copy(spread[u][:, :, e * TT:(e + 1) * TT],
                             psf[:, at:at + TT * NKEY].rearrange("p (t n) -> p n t", n=NKEY)).then_inc(S["spread_out"], 1)
                    if e == 1:
                        act.wait_ge(S["spread_out"], group + 3)
                        act.dma_start(gates_dram[bass.ds(turn * 2 + u, 1), :, :].rearrange("g p n -> p (g n)"),
                                      spread[u].rearrange("p n t -> p (n t)")).then_inc(gates_stored[u], 16)
            def expert_split(i, k, up, parts, last_up=None):
                par, landed = ring_turn(i, up)
                act.wait_ge(w_in_slot[par], landed)
                for u in range(PARTS):
                    if last_up is not None:
                        act.wait_ge(parts_used, last_up + (u + 1))
                        act.copy(a_hi[:, u, :], acts[:, k, u, :]).then_inc(S["a_hi_ready"], 1)
                    act.wait_ge(parts_used, parts + (u + 1 - PARTS))
                    act.copy(w_hi[:, u, :], wring[:, par, u * PART:(u + 1) * PART]).then_inc(split_hi, 1)

            def expert_acts(i, k):
                down, up = slot_parts(i)
                if has_down(i):
                    expert_split(i, k, 0, down)
                act.wait_ge(S["weighed"], i + 1)
                expert_split(i, k, 1, up, (down if has_down(i) else up) - PARTS)
                if has_down(i):
                    act.wait_ge(parts_used, up)
                    down_gelu((k + LEAD) % AR)
                if k % 2 == 0 and not (isinstance(i, int) and i + 2 >= STEPS):
                    act.wait_ge(S["weighed"], i + 1)
                    act.dma_start(gates_in[:, (k // 2 + 1) % 2, :, :, :].rearrange("p g f t -> p g (f t)"),
                                  gates_dram[:, :, bass.ds(i * (EF * 16) + 2 * EF * 16, 2 * EF * 16)]
                                  .rearrange("g p n -> p g n")).then_inc(gates_landed[(k // 2 + 1) % 2], 16)

            expert_steps(act.Fori, expert_acts)

            act.wait_ge(S["x2_ready"], 2)
            squares(0, D, lambda b: (x_tok[:, b, :], ptile[:, b, 0:D]), 0)
            root(NB, 1, 2, "var", 3, "std")
            split("win2", 0)
            h_round(6)

            def take_win2(j):
                b0, n = pair("win2", j), width("win2", j)
                empty("win2", j, z[:, :, j * CHUNK:j * CHUNK + n], ps[:, b0:b0 + 2, 0:n])

            for j in range(3):
                split("win2", j + 1)
                take_win2(j)
            act.wait_ge(S["c_tr"], 1)
            kv = psf[:, 4 * 512:6 * 512].rearrange("p (v g t) -> p v g t", v=2, g=NG)
            act.copy(kvA[0:64, :, :, :], kv[0:64, :, :, :])
            act.copy(kvA[64:P, :, :, 0:T - 1], kv[64:P, :, :, 1:T]).then_inc(S["kv_copied"], 1)
            split("win2", 4)
            take_win2(3)
            root(32, 4, 6, "zrms", 1, "zstd")
            act.wait_ge(emptied_by["act"], emptied_count("win2", 2))
            act.activation(gatec[:, :, :, :].rearrange("p b h k -> p b (h k)"), z[:, :, Z_G:Z_H], ACT.Sigmoid)\
                .then_inc(S["ret_gate"], 1)
            split("win2", 5)
            take_win2(4)
            act.wait_ge(ld_cmp, 64)
            act.wait_ge(S["blk_ready"], 1)
            stands(act, "cmp", 1)
            for v in range(2):
                for f in range(2):
                    at = 6 * 512 + (2 * v + f) * 32
                    src = psf[:, at:at + 2 * NCMP].rearrange("p (g n) -> p g n", g=NG)
                    dst = hdnT[:, f, :].rearrange("p (g n) -> p g n", g=NG)[:, :, 0:NCMP]
                    if v == 1:
                        src = src.unsqueeze(2).to_broadcast([P, NG, R, NCMP])
                        dst = hdnV[:, f, :, :, 0:NCMP]
                    ins = act.activation(dst, src, ACT.Gelu_apprx_tanh, bias=cbias[:, v, f:f + 1])
            ins.then_inc(S["hdn_out"], 1)
            take_win2(5)
            copy_round(7, qT2.rearrange("p c t -> p (c t)"))
            act.wait_ge(S["kvar"], 1)
            act.activation(kcst[:, 2:3], kcst[:, 1:2], ACT.Sqrt).then_inc(S["kstd"], 1)
            act.wait_ge(S["kcmp"], 2)
            for g in range(NG):
                for r in range(R):
                    ins = act.copy(vbd[32 * r:32 * r + 32, g, r, :], ps[32 * r:32 * r + 32, 0, g * HD:(g + 1) * HD])
            ins.then_inc(S["vcmp_out"], 1)
            act.wait_ge(S["c_tr"], 2)
            act.copy(kcmpT[:, :], ps[:, 3, 128:192]).then_inc(S["kct_copied"], 1)

            def exp_batch(i):
                act.wait_ge(S["s_max"], i + 1)
                for b in range(NB):
                    for r in range(R):
                        lo, n = (r * P, P) if b == 0 else (512 + r * T, T)
                        t = ptile[:, i % 2, lo:lo + n]
                        ins = act.activation(t, t, ACT.Exp, bias=mx[:, i % 2, b, r:r + 1],
                                             accum_out=sm[:, i % 2, b, r:r + 1])
                ins.then_inc(S["p_ready"], 1)

            exp_batch(0)
            act.wait_ge(S["c_max"], 1)
            act.activation(pcs, pcs, ACT.Exp).then_inc(S["c_exp"], 1)
            for i in range(1, 4):
                exp_batch(i)
            act.wait_ge(S["c_tr"], 3)
            act.copy(pcT.rearrange("p b g t -> p (b g t)"), ps[:, 4, :]).then_inc(S["c_out"], 1)
            act.wait_ge(S["conv_out"], 1)
            act.wait_ge(S["o_out"], 5)
            for b in range(NB):
                act.activation(tmp[:, b, :], h_tok[:, b, 0:HW], ACT.Square, accum_out=st[:, 0, b:b + 1])
                act.activation(sh1[:, b, :], z[:, b, Z_H:Z_H + HW], ACT.Square, accum_out=st[:, 0, 2 + b:3 + b])\
                    .then_inc(S["sumsq"], 1)
            root(4, 1, 2, "var", 4, "std")
            split("wo", 0)
            h_round(8)
            split("wo", 1)
            act.wait_ge(S["x1_ready"], 4)
            squares(0, D, lambda b: (x_tok[:, b, :], ptile[:, b, 0:D]), 0)
            root(NB, 1, 2, "var", 5, "std")
            split("up", 0)
            h_round(9)
            for j in range(DFF // CHUNK + 1):
                if 1 <= j < DFF // CHUNK:
                    split("up", j)
                if j >= 1:
                    act.wait_ge(S["u2_ready"], j)
                    split("down", j - 1, uT[:, (j - 1) % 2, :, :], NTH["down", j - 2] if j >= 2 else None)
                if j < DFF // CHUNK:
                    b0 = pair("up", j)
                    if j >= 2:
                        act.wait_ge(S["a_lo_ready"], (STEPS + j - 1) * PARTS)
                    empty("up", j, uT[:, j % 2, :, :].rearrange("p f t -> p (f t)"),
                          psf[:, b0 * 512:b0 * 512 + 1024], ACT.Relu)

        @block.gpsimd
        def _(pool):
            own = Chain(pool, pool_own)
            for n in BY_POOL:
                for u in range(PARTS):
                    pool.wait_ge(split_hi, SPLIT_BEFORE[n] + u + 1)
                    hi, lo = (split_part(STREAM[n][0], v, u) for v in (w_hi, w_lo))
                    pool.tensor_tensor(lo, part_of(STREAM[n][0], wring[:, n % RING, :], u), hi, ALU.subtract)\
                        .then_inc(split_lo_pool, 1)
            with pool.Fori(0, T // (4 * TT)) as turn:
                for q in range(4):
                    e = q % 2
                    pool.wait_ge(S["onehot_raw"], turn * 4 + (q + 1))
                    pool.tensor_tensor(onehot[:, 1, e, :, :], onehot[:, 1, e, :, :],
                                       cur[:, e, 2, :].unsqueeze(2).to_broadcast([P, TT, NKEY]), ALU.mult)\
                        .then_inc(S["onehot_ready"], 1)
            for u in range(2):
                pool.wait_ge(gates_stored[u], 16 + 16 * (T // (4 * TT)))
            pool.dma_start(gates_in[:, 0, :, :, :].rearrange("p g f t -> p g (f t)"),
                           gates_dram[:, :, 0:2 * EF * 16].rearrange("g p n -> p g n")).then_inc(ld_gates, 16)
            pool.wait_ge(S["tr_done"], 6)
            own(pool.memset(sh1[0:1, 0, :], 0.0))
            own(pool.memset(sh2[0:2, 0, :], 0.0))
            pool.wait_ge(emptied_by["act"], emptied_count("win2", 4))
            u = z[:, :, Z_H:Z_H + HW]
            pool.tensor_tensor(u, z[:, :, Z_C:Z_C + HW], u, ALU.mult).then_inc(S["u_ready"], 1)
            pool.wait_ge(S["u_ready"], 1)
            for k, v in ((1, sh1), (2, sh2)):
                pool.dma_start(v[k:P, :, :], u[0:P - k, :, :]).then_inc(S["u_shifted"], 16)
                pool.dma_start(v[0:k, 1, :], u[P - k:P, 0, :]).then_inc(S["u_shifted"], 16)
            pool.wait_ge(ld_late, 64)
            pool.wait_ge(S["u_shifted"], 64)
            pool.wait_ge(emptied_by["act"], emptied_count("win2", 5))

            def tap(k):
                return convw[:, k, :].unsqueeze(1).to_broadcast([P, NB, HW])

            own(pool.tensor_tensor(u, u, tap(2), ALU.mult))
            own(pool.tensor_tensor(sh1, sh1, tap(1), ALU.mult))
            own(pool.tensor_tensor(sh2, sh2, tap(0), ALU.mult))
            own(pool.tensor_tensor(sh1, sh1, sh2, ALU.add))
            own(pool.tensor_tensor(u, u, sh1, ALU.add))
            pool.tensor_tensor(u, u, z[:, :, Z_B:Z_B + HW], ALU.mult).then_inc(S["conv_out"], 1)

        @block.vector
        def _(dve):
            own = Chain(dve, dve_own)

            def mean_eps(n, width):
                dve.tensor_scalar(st[:, 1, 0:n], st[:, 0, 0:n], 1.0 / width, EPS, ALU.mult, ALU.add)\
                    .then_inc(S["var"], 1)

            def copy_round(r, dst):
                dve.wait_ge(S["tr_done"], r)
                dve.tensor_copy(dst, psf[:, 6 * 512:8 * 512]).then_inc(S["tr_copied_dve"], 1)

            def split(kind, j, acts=None, step=None):
                n = NTH[kind, j]
                for u in range(PARTS):
                    if acts is not None:
                        act_rest(acts, u, step)
                    dve.wait_ge(split_hi, SPLIT_BEFORE[n] + u + 1)
                    hi, lo = (split_part(kind, v, u, width(kind, j)) for v in (w_hi, w_lo))
                    dve.tensor_tensor(lo, part_of(kind, wring[:, n % RING, :], u, width(kind, j)), hi, ALU.subtract)\
                        .then_inc(split_lo, 1)

            h_rounds = []

            def h_round(r):
                for half in range(2):
                    h_rounds.append(r)
                    dve.wait_ge(S["tr_hi"], len(h_rounds))
                    cols = slice(half * 4, half * 4 + 4)
                    ins = dve.tensor_tensor(hT_lo[:, cols, :].rearrange("p k t -> p (k t)"),
                                            psf[:, (4 + 2 * half) * 512:(6 + 2 * half) * 512],
                                            hT_hi[:, cols, :].rearrange("p k t -> p (k t)"), ALU.subtract)
                ins.then_inc(S["tr_copied_dve"], 1)

            def over_heads(row, n=NH):
                v = st[:, row, 0:NB * n].rearrange("p (b h) -> p b h", b=NB)
                return v.unsqueeze(3).to_broadcast([P, NB, n, HD])

            def head_gain(k, n=NH):
                return small[:, k, :].unsqueeze(1).unsqueeze(1).to_broadcast([P, NB, n, HD])

            def head_sums(row, v, square, n=NH):
                own(dve.tensor_tensor(square, v, v, ALU.mult))
                own(dve.tensor_reduce(st[:, row, 0:NB * n].rearrange("p (b h) -> p b h", b=NB), square, AX.X, ALU.add))

            def norm_x(turn, sums, gain, shift=None):
                dve.wait_ge(S["sumsq"], sums)
                mean_eps(NB, D)
                dve.wait_ge(S["std"], turn)
                own(dve.reciprocal(st[:, 3, 0:NB], st[:, 2, 0:NB]))
                for b in range(NB):
                    ins = dve.scalar_tensor_tensor(h_tok[:, b, :], x_tok[:, b, :], st[:, 3, b:b + 1], gain,
                                                   ALU.mult, ALU.mult)
                    if shift is not None:
                        own(ins)
                        ins = dve.tensor_tensor(h_tok[:, b, :], h_tok[:, b, :], shift, ALU.add)
                    ins.then_inc(S["h_ready"], 1)

            dve.wait_ge(ld_x, 32)
            dve.wait_ge(ld_const, 16)
            own(dve.tensor_copy(posf[:, :], posi[:, :]))
            for b in range(NB):
                own(dve.tensor_scalar(ang[:, b, :], con("freq"), posf[:, b:b + 1], None, ALU.mult))
            for f, quarter in enumerate((0.0, 0.25)):
                t = turns[:, f, :, :]
                own(dve.tensor_scalar(t, ang, 1.0 / TWO_PI, quarter, ALU.mult, ALU.add))
                own(dve.tensor_scalar(t, t, MAGIC, None, ALU.add))
                own(dve.tensor_scalar(t, t, MAGIC, None, ALU.subtract))
                w = ang2[:, f, :, :]
                own(dve.scalar_tensor_tensor(w, t, -C1, ang, ALU.mult, ALU.add))
                own(dve.scalar_tensor_tensor(w, t, -C2, w, ALU.mult, ALU.add))
                own(dve.scalar_tensor_tensor(w, t, -C3, w, ALU.mult, ALU.add))
                own(dve.tensor_scalar(w, w, quarter * TWO_PI, np.pi, ALU.add, ALU.min))
                ins = dve.tensor_scalar(t, w, -np.pi, None, ALU.max)
                if f == 0:
                    own(ins)
            ins.then_inc(S["angles"], 1)

            dve.wait_ge(ld_gain, 32)
            dve.wait_ge(emptied_by["act"], emptied_count("ada", 3))
            own(dve.tensor_tensor(SCALE, SCALE, gain1[:, 0, :], ALU.mult))
            norm_x(1, 2, SCALE, SHIFT)
            split("win", 0)
            h_round(1)
            split("win", 1)
            split("win", 2)

            dve.wait_ge(S["trig_ready"], 1)
            dve.wait_ge(emptied_by["act"], emptied_count("win", 1))
            for b in range(NB):
                src = proj[:, b, 0:2 * HW].rearrange("p (h f d) -> p h f d", f=2, d=HD // 2)
                dst = h_tok[:, b, :].rearrange("p (h f d) -> p h f d", f=2, d=HD // 2)
                sin, cos = (trig[:, f, b, :].unsqueeze(1).to_broadcast([P, 2 * NH, HD // 2]) for f in range(2))
                t = [tiles[:, 2, k * 512:(k + 1) * 512].rearrange("p (h d) -> p h d", d=HD // 2) for k in range(2)]
                own(dve.tensor_tensor(dst[:, :, 0, :], src[:, :, 0, :], cos, ALU.mult))
                own(dve.tensor_tensor(t[0], src[:, :, 1, :], sin, ALU.mult))
                own(dve.tensor_tensor(dst[:, :, 0, :], dst[:, :, 0, :], t[0], ALU.subtract))
                own(dve.tensor_tensor(dst[:, :, 1, :], src[:, :, 1, :], cos, ALU.mult))
                own(dve.tensor_tensor(t[1], src[:, :, 0, :], sin, ALU.mult))
                dve.tensor_tensor(dst[:, :, 1, :], dst[:, :, 1, :], t[1], ALU.add).then_inc(S["rot_ready"], 1)
                split("win", 3 + b)
            split("win", 5)
            split("win", 6)

            dve.wait_ge(emptied_by["act"], emptied_count("win", 5))
            sq_, sk_ = (heads(proj[:, :, (4 + k) * HW:(5 + k) * HW]) for k in range(2))
            flat = tiles[:, 2, 0:1024].rearrange("p (b h d) -> p b h d", b=NB, d=HD)
            head_sums(4, sq_, flat)
            head_sums(5, sk_, flat)
            dve.tensor_scalar(st[:, 4:6, :], st[:, 4:6, :], 1.0 / HD, EPS, ALU.mult, ALU.add).then_inc(S["var_s"], 1)
            copy_round(2, kT.rearrange("p c t -> p (c t)"))
            dve.wait_ge(ld_early, 112)
            own(dve.tensor_scalar(small[:, 0, :], small[:, 0, :], HD ** -0.5, None, ALU.mult))
            own(dve.tensor_scalar(small[:, 3, :], small[:, 3, :], HD ** -0.5, None, ALU.mult))

            for b4 in range(2):
                dve.wait_ge(S["ret_scores"], b4 + 1)
                for n in range(3):
                    ins = dve.tensor_tensor(tiles[:, b4, n * 512:(n + 1) * 512].rearrange("p (h i) -> p h i", h=4),
                                            ps[:, 4 + n, :].rearrange("p (h i) -> p h i", h=4),
                                            decay[:, n % 2, b4::2, :], ALU.mult)
                ins.then_inc(S["ret_decayed"], 1)
                if b4 == 0:
                    dve.wait_ge(S["std_s"], 1)
                    own(dve.reciprocal(st[:, 8:10, :], st[:, 6:8, :]))
                    own(dve.tensor_tensor(sq_, sq_, over_heads(8), ALU.mult))
                    dve.tensor_tensor(sq_, sq_, head_gain(0), ALU.mult).then_inc(S["sbq_ready"], 1)
                    own(dve.tensor_tensor(sk_, sk_, over_heads(9), ALU.mult))
                    dve.tensor_tensor(sk_, sk_, head_gain(1), ALU.mult).then_inc(S["sbq_ready"], 1)
            for b4 in range(2):
                dve.wait_ge(S["ret_y"], b4 + 1)
                for b in range(NB):
                    ins = dve.tensor_copy(every_other(proj[:, b, 0:HW], b4),
                                          ps[:, 7, b * 256:(b + 1) * 256].rearrange("p (h d) -> p h d", d=HD))
                ins.then_inc(S["ret_y_out"], 1)
            copy_round(3, kT.rearrange("p c t -> p (c t)"))

            dve.wait_ge(S["ret_y_out"], 2)
            yr = heads(proj[:, :, 0:HW])
            ysum = st[:, 4, :].rearrange("p (b h) -> p b h", b=NB)
            own(dve.tensor_reduce(ysum, yr, AX.X, ALU.add))
            own(dve.tensor_scalar(st[:, 4, :], st[:, 4, :], 1.0 / HD, None, ALU.mult))
            own(dve.tensor_tensor(yr, yr, over_heads(4), ALU.subtract))

            def sb_logs(b4):
                bank, t = 4 - 4 * b4, [tiles[:, 2 * b4 + k, :] for k in range(2)]
                zed = psf[:, bank * 512:(bank + 3) * 512]
                dve.wait_ge(S["sb_L"], b4 + 1)
                own(dve.scalar_tensor_tensor(t[0], zed, 0.0, t[0], ALU.min, ALU.subtract))
                own(dve.tensor_tensor(t[1], t[0], zed, ALU.subtract))
                mask = con("before").unsqueeze(1).to_broadcast([P, 4, P])
                for n in (0, 2):
                    v = t[1][:, n * 512:(n + 1) * 512].rearrange("p (h i) -> p h i", h=4)
                    ins = dve.tensor_tensor(v, v, mask, ALU.mult)
                ins.then_inc(S["sb_ls"], 1)

            def sb_weights(b4):
                bank, t = 4 - 4 * b4, tiles[:, 2 * b4, :]
                dve.wait_ge(S["sb_cum"], b4 + 1)
                dve.tensor_tensor(t, t, psf[:, bank * 512:(bank + 3) * 512], ALU.add).then_inc(S["sb_logw"], 1)

            def sb_mask(b4):
                t = tiles[:, 2 * b4, :]
                mask = con("before").unsqueeze(1).to_broadcast([P, 4, P])
                dve.wait_ge(S["sb_exp"], b4 + 1)
                for n in (0, 2):
                    v = t[:, n * 512:(n + 1) * 512].rearrange("p (h i) -> p h i", h=4)
                    ins = dve.tensor_tensor(v, v, mask, ALU.mult)
                ins.then_inc(S["sb_w"], 1)

            sb_logs(0)
            sb_logs(1)
            sb_weights(0)
            sqr = tiles[:, 1, 0:1024].rearrange("p (b h d) -> p b h d", b=NB, d=HD)
            head_sums(4, yr, sqr)
            dve.tensor_scalar(st[:, 4, :], st[:, 4, :], 1.0 / HD, EPS, ALU.mult, ALU.add).then_inc(S["var_s"], 1)
            sb_weights(1)
            dve.wait_ge(S["std_s"], 2)
            own(dve.reciprocal(st[:, 8, :], st[:, 6, :]))
            own(dve.tensor_tensor(yr, yr, over_heads(8), ALU.mult))
            dve.wait_ge(S["ret_gate"], 1)
            yw = proj[:, :, 0:HW]
            own(dve.tensor_tensor(yw, yw, rgain.unsqueeze(1).to_broadcast([P, NB, HW]), ALU.mult))
            dve.tensor_tensor(yw, yw, proj[:, :, 3 * HW:4 * HW], ALU.mult).then_inc(S["y_ready"], 1)
            sb_mask(0)
            sb_mask(1)
            ys = heads(proj[:, :, HW:2 * HW])
            for b4 in range(2):
                dve.wait_ge(S["sb_y"], b4 + 1)
                for b in range(NB):
                    own(dve.tensor_copy(every_other(proj[:, b, HW:2 * HW], b4),
                                        ps[:, 7 - 4 * b4, b * 256:(b + 1) * 256].rearrange("p (h d) -> p h d", d=HD)))
            head_sums(5, ys, sqr)
            dve.tensor_scalar(st[:, 5, :], st[:, 5, :], 1.0 / HD, EPS, ALU.mult, ALU.add).then_inc(S["var_s"], 1)
            dve.wait_ge(S["std_s"], 3)
            own(dve.reciprocal(st[:, 9, :], st[:, 7, :]))
            own(dve.tensor_tensor(ys, ys, over_heads(9), ALU.mult))
            dve.tensor_tensor(ys, ys, head_gain(2), ALU.mult).then_inc(S["y_ready"], 1)
            split("wout", 0)
            h_round(4)
            split("wout", 1)

            for j in range(2):
                b0, cols = pair("wout", j), slice(j * CHUNK, (j + 1) * CHUNK)
                stands(dve, "wout", j)
                gated = tiles[:, 0, 0:1024].rearrange("p (b n) -> p b n", b=NB)
                own(dve.tensor_tensor(gated, ps[:, b0:b0 + 2, :],
                                      GATE1[:, cols].unsqueeze(1).to_broadcast([P, NB, CHUNK]), ALU.mult))
                own(dve.tensor_tensor(x_tok[:, :, cols], x_tok[:, :, cols], gated, ALU.add))
                dve.sem_inc(emptied_by["dve"], 1)
                dve.sem_inc(S["x1_ready"], 1)
            own(dve.tensor_tensor(SCALE, SCALE, gain1[:, 1, :], ALU.mult))
            norm_x(2, 4, SCALE, SHIFT)
            split("wq", 0)
            h_round(5)
            split("wq", 1)
            class TwoChains:

                def __init__(self):
                    self.sems, self.n = [S["choose0"], S["choose1"]], 0

                def __call__(self, op):
                    for b in range(NB):
                        if self.n:
                            dve.wait_ge(self.sems[b], self.n)
                        op(b).then_inc(self.sems[b], 1)
                    self.n += 1

                def finish(self):
                    for b in range(NB):
                        dve.wait_ge(self.sems[b], self.n)
                        dve.sem_clear(self.sems[b])
                    self.n = 0

            both = TwoChains()

            def top16(vals, work, values, index):
                both(lambda b: dve.max(values(b)[:, 0:8], vals(b)))
                both(lambda b: dve.max_index(index(b)[:, 0:8], values(b)[:, 0:8], vals(b)))
                both(lambda b: dve.match_replace(work(b), values(b)[:, 0:8], vals(b), -3.0e38))
                both(lambda b: dve.max(values(b)[:, 8:16], work(b)))
                both(lambda b: dve.max_index(index(b)[:, 8:16], values(b)[:, 8:16], work(b)))

            with dve.Fori(0, PH // 2) as turn:
                dve.wait_ge(S["sub_out"], turn + 1)
                for hh in range(2):
                    head = turn * 2 + hh
                    both(lambda b: dve.tensor_copy(sc2[:, b, :], score[:, b, bass.ds(head, 1), :]
                                                   .rearrange("p c n -> p (c n)")))
                    for half in range(2):
                        top16(lambda b: sc2[:, b, half * NKEY:(half + 1) * NKEY], lambda b: cand2[:, b, 0:NKEY],
                              lambda b: top[:, b, half, :], lambda b: topi[:, b, half, :])
                    both(lambda b: dve.tensor_tensor(cand[:, b, :].rearrange("p (i j) -> p i j", i=PK),
                                                     top[:, b, 0, :].unsqueeze(2).to_broadcast([P, PK, PK]),
                                                     top[:, b, 1, :].unsqueeze(1).to_broadcast([P, PK, PK]), ALU.add))
                    top16(lambda b: cand[:, b, :], lambda b: cand2[:, b, :], lambda b: best1[:, b, :],
                          lambda b: besti1[:, b, :])
                    both(lambda b: dve.tensor_copy(topf[:, b, bass.ds(head, 1), :, :].rearrange("p h k n -> p (h k) n"),
                                                   topi[:, b, :, :]))
                    both(lambda b: dve.tensor_copy(best[:, b, bass.ds(head, 1), :].rearrange("p h n -> p (h n)"),
                                                   best1[:, b, :]))
                    both(lambda b: dve.tensor_copy(besti[:, b, 0, bass.ds(head, 1), :].rearrange("p h n -> p (h n)"),
                                                   besti1[:, b, :]))
                both.finish()
            gate = [sel[:, b, 2, :].rearrange("p (h k) -> p h k", h=PH) for b in range(NB)]
            for b in range(NB):
                dve.tensor_tensor(gate[b], best[:, b, :, :], best[:, b, :, 0:1].to_broadcast([P, PH, PK]), ALU.subtract)\
                    .then_inc(S["score_max"], 1)
            both(lambda b: dve.tensor_scalar(besti[:, b, 1, :, :], besti[:, b, 0, :, :], 15, None, ALU.bitwise_and))
            both(lambda b: dve.tensor_scalar(besti[:, b, 0, :, :], besti[:, b, 0, :, :], 4, None, ALU.logical_shift_right))
            both(lambda b: dve.tensor_copy(bestf[:, b, :, :, :], besti[:, b, :, :, :]))
            for half in range(2):
                both(lambda b: dve.tensor_tensor(pick[:, b], bestf[:, b, half, :, :].unsqueeze(3)
                                                 .to_broadcast([P, PH, PK, PK]),
                                                 con("iota")[:, 0:PK].unsqueeze(1).unsqueeze(1)
                                                 .to_broadcast([P, PH, PK, PK]), ALU.is_equal))
                both(lambda b: dve.tensor_tensor(pick[:, b], pick[:, b], topf[:, b, :, half, :].unsqueeze(2)
                                                 .to_broadcast([P, PH, PK, PK]), ALU.mult))
                both(lambda b: dve.tensor_reduce(sel[:, b, half, :].rearrange("p (h k) -> p h k", h=PH), pick[:, b],
                                                 AX.X, ALU.add))
            dve.wait_ge(S["exp_done"], 1)
            both(lambda b: dve.tensor_reduce(gsum[:, b, :], gate[b], AX.X, ALU.add))
            both(lambda b: dve.reciprocal(gsum[:, b, :], gsum[:, b, :]))
            both.finish()
            for b in range(NB):
                dve.tensor_tensor(gate[b], gate[b], gsum[:, b, :].unsqueeze(2).to_broadcast([P, PH, PK]), ALU.mult)\
                    .then_inc(S["sel_ready"], 1)
            dve.wait_ge(S["sel_turned"], 1)
            own(dve.tensor_copy(selT.rearrange("p k (b t) -> p k b t", b=NB),
                                ps[:, 4:6, 0:3 * P].rearrange("p b (k t) -> p k b t", k=3)))
            dve.sem_inc(S["onehot_used"], 2)
            with dve.Fori(0, T // (4 * TT)) as turn:
                for q in range(4):
                    group, e = turn * 4 + q, q % 2
                    dve.wait_ge(S["onehot_used"], group + 1)
                    dve.tensor_copy(cur[:, e, :, :], selT[:, :, bass.ds(turn * (4 * TT) + q * TT, TT)])\
                        .then_inc(S["cur_ready"], 1)
                    dve.wait_ge(S["cur_ready"], group + 1)
                    dve.tensor_tensor(onehot[:, :, e, :, :],
                                      con("iota").unsqueeze(1).unsqueeze(1).to_broadcast([P, 2, TT, NKEY]),
                                      cur[:, e, 0:2, :].unsqueeze(3).to_broadcast([P, 2, TT, NKEY]), ALU.is_equal)\
                        .then_inc(S["onehot_raw"], 1)
            dve.sem_inc(S["late_free"], 1)

            def weigh(i, k):
                act_k = acts[:, k, :, :].rearrange("p f (g t) -> p f g t", t=16)
                gates = gates_in[:, k // 2, :, (k % 2) * EF:(k % 2 + 1) * EF, :].rearrange("p g f t -> p f g t")
                dve.wait_ge(emptied_by["act"], i + (out3 - LEAD))
                if k == 0:
                    dve.wait_ge(ld_gates, 16)
                dve.wait_ge(gates_landed[k // 2], 16 * (i // AR + 1) if isinstance(i, int) else i * (16 // AR) + (16 - 16 // AR * k))
                dve.tensor_tensor(act_k, act_k, gates, ALU.mult).then_inc(S["weighed"], 1)

            def act_rest(source, u, step):
                dve.wait_ge(S["a_hi_ready"], step * PARTS + (u + 1))
                dve.tensor_tensor(a_lo[:, u, :], source[:, u, :], a_hi[:, u, :], ALU.subtract)\
                    .then_inc(S["a_lo_ready"], 1)

            def expert_rests(i, up, parts, source=None, step=None):
                par, _ = ring_turn(i, up)
                for u in range(PARTS):
                    if source is not None:
                        act_rest(source, u, step)
                    dve.wait_ge(split_hi, parts + (u + 1))
                    dve.tensor_tensor(w_lo[:, u, :], wring[:, par, u * PART:(u + 1) * PART], w_hi[:, u, :],
                                      ALU.subtract).then_inc(split_lo, 1)

            def expert_acts(i, k):
                down, up = slot_parts(i)
                if has_down(i):
                    expert_rests(i, 0, down)
                weigh(i, k)
                expert_rests(i, 1, up, acts[:, k, :, :], i)
            expert_steps(dve.Fori, expert_acts)
            stands(dve, "ex", STEPS - 1)
            for b in range(NB):
                own(dve.tensor_tensor(h_tok[:, b, :], psf[:, 1024 * (2 + b):1024 * (3 + b)], GATE2, ALU.mult))
                dve.tensor_tensor(x_tok[:, b, :], x_tok[:, b, :], h_tok[:, b, :], ALU.add).then_inc(S["x2_ready"], 1)

            own(dve.memset(hdnT, 0.0))
            own(dve.memset(hdnV, 0.0))
            own(dve.memset(vbd, 0.0))
            own(dve.memset(pcmp, 0.0))
            dve.wait_ge(ld_late, 64)
            norm_x(3, 6, gmix)
            split("win2", 0)
            h_round(6)
            split("win2", 1)
            split("win2", 2)
            zq = heads(z[:, :, Z_Q:Z_Q + HW])
            zk = [heads(z[:, :, c:c + NG * HD]) for c in (Z_KS, Z_KW)]
            dve.wait_ge(emptied_by["act"], emptied_count("win2", 0))
            head_sums(4, zq, sqq)

            def key_sums(r):
                tk = tmp_k
                own(dve.tensor_tensor(tk, zk[r], zk[r], ALU.mult))
                return dve.tensor_reduce(st[:, 5, 4 * r:4 * r + 4].rearrange("p (b g) -> p b g", b=NB), tk, AX.X, ALU.add)

            dve.wait_ge(emptied_by["act"], emptied_count("win2", 1))
            for v, c in enumerate((Z_KC, Z_VC)):
                for b in range(NB):
                    src = z[:, b, c:c + NG * HD].rearrange("p (g d) -> p g d", g=NG)
                    ins = dve.tensor_copy(kvdup[:, b, v, :, :, :], src.unsqueeze(2).to_broadcast([P, NG, 2, HD]))
            ins.then_inc(S["kv_ready"], 1)
            own(key_sums(0))
            split("win2", 3)
            dve.wait_ge(S["kv_copied"], 1)
            dve.wait_ge(ld_cmp, 64)
            for v in range(2):
                for hi in range(2):
                    win = kvA[:, v, :, :].rearrange("p g (n m two) -> p two m g n", two=2, m=8)
                    code = peT[:, v, 8 * hi:8 * hi + 8].unsqueeze(2).unsqueeze(2).to_broadcast([P, 8, NG, NCMP])
                    dst = blkT[:, v, 8 * hi:8 * hi + 8, :].rearrange("p m (g n) -> p m g n", g=NG)
                    ins = dve.tensor_tensor(dst, win[:, 0, :, :, hi:hi + NCMP], code, ALU.add)
            ins.then_inc(S["blk_ready"], 1)
            split("win2", 4)
            dve.wait_ge(emptied_by["act"], emptied_count("win2", 2))
            own(key_sums(1))
            dve.tensor_scalar(st[:, 4:6, :], st[:, 4:6, :], 1.0 / HD, EPS, ALU.mult, ALU.add).then_inc(S["zrms"], 1)
            split("win2", 5)
            dve.wait_ge(S["zstd"], 1)
            own(dve.reciprocal(st[:, 8:10, :], st[:, 6:8, :]))
            own(dve.tensor_tensor(zq, zq, over_heads(8), ALU.mult))
            dve.tensor_tensor(zq, zq, head_gain(3), ALU.mult)
            for r in range(2):
                spread_r = st[:, 9, 4 * r:4 * r + 4].rearrange("p (b g) -> p b g", b=NB)
                own(dve.tensor_tensor(zk[r], zk[r], spread_r.unsqueeze(3).to_broadcast([P, NB, NG, HD]), ALU.mult))
                for b in range(NB):
                    ins = dve.tensor_tensor(kdup[:, b, r, :, :, :],
                                            zk[r][:, b, :, :].unsqueeze(2).to_broadcast([P, NG, 2, HD]),
                                            small[:, 5 + r, :].unsqueeze(1).unsqueeze(1).to_broadcast([P, NG, 2, HD]),
                                            ALU.mult)
            ins.then_inc(S["kv_ready"], 1)
            copy_round(7, kT2.rearrange("p r g t -> p (r g t)"))

            def bias_batch(i):
                pt, base = ptile[:, i % 2, :], bank_set(i) * 512
                dve.wait_ge(S["s_done"], i + 1)
                if i >= 2:
                    dve.wait_ge(S["pt_done"], i - 1)
                lo, hi = CONST["dist"]
                dist = const[:, lo:hi].rearrange("p (b s) -> p b s", b=NB)
                for b in range(NB):
                    for r in range(R):
                        at, n = (r * P, P) if b == 0 else (512 + r * T, T)
                        slope = 2.0 ** -(2 * r + i % 2 + 1)
                        ins = dve.scalar_tensor_tensor(pt[:, at:at + n], dist[:, b, 0:n], slope,
                                                       psf[:, base + at:base + at + n], ALU.mult, ALU.add)
                own(ins)
                dve.tensor_reduce(mx[:, i % 2, 0, :], pt[:, 0:512].rearrange("p (r s) -> p r s", r=R), AX.X, ALU.max,
                                  negate=True)
                dve.tensor_reduce(mx[:, i % 2, 1, :], pt[:, 512:1536].rearrange("p (r s) -> p r s", r=R), AX.X,
                                  ALU.max, negate=True).then_inc(S["s_max"], 1)

            def take_turned(i):
                dve.wait_ge(S["pt_done"], i + 1)
                if i >= 1:
                    dve.wait_ge(S["o_done"], i)
                base = bank_set(i) * 512
                dve.tensor_copy(pT.rearrange("p k r t -> p (k r t)"), psf[:, base:base + 3 * 512]).then_inc(S["pt_out"], 1)

            def add_branch(coef, src, dst, fresh):
                c = coef.unsqueeze(3).to_broadcast([P, NB, coef.shape[2], HD])
                if fresh:
                    return dve.tensor_tensor(dst, src, c, ALU.mult)
                t = tmp[:, :, 0:coef.shape[2] * HD].rearrange("p b (h d) -> p b h d", d=HD)
                own(dve.tensor_tensor(t, src, c, ALU.mult))
                return dve.tensor_tensor(dst, dst, t, ALU.add)

            oh = heads(h_tok[:, :, 0:HW])

            def take_out(i):
                br, par = i // 2, i % 2
                s = sm[:, i % 2, :, :]
                own(dve.tensor_scalar(s, s, 1e-30, None, ALU.max))
                own(dve.reciprocal(s, s))
                own(dve.tensor_tensor(s, s, gatec[:, :, par::2, br + 1], ALU.mult))
                dve.wait_ge(S["o_done"], i + 1)
                own(add_branch(s, ps[:, bank_set(i) + 3, :].rearrange("p (b r d) -> p b r d", b=NB, r=R),
                               oh[:, :, par::2, :], br == 0))
                dve.sem_inc(S["o_out"], 1)

            def compressed_norm():
                dve.wait_ge(S["kcmp"], 1)
                own(dve.tensor_copy(kcn[:, 0, :], ps[0:64, 3, 0:HD]))
                own(dve.tensor_tensor(kcq[:, :], kcn[:, 0, :], kcn[:, 0, :], ALU.mult))
                own(dve.tensor_reduce(kcst[:, 0:1], kcq[:, :], AX.X, ALU.add))
                dve.tensor_scalar(kcst[:, 1:2], kcst[:, 0:1], 1.0 / HD, EPS, ALU.mult, ALU.add).then_inc(S["kvar"], 1)
                dve.wait_ge(S["kstd"], 1)
                own(dve.reciprocal(kcst[:, 3:4], kcst[:, 2:3]))
                own(dve.scalar_tensor_tensor(kcn[:, 0, :], kcn[:, 0, :], kcst[:, 3:4], small[0:64, 4, :],
                                             ALU.mult, ALU.mult))
                dve.tensor_copy(kcn[:, 1, :], kcn[:, 0, :]).then_inc(S["kcn_ready"], 1)

            def by_head(v):
                return v.rearrange("p (b h) n -> p b h n", b=NB)

            def compressed_scores():
                dve.wait_ge(S["cs_done"], 1)
                lo, hi = CONST["cdist"]
                dist = const[:, lo:hi].rearrange("p (b n) -> p b n", b=NB)
                for h in range(NH):
                    raw = ps[:, 3 + 4 * (h % 2), 0:NB * R * CSTEP].rearrange("p (b h n) -> p b h n", b=NB, n=CSTEP)
                    ins = dve.scalar_tensor_tensor(by_head(pcs)[:, :, h, :], dist, 2.0 ** -(h + 1),
                                                   raw[:, :, h // 2, :], ALU.mult, ALU.add)
                own(ins)
                own(dve.tensor_reduce(cst[:, 0, :], pcs, AX.X, ALU.max))
                dve.tensor_tensor(pcs, pcs, cst[:, 0, :].unsqueeze(2).to_broadcast([P, NB * NH, CSTEP]),
                                  ALU.subtract).then_inc(S["c_max"], 1)

            def compressed_weights():
                lo, hi = CONST["cmask"]
                mask = const[:, lo:hi].rearrange("p (b n) -> p b n", b=NB)
                dve.wait_ge(S["c_exp"], 1)
                dst = pcmp[:, :, :, 0:CSTEP]
                dve.tensor_tensor(dst, by_head(pcs), mask.unsqueeze(2).to_broadcast([P, NB, NH, CSTEP]), ALU.mult)\
                    .then_inc(S["c_ready"], 1)
                dve.wait_ge(S["c_ready"], 1)
                total, coef = (cst[:, k, :].rearrange("p (b h) -> p b h", b=NB) for k in (1, 2))
                own(dve.tensor_reduce(total, dst, AX.X, ALU.add))
                own(dve.tensor_scalar(total, total, 1e-30, None, ALU.max))
                own(dve.reciprocal(total, total))
                own(dve.tensor_tensor(coef, total, gatec[:, :, :, 0], ALU.mult))
                return coef

            compressed_norm()
            bias_batch(0)
            compressed_scores()
            bias_batch(1)
            take_turned(0)
            dve.wait_ge(S["ret_gate"], 2)
            take_out(0)
            bias_batch(2)
            take_turned(1)
            coef = compressed_weights()
            take_out(1)
            bias_batch(3)
            take_turned(2)
            take_out(2)
            take_turned(3)
            take_out(3)
            dve.wait_ge(S["co_done"], 1)
            own(add_branch(coef, psf[:, 5 * 512:7 * 512].rearrange("p (b h d) -> p b h d", b=NB, d=HD), oh, False))
            dve.sem_inc(S["o_out"], 1)

            dve.wait_ge(S["sumsq"], 8)
            mean_eps(4, HW)
            dve.wait_ge(S["std"], 4)
            own(dve.reciprocal(st[:, 3, 0:4], st[:, 2, 0:4]))
            for b in range(NB):
                dve.scalar_tensor_tensor(h_tok[:, b, 0:HW], h_tok[:, b, 0:HW], st[:, 3, b:b + 1], gout[:, 0:HW],
                                         ALU.mult, ALU.mult)
                dve.scalar_tensor_tensor(h_tok[:, b, HW:D], z[:, b, Z_H:Z_H + HW], st[:, 3, 2 + b:3 + b],
                                         gout[:, HW:D], ALU.mult, ALU.mult).then_inc(S["h_ready"], 1)
            split("wo", 0)
            h_round(8)
            split("wo", 1)
            for j in range(2):
                b0, cols = pair("wo", j), slice(j * CHUNK, (j + 1) * CHUNK)
                stands(dve, "wo", j)
                own(dve.tensor_tensor(x_tok[:, :, cols], x_tok[:, :, cols], ps[:, b0:b0 + 2, :], ALU.add))
                dve.sem_inc(emptied_by["dve"], 1)
                dve.sem_inc(S["x1_ready"], 1)
            norm_x(5, 10, gffn)
            split("up", 0)
            h_round(9)
            for j in range(DFF // CHUNK + 1):
                if 1 <= j < DFF // CHUNK:
                    split("up", j)
                if j >= 1:
                    split("down", j - 1, uT[:, (j - 1) % 2, :, :], STEPS + j - 1)
                if j < DFF // CHUNK:
                    t = uT[:, j % 2, :, :].rearrange("p f t -> p (f t)")
                    dve.wait_ge(emptied_by["act"], emptied_count("up", j))
                    dve.tensor_tensor(t, t, t, ALU.mult).then_inc(S["u2_ready"], 1)
            stands(dve, "down", DFF // CHUNK - 1)
            for b in range(NB):
                dve.tensor_tensor(x_tok[:, b, :], x_tok[:, b, :], psf[:, (4 + 2 * b) * 512:(6 + 2 * b) * 512], ALU.add)\
                    .then_inc(S["x_out"], 1)


def kernel(**inputs):
    from concourse import bacc
    from concourse.bass_utils import run_bass_kernel_spmd

    def of(name):
        return np.asarray(inputs[name])

    def put(a):
        return np.ascontiguousarray(a)

    arrays = {
        "x": of("x")[0],
        "c": of("c").reshape(KC, P).T,
        "positions": of("positions")[0],
        "ada_w": of("ada_w")[0],
        "ada_b": of("ada_b").reshape(12, CHUNK),
        "gain1": of("norm1_gain")[0],
        "gain2": of("norm2_gain")[0],
        "w_in": of("w_in")[0],
        "ret_gain": of("ret_norm_gain")[0],
        "sb_q": of("sb_q_gain")[0],
        "sb_k": of("sb_k_gain")[0],
        "sb_out": of("sb_out_gain")[0],
        "w_out": of("w_out")[0],
        "w_query": of("peer_w_query")[0],
        "keys": of("peer_sub_keys")[0].transpose(3, 0, 1, 2).reshape(P, -1),
        "peer_down": of("peer_down")[0].reshape(STEPS, EF, P, KC, P).transpose(0, 4, 1, 3, 2).reshape(STEPS * P, SLOT),
        "peer_up": of("peer_up")[0],
        "g_mix": of("g_mix_norm_2")[0],
        "w_in2": of("w_in_2")[0],
        "g_q": of("g_q_2")[0],
        "g_k": of("g_k_2").reshape(-1),
        "pe": of("pe_cmp_2")[0].reshape(2, NPAIR, 2, HD).transpose(2, 3, 0, 1).reshape(P, 2, NPAIR),
        "w_cmp1": of("w_cmp1_2")[0],
        "b_cmp1": of("b_cmp1_2")[0].reshape(2, 2, P).transpose(2, 0, 1),
        "w_cmp2": of("w_cmp2_2")[0],
        "b_cmp2": of("b_cmp2_2").reshape(1, 2, HD),
        "conv_w": of("conv_w_2").reshape(-1),
        "g_out": of("g_out_2")[0],
        "w_o": of("w_o_2")[0],
        "g_ffn": of("g_ffn_norm_2")[0],
        "w_up": of("w_up_2")[0],
        "w_down": of("w_down_2")[0],
        "const": constants(),
        "decay": decay_table(),
    }
    arrays = {name: put(a) for name, a in arrays.items()}
    nc = bacc.Bacc("TRN2", target_bir_lowering=False, num_devices=1)
    aps = {name: nc.dram_tensor("in_" + name, a.shape, mybir.dt.from_np(a.dtype), kind="ExternalInput").ap()
           for name, a in arrays.items()}
    out = nc.dram_tensor("out", (T, D), F32, kind="ExternalOutput").ap()
    two_blocks(nc, aps, out)
    result = run_bass_kernel_spmd(nc, [{"in_" + name: a for name, a in arrays.items()}], core_ids=[0])
    return result.results[0]["out"].reshape(1, T, D)
```

```python
from contextlib import ExitStack

import numpy as np

import concourse.bass as bass
from concourse import mybir

ALU = mybir.AluOpType
ACT = mybir.ActivationFunctionType
AX = mybir.AxisListType
F32 = mybir.dt.float32
F32R = mybir.dt.float32r
U32 = mybir.dt.uint32
I32 = mybir.dt.int32

P = 128
NB = 2
T = NB * P
D = 1024
KC = D // P
HD = 64
NH = 8
HW = NH * HD
CHUNK = 512
SLOT = KC * CHUNK
PARTS = 4
PART = SLOT // PARTS
RING = 2
EPS = 1e-6

PH = 8
PK = 16
NKEY = 128
NE = NKEY * NKEY
EF = CHUNK // NKEY
STEPS = NE // CHUNK
LEAD = 8
OT = 4
OB = 4
TT = 8

NCMP = 15
CMPW = 32
CSTEP = 16
NPAIR = CMPW // 2
CF = 256
NG = 2
R = NH // NG
ZW = 2840
DFF = 4096

Z_Q, Z_KC, Z_VC, Z_KS, Z_VS, Z_KW, Z_VW, Z_G, Z_H, Z_C, Z_B = (
    0, 512, 640, 768, 896, 1024, 1152, 1280, 1304, 1816, 2328)

PAIRS = [(0, 0), (0, 1), (1, 1)]

TWO_PI = 2.0 * np.pi
MAGIC = 1.5 * 2.0 ** 23
C1 = 6.28125
C2 = float(np.float32(TWO_PI - C1))
C3 = float(np.float32(TWO_PI - C1 - np.float64(np.float32(TWO_PI - C1))))
FAR = -1e32

CONST = {}


def constants():
    i = np.arange(P)
    parts = {
        "ident": np.eye(P),
        "ones": np.ones((P, P)),
        "after": i[:, None] > i[None, :],
        "before": i[:, None] < i[None, :],
    }
    dist = np.empty((P, NB, T))
    cdist = np.empty((P, NB, CSTEP))
    for b in range(NB):
        t = b * P + i
        far = t[:, None] - np.arange(T)[None, :]
        dist[:, b] = np.where(far >= 0, -far, FAR)
        far = t[:, None] - (np.arange(CSTEP) * CSTEP + CMPW - 1)[None, :]
        cdist[:, b] = np.where(far >= 0, -far, FAR)
    parts["dist"] = dist
    parts["cdist"] = cdist
    parts["cmask"] = cdist > FAR
    half = HD // 2
    parts["freq"] = np.tile(np.float32(10000.0) ** (-np.arange(half, dtype=np.float32) / np.float32(half)), (P, 1))
    parts["iota"] = np.tile(np.arange(NKEY), (P, 1))
    at, out = 0, []
    for name, a in parts.items():
        a = np.asarray(a, np.float32).reshape(P, -1)
        CONST[name] = (at, at + a.shape[1])
        at += a.shape[1]
        out.append(a)
    return np.ascontiguousarray(np.concatenate(out, 1))


def decay_table():
    i = np.arange(P, dtype=np.float64)
    log_g = np.log1p(-(2.0 ** (-5.0 - np.arange(NH))))
    rel = i[None, :] - i[:, None]
    table = np.empty((P, 2, NH, P))
    for h in range(NH):
        table[:, 0, h] = np.where(rel >= 0, np.exp(log_g[h] * np.maximum(rel, 0)), 0)
        table[:, 1, h] = np.exp(log_g[h] * (P + rel))
    return (table * HD ** -0.5).astype(np.float32).reshape(P, -1)


R_Q, R_K, R_V, R_G, S_Q, S_K, S_V = range(7)
WIN = (S_Q, S_K, R_Q, R_K, S_V, R_V, R_G)
ADA_FIRST = 4
ADA_SECOND = (6, 7, 8, 9)
ADA_GATE1 = (4, 5)
ADA_GATE2 = (10, 11)
ADA = ADA_SECOND + ADA_GATE1 + ADA_GATE2
GROUPS = CHUNK // P
M_SHIFT, M_SCALE, M_SHIFT2, M_SCALE2 = 0, KC, 3 * KC, 4 * KC
G_1, G_2, G_MIX, G_OUT, G_FFN = range(5)

STREAM = (
    [("win", j, "act") for j in WIN] + [("wout", j, "dve") for j in range(2)]
    + [("wq", j, "act") for j in range(4)] + [("dn", j, "act") for j in range(LEAD)]
    + [x for j in range(STEPS) for x in ([("dn", j + LEAD, "act")] if j + LEAD < STEPS else []) + [("ex", j, None)]]
    + [("win2", j, "act") for j in range(6)] + [("cmp", j, None) for j in range(2)]
    + [("wo", j, "dve") for j in range(2)]
    + [("up", 0, "act")]
    + [x for j in range(1, 8) for x in (("up", j, "act"), ("down", j - 1, None))] + [("down", 7, None)]
)
NTH = {(k, j): n for n, (k, j, _) in enumerate(STREAM)}


def emptied():
    found, count, place = {}, {"act": 0, "dve": 0}, 0
    for n, (_, _, who) in enumerate(STREAM):
        if who:
            count[who] += 1
            found[n] = (place, who, count[who])
            place += 1
    return found


RAW = ("cmp",)
SPLIT_BEFORE = [sum(k not in RAW for k, _, _ in STREAM[:n]) * PARTS for n in range(len(STREAM) + 1)]
RAW_BEFORE = [sum(k in RAW for k, _, _ in STREAM[:n]) for n in range(len(STREAM) + 1)]
BY_POOL = [NTH["wq", j] for j in range(2, 4)] + [NTH["dn", j] for j in range(LEAD)]
POOL0, POOL1 = SPLIT_BEFORE[BY_POOL[0]], SPLIT_BEFORE[BY_POOL[-1] + 1]
EMPTIED = emptied()
BY_PLACE = {p: (who, c) for p, who, c in EMPTIED.values()}


class Chain:

    def __init__(self, eng, sem):
        self.eng, self.sem, self.n = eng, sem, 0

    def __call__(self, ins):
        self.n += 1
        ins.then_inc(self.sem, 1)
        self.eng.wait_ge(self.sem, self.n)

    def restart(self):
        self.eng.sem_clear(self.sem)
        self.n = 0


def two_blocks(nc, a, out, stop=None):
    ctx = ExitStack()
    with ctx:
        def sb(name, shape, dt=F32):
            return ctx.enter_context(nc.sbuf_tensor(name, shape, dt))

        def sem(name):
            return ctx.enter_context(nc.semaphore(name))

        n_const = a["const"].shape[1]
        const = sb("const", [P, n_const])
        x_tok = sb("x_tok", [P, NB, D])
        h_tok = sb("h_tok", [P, NB, D])
        hT_hi = sb("hT_hi", [P, KC, T], F32R)
        hT_lo = sb("hT_lo", [P, KC, T], F32R)
        pages = sb("pages", [P, 4 * D])
        spare = sb("spare", [P, 2 * D])
        late = sb("late", [P, 1536])
        diag = sb("diag", [P, 4, P])
        modc = sb("modc", [P, 5 * KC])
        gains = sb("gains", [P, 5, KC])
        small = sb("small", [P, 7, HD])
        wring = sb("wring", [P, RING, SLOT])
        w_hi = sb("w_hi", [P, PARTS, PART], F32R)
        w_lo = sb("w_lo", [P, PARTS, PART], F32R)
        csilu = sb("csilu", [P, 2, KC])
        adab = sb("adab", [P, 6 * KC])
        adab_rows = sb("adab_rows", [12, CHUNK])
        posi = sb("posi", [P, NB], I32)
        posf = sb("posf", [P, NB])
        st = sb("st", [P, 10, 16])
        cbias = sb("cbias", [P, 2, 2])
        w2 = sb("w2", [P, 2, 2, HD])
        b2 = sb("b2", [1, 2, HD])
        topi = sb("topi", [P, NB, 2, PK], U32)
        besti1 = sb("besti1", [P, NB, PK], U32)
        besti = sb("besti", [P, NB, 2, PH, PK], U32)
        cur = sb("cur", [P, 2, 3, OB * OT])
        gatec = sb("gatec", [P, NB, NH, 3])
        mx = sb("mx", [P, 2, NB, R])
        sm = sb("sm", [P, 2, NB, R])
        kcn = sb("kcn", [64, 2, HD])
        kcq = sb("kcq", [64, HD])
        kcst = sb("kcst", [64, 4])
        kcmpT = sb("kcmpT", [P, 64])
        peT = sb("peT", [P, 2, NPAIR])
        with ExitStack() as peer_only:
            a_hi = peer_only.enter_context(nc.sbuf_tensor("a_hi", [P, 4, T], F32R))
            a_lo = peer_only.enter_context(nc.sbuf_tensor("a_lo", [P, 4, T], F32R))
            peer_arena = peer_only.enter_context(nc.sbuf_tensor("peer_arena", [P, 14336], F32))
        arena = sb("arena", [P, 16384])
        ps = ctx.enter_context(nc.psum_tensor("ps", [P, 8, 512], F32))
        psf = ps[:, :, :].rearrange("p b n -> p (b n)")

        def con(name, *dims):
            lo, hi = CONST[name]
            v = const[:, lo:hi]
            return v

        ident, ones = con("ident"), con("ones")
        PAGES = [pages[:, k * D:(k + 1) * D] for k in range(4)]
        GATE1, GATE2 = late[:, 512:512 + D], PAGES[3]

        proj = arena[:, 0:NB * 3584].rearrange("p (b n) -> p b n", b=NB)
        qT = arena[:, 7168:8192].rearrange("p (c t) -> p c t", c=4)
        kT = arena[:, 8192:9216].rearrange("p (c t) -> p c t", c=4)
        tiles = arena[:, 9216:15360].rearrange("p (k n) -> p k n", k=4)
        ada_places = [pages[:, :], arena[:, 0:4096], arena[:, 4096:8192], arena[:, 8192:12288]]
        trig = arena[:, 15360:15488].rearrange("p (f b n) -> p f b n", f=2, b=NB)
        ang = late[:, 512:576].rearrange("p (b n) -> p b n", b=NB)
        turns = late[:, 576:704].rearrange("p (f b n) -> p f b n", f=2, b=NB)
        ang2 = late[:, 704:832].rearrange("p (f b n) -> p f b n", f=2, b=NB)
        ada_sum = arena[:, 15488:16000]
        rot = [late[:, 512 + k * 512:1024 + k * 512].rearrange("p (h d) -> p h d", d=HD // 2) for k in range(2)]
        decay = spare[:, :].rearrange("p (k h i) -> p k h i", k=2, h=NH)
        rgain = late[:, 0:HW]

        def heads(v):
            return v.rearrange("p b (h d) -> p b h d", d=HD)

        def every_other(v, par):
            return v.rearrange("p (h u d) -> p u h d", u=2, d=HD)[:, par, :, :]

        h_flat = h_tok[:, :, :].rearrange("p b n -> p (b n)")
        h_full = h_flat.rearrange("p (k t) -> p k t", k=KC)
        qryT = peer_arena[:, 0:16 * T].rearrange("p (c t) -> p c t", c=16)
        onehot = peer_arena[:, 0:4096].rearrange("p (k s t n) -> p k s t n", k=2, s=OB, t=OT)
        score = peer_arena[:, 4096:8192].rearrange("p (b h n) -> p b h n", b=NB, h=PH)
        gates_in = peer_arena[:, 4096:8192].rearrange("p (s g f t) -> p s g f t", s=2, g=T // 16, t=16)
        keys = peer_arena[:, 10240:12288].rearrange("p (c n) -> p c n", n=NKEY)
        acts = [v.rearrange("p (f t) -> p f t", f=EF) for v in
                [peer_arena[:, 8192 + k * 1024:9216 + k * 1024] for k in range(4)]
                + PAGES[0:3] + [h_flat[:, 0:1024]]]
        spread = [v.rearrange("p (n t) -> p n t", t=16) for v in (peer_arena[:, 12288:14336], spare[:, :])]
        pick = peer_arena[:, 0:4096].rearrange("p (b h i j) -> p b h i j", b=NB, h=PH, j=PK)
        sc2, cand, cand2 = (h_flat[:, k * 512:(k + 1) * 512].rearrange("p (b n) -> p b n", b=NB) for k in range(3))
        best1 = h_flat[:, 1536:1568].rearrange("p (b n) -> p b n", b=NB)
        top = h_flat[:, 1568:1632].rearrange("p (b k n) -> p b k n", b=NB, k=2)
        best = h_flat[:, 1632:1888].rearrange("p (b h n) -> p b h n", b=NB, h=PH)
        gsum = h_flat[:, 1888:1904].rearrange("p (b h) -> p b h", b=NB)
        topf = spare[:, 0:512].rearrange("p (b h k n) -> p b h k n", b=NB, h=PH, k=2)
        bestf = spare[:, 512:1024].rearrange("p (b k h n) -> p b k h n", b=NB, k=2, h=PH)
        sel = late[:, 0:768].rearrange("p (b k n) -> p b k n", b=NB, k=3)
        selT = late[:, 768:1536].rearrange("p (k t) -> p k t", k=3)
        gates_dram = nc.dram_tensor("gates_by_expert", (T // 16, P, NKEY * 16), F32, kind="Internal").ap()

        z = arena[:, 0:NB * ZW].rearrange("p (b n) -> p b n", b=NB)
        o = NB * ZW
        qT2 = arena[:, o:o + 1024].rearrange("p (c t) -> p c t", c=4)
        kT2 = arena[:, o + 1024:o + 2048].rearrange("p (r g t) -> p r g t", r=2, g=NG)
        kvA = arena[:, o + 2048:o + 3072].rearrange("p (v g t) -> p v g t", v=2, g=NG)
        blkT = arena[:, o + 3072:o + 4032].rearrange("p (v m c) -> p v m c", v=2, m=NPAIR)
        hdnT = arena[:, o + 4032:o + 4160].rearrange("p (f c) -> p f c", f=2)
        o += 4288
        ptile = arena[:, o:o + 3072].rearrange("p (k n) -> p k n", k=2)
        pT = arena[:, o + 3072:o + 4608].rearrange("p (k r t) -> p k r t", k=3, r=R)
        kdup = arena[:, o:o + 1024].rearrange("p (b r g u d) -> p b r g u d", b=NB, r=2, g=NG, u=2)
        o += 4608
        tmp = arena[:, o:o + 1024].rearrange("p (b n) -> p b n", b=NB)
        sqq = ptile[:, 0, 0:1024].rearrange("p (b h d) -> p b h d", b=NB, d=HD)
        tmp_k = ptile[:, 1, 1024:1280].rearrange("p (b g d) -> p b g d", b=NB, g=NG)
        kvdup = arena[:, o:o + 1024].rearrange("p (b v g u d) -> p b v g u d", b=NB, v=2, g=NG, u=2)
        hdnV = arena[:, o + 1024:o + 1536].rearrange("p (f g r n) -> p f g r n", f=2, g=NG, r=R)
        assert o + 1536 <= 16384
        sh1 = h_tok[:, :, HW:D]
        sh2 = GATE2.rearrange("p (b n) -> p b n", b=NB)
        convw = late[:, 0:3 * HW].rearrange("p (k n) -> p k n", k=3)
        vbd = spare[:, 0:512].rearrange("p (g r d) -> p g r d", g=NG, r=R)
        pcmp = spare[:, 512:1024].rearrange("p (b h n) -> p b h n", b=NB, h=NH)
        pcT = spare[:, 1024:1536].rearrange("p (b g t) -> p b g t", b=NB, g=NG)
        pcs = spare[:, 1536:1792].rearrange("p (c n) -> p c n", n=CSTEP)
        cst = spare[:, 1792:1840].rearrange("p (k c) -> p k c", k=3)
        uT = arena[:, 4096:6144].rearrange("p (s f t) -> p s f t", s=2, f=4)

        ld_ident, ld_const, ld_x, ld_pos, ld_c, ld_gain, ld_early, ld_keys, ld_gates, ld_late, ld_cmp = (
            sem(s) for s in ("ld_ident", "ld_const", "ld_x", "ld_pos", "ld_c", "ld_gain", "ld_early", "ld_keys", "ld_gates",
                             "ld_late", "ld_cmp"))
        ada_in = [sem(f"ada_in{k}") for k in range(ADA_FIRST)]
        ada_later_in = sem("ada_later_in")
        w_in_slot = [sem(f"w_in_slot{k}") for k in range(RING)]
        w_used = sem("w_used")
        split_hi = sem("split_hi")
        split_lo = sem("split_lo")
        split_lo_pool = sem("split_lo_pool")
        parts_used = sem("parts_used")
        emptied_by = {"act": sem("emptied_by_act"), "dve": sem("emptied_by_dve")}
        dve_own, act_own, pool_own = sem("dve_own"), sem("act_own"), sem("pool_own")
        names = """silu_c h_scaled ada_summed ada_used mod_taken mod_ready gate_out sumsq var std h_ready h_turned h_split tr_done tr_copied_act tr_copied_dve angles trig_ready
        rot_ready ret_scores ret_decayed ret_y ret_y_out ret_gate var_s std_s sbq_ready sb_z sb_exp sb_L sb_ls sb_cum
        sb_logw sb_w sb_y sb_y_out y_ready x1_ready sub_done sub_out
        tr_hi a_hi_ready a_lo_ready score_max exp_done sel_ready sel_turned cur_ready onehot_raw onehot_ready onehot_used spread_out weighed x2_ready
        late_free zrms zstd kv_ready kv_copied blk_ready hdn_out kcmp kvar kstd kcn_ready vcmp_out kct_copied
        s_done s_max p_ready pt_done pt_out o_done o_out cs_done c_max c_exp c_ready c_tr c_out co_done
        u_ready u_shifted conv_out u2_ready x_out stored choose0 choose1""".split()
        S = {n: sem(n) for n in names}
        gates_stored = [sem(f"gates_stored{k}") for k in range(2)]
        gates_landed = [sem(f"gates_landed{k}") for k in range(2)]

        block = ctx.enter_context(nc.Block())

        def emptied_count(kind, j):
            return EMPTIED[NTH[kind, j]][2]

        def pair(kind, j):
            return 2 * (EMPTIED[NTH[kind, j]][0] % 2)

        def ada_rows(j):
            return a["ada_w"][:, j * CHUNK:(j + 1) * CHUNK].rearrange("(k p) n -> p k n", p=P)

        def ada_landed(eng, j):
            first = j < ADA_FIRST
            if first:
                eng.wait_ge(ada_in[j], 16)
            else:
                eng.wait_ge(ada_later_in, 16 * (ADA.index(j) + 1))
            return ada_places[j if first else 0].rearrange("p (k n) -> p k n", n=CHUNK)

        sum_place = {j: ada_places[j][:, 0:CHUNK] for j in range(ADA_FIRST)}
        sum_place.update({j: ada_sum for j in ADA_SECOND})
        sum_place.update({j: spare[:, D + n * CHUNK:D + (n + 1) * CHUNK] for n, j in enumerate(ADA_GATE2)})

        def summed(j):
            return list(sum_place).index(j) + 1

        def stands(eng, kind, j):
            n = NTH[kind, j]
            if kind in RAW:
                eng.wait_ge(w_used, RAW_BEFORE[n + 1])
            else:
                eng.wait_ge(parts_used, SPLIT_BEFORE[n + 1])

        def slot_left(eng, n):
            if STREAM[n][0] in RAW:
                eng.wait_ge(w_used, RAW_BEFORE[n + 1])
            elif n in BY_POOL:
                eng.wait_ge(split_lo_pool, SPLIT_BEFORE[n + 1] - POOL0)
            else:
                eng.wait_ge(split_lo, rests(SPLIT_BEFORE[n + 1]))

        def rests(parts):
            if isinstance(parts, int) and parts <= POOL0:
                return parts
            return parts - (POOL1 - POOL0)

        def part_of(kind, raw, u, cols=CHUNK):
            if kind in ("wq", "up"):
                return raw.rearrange("p (k n) -> p k n", n=CHUNK)[:, :, u * P:(u + 1) * P]
            part = raw[:, u * PART:(u + 1) * PART]
            return part.rearrange("p (k n) -> p k n", n=CHUNK)[:, :, 0:cols]

        def split_part(kind, v, u, cols=CHUNK):
            if kind in ("wq", "up"):
                return v[:, u, :].rearrange("p (k n) -> p k n", n=P)
            return v[:, u, :].rearrange("p (k n) -> p k n", n=CHUNK)[:, :, 0:cols]

        def bank_set(i):
            return 4 - 4 * (i % 2)

        def column(v, first):
            return lambda k: v[:, first + k:first + k + 1]

        def gain(which):
            return lambda k: gains[:, which, k:k + 1]

        def width(kind, j):
            return min(CHUNK, ZW - j * CHUNK) if kind == "win2" else CHUNK

        down0, down_next, out_next = NTH["dn", 0], NTH["dn", LEAD], EMPTIED[NTH["dn", LEAD]][2]
        TURNS = (STEPS - LEAD) // LEAD

        def part0(i):
            return i * (2 * PARTS) + SPLIT_BEFORE[down_next]

        def slot_parts(i):
            if has_down(i):
                return part0(i), part0(i) + PARTS
            return None, SPLIT_BEFORE[NTH["ex", i]]

        def ring_turn(i, up):
            if not isinstance(i, int):
                n = down_next + up
                return n % RING, i * 16 + 16 * (n // RING + 1)
            n = NTH["ex", i] if up else NTH["dn", i + LEAD]
            return n % RING, 16 * (n // RING + 1)

        def expert_steps(fori, body):
            with fori(0, TURNS) as turn:
                for k in range(LEAD):
                    body(turn * LEAD + k, k)
            for i in range(TURNS * LEAD, STEPS):
                body(i, i % LEAD)

        def has_down(i):
            return not isinstance(i, int) or i + LEAD < STEPS

        @block.sync
        def _(sp):
            sp.dma_start(csilu[:, 0, :], a["c"]).then_inc(ld_c, 16)
            sp.dma_start(adab[:, :], a["ada_b"]).then_inc(ld_c, 16)
            sp.dma_start(adab_rows[:, :], a["ada_b_rows"]).then_inc(ld_c, 16)
            hi = CONST["ones"][1]
            sp.dma_start(const[:, 0:hi], a["const"][:, 0:hi]).then_inc(ld_ident, 16)
            sp.dma_start(x_tok[:, :, :], a["x"].rearrange("(b p) n -> p b n", p=P)).then_inc(ld_x, 16)

            def weights(n):
                kind, j, _ = STREAM[n]
                slot = wring[:, n % RING, :]
                if n >= RING:
                    slot_left(sp, n - RING)
                cols = slice(j * CHUNK, (j + 1) * CHUNK)
                if kind == "dn":
                    src, dst = a["peer_down"][j * P:(j + 1) * P, :], slot
                elif kind == "cmp":
                    src = a["w_cmp1"][j].rearrange("(m p) n -> p m n", p=P)
                    dst = slot.rearrange("p (m n) -> p m n", n=CF)
                elif kind == "down":
                    src = a["w_down"][cols, :].rearrange("(f p) n -> p f n", p=P)
                    dst = slot.rearrange("p (f n) -> p f n", n=D)
                else:
                    w = a[{"win": "w_in", "wout": "w_out", "wq": "w_query", "win2": "w_in2",
                           "wo": "w_o", "up": "w_up"}[kind]]
                    last = min((j + 1) * CHUNK, w.shape[1])
                    src = w[:, j * CHUNK:last].rearrange("(k p) n -> p k n", p=P)
                    dst = slot.rearrange("p (k n) -> p k n", k=KC)[:, :, 0:last - j * CHUNK]
                sp.dma_start(dst, src).then_inc(w_in_slot[n % RING], 16)

            for j in range(ADA_FIRST):
                sp.dma_start(ada_places[j].rearrange("p (k n) -> p k n", k=KC), ada_rows(j)).then_inc(ada_in[j], 16)
            sp.dma_start(gains[:, :, :], a["gains"]).then_inc(ld_gain, 16)
            for n in range(RING):
                weights(n)
            sp.dma_start(const[:, hi:], a["const"][:, hi:]).then_inc(ld_const, 16)
            sp.dma_start(posi[:, :], a["positions"].rearrange("(b p) -> p b", p=P),
                         allow_slow_non_contiguous=True).then_inc(ld_pos, 16)
            sp.dma_start(spare[:, :], a["decay"]).then_inc(ld_early, 16)
            sp.dma_start(rgain, a["ret_gain"].partition_broadcast(P)).then_inc(ld_early, 16)
            for k, name in enumerate(("sb_q", "sb_k", "sb_out", "g_q")):
                sp.dma_start(small[:, k, :], a[name].partition_broadcast(P)).then_inc(ld_early, 16)
            sp.dma_start(small[:, 4:7, :].rearrange("p k d -> p (k d)"),
                         a["g_k"].partition_broadcast(P)).then_inc(ld_early, 16)
            sp.dma_start(peT[:, :, :], a["pe"]).then_inc(ld_cmp, 16)
            sp.dma_start(cbias[:, :, :], a["b_cmp1"]).then_inc(ld_cmp, 16)
            sp.dma_start(w2[:, :, :, :], a["w_cmp2"].rearrange("v (f p) d -> p v f d", p=P)).then_inc(ld_cmp, 16)
            sp.dma_start(b2[:, :, :], a["b_cmp2"]).then_inc(ld_cmp, 16)
            for n in range(RING, NTH["wq", RING]):
                weights(n)
            sp.wait_ge(S["h_ready"], 4)
            sp.dma_start(keys.rearrange("p c n -> p (c n)"), a["keys"]).then_inc(ld_keys, 16)
            for n in range(NTH["wq", RING], down_next):
                weights(n)

            def expert_slots(i, k):
                down, up = slot_parts(i)
                if has_down(i):
                    par, _ = ring_turn(i, 0)
                    if isinstance(i, int):
                        slot_left(sp, NTH["dn", i + LEAD] - RING)
                    elif k == 0:
                        slot_left(sp, down_next - RING)
                        sp.wait_ge(split_lo, rests(down - PARTS))
                    else:
                        sp.wait_ge(split_lo, rests(down - PARTS))
                    sp.dma_start(wring[:, par, :], a["peer_down"][bass.ds(i * P + LEAD * P, P), :])\
                        .then_inc(w_in_slot[par], 16)
                par, _ = ring_turn(i, 1)
                if k == 0 and not isinstance(i, int):
                    slot_left(sp, down_next + 1 - RING)
                sp.wait_ge(split_lo, rests(up - PARTS))
                sp.dma_start(wring[:, par, :].rearrange("p (f n) -> p f n", n=D),
                             a["peer_up"][bass.ds(i * CHUNK, CHUNK), :].rearrange("(f p) n -> p f n", p=P))\
                    .then_inc(w_in_slot[par], 16)

            expert_steps(sp.Fori, expert_slots)
            first_late = NTH["win2", 0]
            for n in range(first_late, first_late + RING):
                weights(n)
            sp.wait_ge(S["late_free"], 1)
            sp.dma_start(late[:, 0:3 * HW], a["conv_w"].partition_broadcast(P)).then_inc(ld_late, 16)
            for n in range(first_late + RING, len(STREAM)):
                weights(n)
            for b in range(NB):
                sp.wait_ge(S["x_out"], b + 1)
                sp.dma_start(out[b * P:(b + 1) * P, :], x_tok[:, b, :]).then_inc(S["stored"], 16)
            sp.wait_ge(S["stored"], 16 * NB)

        @block.tensor
        def _(pe):
            def slot(n, inner):
                pe.wait_ge(w_in_slot[n % RING], 16 * (n // RING + 1))
                return wring[:, n % RING, :].rearrange("p (k n) -> p k n", n=inner)

            def free_banks(n):
                place = EMPTIED[n][0]
                if place >= 2:
                    who, count = BY_PLACE[place - 2]
                    pe.wait_ge(emptied_by[who], count)
                return 2 * (place % 2)

            def ada_columns(j, bank):
                pe.wait_ge(S["ada_summed"], summed(j))
                for g in range(GROUPS):
                    at = bank * 512 + GROUPS * j + g
                    mm = pe.matmul(psf[:, at:at + 1], sum_place[j][:, g * P:(g + 1) * P], ones[:, 0:1],
                                   start=True, stop=True)
                mm.then_inc(S["ada_used"], 1)

            def ada_bias(j, bank):
                pe.matmul(ps[:, bank, :], ident[0:12, j:j + 1].to_broadcast([12, P]), adab_rows[:, :],
                          start=False, stop=True).then_inc(S["ada_used"], 1)

            def ada_gate1(j, bank):
                w = ada_landed(pe, j)
                for k in range(KC):
                    pe.matmul(ps[:, bank, :], csilu[:, 1, k:k + 1].to_broadcast([P, P]), w[:, k, :],
                              start=(k == 0), stop=False)
                ada_bias(j, bank)

            def ada_gate2(j, bank):
                pe.wait_ge(S["ada_summed"], summed(j))
                pe.matmul(ps[:, bank, :], ones, sum_place[j], start=True, stop=False)
                ada_bias(j, bank)

            def split_landed(n, u):
                if n in BY_POOL:
                    pe.wait_ge(split_lo_pool, SPLIT_BEFORE[n] - POOL0 + u + 1)
                else:
                    pe.wait_ge(split_lo, rests(SPLIT_BEFORE[n] + u + 1))

            def token_part(kind, u, bank, cols):
                hi, lo = (split_part(kind, v, u, cols) for v in (w_hi, w_lo))
                for kk in range(2):
                    k = 2 * u + kk
                    for b in range(NB):
                        t = slice(b * P, (b + 1) * P)
                        o = ps[:, bank + b, 0:cols]
                        pe.matmul(o, hT_hi[:, k, t], hi[:, kk, :], start=(k == 0), stop=False)
                        pe.matmul(o, hT_hi[:, k, t], lo[:, kk, :], start=False, stop=False)
                        mm = pe.matmul(o, hT_lo[:, k, t], hi[:, kk, :], start=False, stop=(k == KC - 1))
                mm.then_inc(parts_used, 1)

            def column_part(bank, u):
                hi, lo = (v[:, u, :].rearrange("p (k n) -> p k n", n=P) for v in (w_hi, w_lo))
                o = psf[:, bank * 512 + u * T:bank * 512 + (u + 1) * T]
                for k in range(KC):
                    pe.matmul(o, hi[:, k, :], hT_hi[:, k, :], start=(k == 0), stop=False)
                    pe.matmul(o, hi[:, k, :], hT_lo[:, k, :], start=False, stop=False)
                    mm = pe.matmul(o, lo[:, k, :], hT_hi[:, k, :], start=False, stop=(k == KC - 1))
                mm.then_inc(parts_used, 1)

            def row_part(u, first, last):
                hi, lo = (v[:, u, :].rearrange("p (s n) -> p s n", n=512) for v in (w_hi, w_lo))
                for b in range(NB):
                    t = slice(b * P, (b + 1) * P)
                    for half in range(2):
                        o = ps[:, 4 + 2 * b + half, :]
                        pe.matmul(o, a_hi[:, u, t], hi[:, half, :], start=first, stop=False, skip_group_check=True)
                        pe.matmul(o, a_hi[:, u, t], lo[:, half, :], start=False, stop=False, skip_group_check=True)
                        mm = pe.matmul(o, a_lo[:, u, t], hi[:, half, :], start=False, stop=last, skip_group_check=True)
                mm.then_inc(parts_used, 1)

            def by_tokens(kind, j, rounds=None, parts=range(PARTS)):
                n = NTH[kind, j]
                bank = free_banks(n)
                for u in parts:
                    if rounds and u % 2 == 0:
                        h_stands(rounds, u // 2)
                    split_landed(n, u)
                    token_part(kind, u, bank, width(kind, j))

            def by_columns(kind, j):
                n = NTH[kind, j]
                bank = free_banks(n)
                for u in range(PARTS):
                    split_landed(n, u)
                    column_part(bank, u)

            def turn_round(src, what):
                for k in range(what):
                    for b in range(NB):
                        at = 4 * 512 + k * T + b * P
                        mm = pe.transpose(psf[:, at:at + P], src(k, b), ident)
                mm.then_inc(S["tr_done"], 1)

            def turn_h(count, src, scale=lambda b, k: b):
                for b in range(NB):
                    pe.wait_ge(S["h_ready"], count - 1 + b)
                    for k in range(KC):
                        at = 4 * 512 + k * T + b * P
                        mm = pe.matmul(psf[:, at:at + P], src(b, k), diag[:, scale(b, k), :], start=True, stop=True)
                        if b == 1 and k % 4 == 3:
                            mm.then_inc(S["h_turned"], 1)

            def turn_x(count):
                turn_h(count, lambda b, k: x_tok[:, b, k * P:(k + 1) * P])

            def h_stands(rounds, half):
                pe.wait_ge(S["h_split"], 2 * rounds - 1 + half)

            def copied(r):
                pe.wait_ge(S["tr_copied_act"], r)
                pe.wait_ge(S["tr_copied_dve"], r)

            def head_scores(bank, b4):
                for n, (jb, ib) in enumerate(PAIRS):
                    for c in range(4):
                        lo = HD * b4
                        mm = pe.matmul(ps[:, bank + n, c * P:(c + 1) * P], kT[lo:lo + HD, c, jb * P:(jb + 1) * P],
                                       qT[lo:lo + HD, c, ib * P:(ib + 1) * P], start=True, stop=True)
                return mm

            def head_values(bank, tile, v, b4):
                for hh in range(4):
                    col = (2 * hh + b4) * HD
                    w = [tile[:, n * 512 + hh * P:n * 512 + (hh + 1) * P] for n in range(3)]
                    pe.matmul(ps[:, bank, hh * HD:(hh + 1) * HD], w[0], v[:, 0, col:col + HD], start=True, stop=True)
                    at = 4 * HD + hh * HD
                    pe.matmul(ps[:, bank, at:at + HD], w[1], v[:, 0, col:col + HD], start=True, stop=False)
                    mm = pe.matmul(ps[:, bank, at:at + HD], w[2], v[:, 1, col:col + HD], start=False, stop=True)
                return mm

            def log_stays(b4):
                ls = tiles[:, 2 * b4 + 1, :].rearrange("p (k n) -> p k n", k=3)
                pe.wait_ge(S["sb_ls"], b4 + 1)
                pe.matmul(ps[:, 4, :], con("after"), ls[:, 0, :], start=True, stop=True)
                pe.matmul(ps[:, 5, :], con("after"), ls[:, 1, :], start=True, stop=False)
                pe.matmul(ps[:, 5, :], ones, ls[:, 2, :], start=False, stop=True)
                pe.matmul(ps[:, 6, :], con("after"), ls[:, 2, :], start=True, stop=True).then_inc(S["sb_cum"], 1)

            pe.wait_ge(ld_ident, 16)
            turn_x(2)
            for j in range(ADA_FIRST):
                ada_columns(j, 3)
            by_tokens("win", S_Q, 1)
            by_tokens("win", S_K)
            by_tokens("win", R_Q)
            pe.wait_ge(S["sbq_ready"], 2)
            turn_round(lambda k, b: proj[:, b, (4 * HW + k * P):(4 * HW + (k + 1) * P)], KC)
            copied(1)
            ada_columns(6, 7)
            head_scores(4, 0).then_inc(S["sb_z"], 1)
            by_tokens("win", R_K)
            pe.wait_ge(ld_const, 16)
            log_stays(0)
            ada_columns(7, 7)
            pe.wait_ge(S["sb_logw"], 1)
            head_scores(4, 1).then_inc(S["sb_z"], 1)
            by_tokens("win", S_V)
            log_stays(1)
            ada_columns(8, 7)
            by_tokens("win", R_V, parts=range(0, 2))
            pe.wait_ge(emptied_by["act"], emptied_count("win", S_V))
            for b4 in range(2):
                pe.wait_ge(S["sb_w"], b4 + 1)
                head_values(b4, tiles[:, 2 * b4, :], proj[:, :, 6 * HW:7 * HW], b4).then_inc(S["sb_y"], 1)
            pe.wait_ge(S["rot_ready"], 2)
            pe.wait_ge(S["sb_logw"], 2)
            pe.wait_ge(S["mod_taken"], 1)
            turn_round(lambda k, b: h_tok[:, b, k * P:(k + 1) * P], KC)
            by_tokens("win", R_V, parts=range(2, PARTS))
            copied(2)
            head_scores(4, 0).then_inc(S["ret_scores"], 1)
            pe.wait_ge(S["sb_y_out"], 2)
            by_tokens("win", R_G, parts=range(0, 2))
            pe.wait_ge(S["ret_decayed"], 1)
            head_scores(4, 1).then_inc(S["ret_scores"], 1)
            by_tokens("win", R_G, parts=range(2, PARTS))
            ada_columns(9, 7)
            pe.wait_ge(emptied_by["act"], emptied_count("win", R_V))
            for b4 in range(2):
                pe.wait_ge(S["ret_decayed"], b4 + 1)
                head_values(2 + b4, tiles[:, b4, :], proj[:, :, 2 * HW:3 * HW], b4).then_inc(S["ret_y"], 1)
            pe.wait_ge(ld_c, 48)
            pe.wait_ge(emptied_by["act"], emptied_count("win", R_G))
            ada_gate1(4, 0)
            for half in (1, 0):
                pe.wait_ge(S["y_ready"], 2 - half)
                if half == 1:
                    pe.wait_ge(S["mod_ready"], 2)
                for k in range(4 * half, 4 * half + 4):
                    for b in range(NB):
                        at = 4 * 512 + k * T + b * P
                        mm = pe.transpose(psf[:, at:at + P], proj[:, b, k * P:(k + 1) * P], ident)
                mm.then_inc(S["h_turned"], 1)
            ada_gate1(5, 1)
            h_stands(2, 1)
            by_tokens("wout", 0)
            pe.wait_ge(S["gate_out"], 1)
            by_tokens("wout", 1)

            turn_x(4)
            for half in range(2):
                h_stands(3, half)
            def key_scores(j):
                pe.wait_ge(emptied_by["act"], emptied_count("wq", j))
                if j >= 2:
                    pe.wait_ge(S["sub_out"], j - 1)
                for b in range(NB):
                    for i in range(4):
                        mm = pe.matmul(ps[:, 4 + 2 * (j % 2) + b, i * NKEY:(i + 1) * NKEY],
                                       qryT[:, 4 * j + i, b * P:(b + 1) * P], keys[:, 4 * j + i, :], start=True, stop=True)
                mm.then_inc(S["sub_done"], 1)

            by_columns("wq", 0)
            pe.wait_ge(ld_keys, 16)
            for j in range(1, 4):
                by_columns("wq", j)
                if j == 1:
                    for n, k in enumerate(ADA_GATE2):
                        ada_gate2(k, 6 + n)
                if j == 2:
                    pe.wait_ge(S["gate_out"], 2)
                key_scores(j - 1)
            by_columns("dn", 0)
            key_scores(3)
            for j in range(1, LEAD):
                by_columns("dn", j)
            pe.wait_ge(S["sel_ready"], NB)
            for b in range(NB):
                for k in range(3):
                    mm = pe.transpose(ps[:, 4 + b, k * P:(k + 1) * P], sel[:, b, k, :], ident)
            mm.then_inc(S["sel_turned"], 1)
            with pe.Fori(0, T // (2 * OB * OT)) as turn:
                for q in range(2 * OB):
                    pe.wait_ge(S["onehot_ready"], turn * (2 * OB) + (q + 1))
                    if q % 2 == 0:
                        pe.wait_ge(S["spread_out"], turn * OB + (q // 2 + 1))
                    for t in range(OT):
                        at = (4 + 2 * (q // 2 % 2)) * 512 + (q % 2 * OT + t) * NKEY
                        mm = pe.matmul(psf[:, at:at + NKEY], onehot[:, 1, q % OB, t, :], onehot[:, 0, q % OB, t, :],
                                       start=True, stop=True)
                    mm.then_inc(S["onehot_used"], 1)

            pe.wait_ge(S["spread_out"], 2 + T // TT)
            for bank in range(4, 8):
                pe.matmul(ps[:, bank, 0:P], ones[0:1, :], con("after")[0:1, :], start=True, stop=False,
                          skip_group_check=True)

            def expert_products(i, k):
                down, up = slot_parts(i)
                if has_down(i):
                    pe.wait_ge(emptied_by["act"], i + (out_next - 2))
                    for u in range(PARTS):
                        pe.wait_ge(split_lo, rests(down + (u + 1)))
                        column_part(2 * ((EMPTIED[down0][0] + k + LEAD) % 2), u)
                for u in range(PARTS):
                    pe.wait_ge(S["a_lo_ready"], i * PARTS + (u + 1))
                    pe.wait_ge(split_lo, rests(up + (u + 1)))
                    row_part(u, False, False)

            expert_steps(pe.Fori, expert_products)

            turn_x(6)
            for j in range(3):
                by_tokens("win2", j, 4 if j == 0 else None)
            pe.wait_ge(S["kv_ready"], 1)
            for v in range(2):
                for g in range(NG):
                    for b in range(NB):
                        at = 4 * 512 + (v * NG + g) * T + b * P
                        mm = pe.transpose(psf[:, at:at + P],
                                          kvdup[:, b, v, g, :, :].rearrange("p u d -> p (u d)"), ident)
            mm.then_inc(S["c_tr"], 1)
            for j in (3, 4, 5):
                by_tokens("win2", j)

            pe.wait_ge(S["kv_ready"], 2)
            pe.wait_ge(S["kv_copied"], 1)
            turn_round(lambda k, b: z[:, b, k * P:(k + 1) * P] if k < 4 else
                       kdup[:, b, (k - 4) // 2, (k - 4) % 2, :, :].rearrange("p u d -> p (u d)"), KC)
            pe.wait_ge(emptied_by["act"], emptied_count("win2", 5))
            pe.wait_ge(S["blk_ready"], 1)
            for v in range(2):
                w = slot(NTH["cmp", v], CF)
                for f in range(2):
                    at = 3 * 512 + (2 * v + f) * 32
                    for m in range(NPAIR):
                        mm = pe.matmul(psf[:, at:at + 2 * NCMP], w[:, m, f * P:(f + 1) * P], blkT[:, v, m, :],
                                       start=(m == 0), stop=(m == NPAIR - 1))
                mm.then_inc(w_used, 1)
            copied(3)

            def scores(i):
                br, lo = i // 2, HD * (i % 2)
                for r in range(R):
                    for b in range(NB):
                        at = bank_set(i) * 512 + (r * P if b == 0 else 512 + r * T)
                        mm = pe.matmul(psf[:, at:at + (b + 1) * P], qT2[lo:lo + HD, r, b * P:(b + 1) * P],
                                       kT2[lo:lo + HD, br, r // 2, 0:(b + 1) * P], start=True, stop=True)
                mm.then_inc(S["s_done"], 1)

            def weigh(i):
                br, pt, bank = i // 2, ptile[:, i % 2, :], bank_set(i)
                pe.wait_ge(S["p_ready"], i + 1)
                for n, (jb, ib) in enumerate(PAIRS):
                    for r in range(R):
                        lo = r * P if ib == 0 else 512 + r * T + jb * P
                        at = (bank + n) * 512 + r * P
                        mm = pe.transpose(psf[:, at:at + P], pt[:, lo:lo + P], ident)
                mm.then_inc(S["pt_done"], 1)
                pe.wait_ge(S["pt_out"], i + 1)
                if i >= 2:
                    pe.wait_ge(S["o_out"], i - 1)
                elif i == 0:
                    pe.wait_ge(S["c_max"], 1)
                for r in range(R):
                    col = (Z_VS, Z_VW)[br] + (r // 2) * HD
                    v = [z[:, b, col:col + HD] for b in range(NB)]
                    o = ps[:, bank + 3, :]
                    pe.matmul(o[:, r * HD:(r + 1) * HD], pT[:, 0, r, :], v[0], start=True, stop=True)
                    at = (R + r) * HD
                    pe.matmul(o[:, at:at + HD], pT[:, 1, r, :], v[0], start=True, stop=False)
                    mm = pe.matmul(o[:, at:at + HD], pT[:, 2, r, :], v[1], start=False, stop=True)
                mm.then_inc(S["o_done"], 1)

            scores(0)
            pe.wait_ge(S["hdn_out"], 1)
            pe.wait_ge(ld_cmp, 64)
            for f in range(2):
                pe.matmul(ps[0:64, 7, 0:HD], hdnT[:, f, :], w2[:, 0, f, :], start=(f == 0), stop=False)
            pe.matmul(ps[0:64, 7, 0:HD], ones[0:1, 0:64], b2[:, 0, :], start=False, stop=True)
            for g in range(NG):
                o = ps[:, 7, (2 + g) * HD:(3 + g) * HD]
                for f in range(2):
                    pe.matmul(o, hdnV[:, f, g, :, :].rearrange("p r n -> p (r n)"), w2[:, 1, f, :],
                              start=(f == 0), stop=False)
                mm = pe.matmul(o, ones[0:1, :], b2[:, 1, :], start=False, stop=True)
            mm.then_inc(S["kcmp"], 1)
            scores(1)
            pe.wait_ge(S["kcn_ready"], 1)
            pe.wait_ge(S["vcmp_out"], 1)
            pe.transpose(ps[:, 7, 256:320], kcn[:, :, :].rearrange("p u d -> p (u d)"), ident[0:64, 0:64])\
                .then_inc(S["c_tr"], 1)
            pe.wait_ge(S["kct_copied"], 1)
            for b in range(NB):
                for h in range(NH):
                    lo, g = HD * (h % 2), h // R
                    at = (3 + 4 * (h % 2)) * 512 + (b * R + h // 2) * CSTEP
                    mm = pe.matmul(psf[:, at:at + CSTEP], qT2[lo:lo + HD, h // 2, b * P:(b + 1) * P],
                                   kcmpT[lo:lo + HD, g * 32:g * 32 + CSTEP], start=True, stop=True)
            mm.then_inc(S["cs_done"], 1)
            weigh(0)
            scores(2)
            weigh(1)
            scores(3)
            weigh(2)
            pe.wait_ge(S["c_ready"], 1)
            for b in range(NB):
                for g in range(NG):
                    at = 4 * 512 + (b * NG + g) * P
                    mm = pe.transpose(psf[:, at:at + P],
                                      pcmp[:, b, g * R:(g + 1) * R, :].rearrange("p r n -> p (r n)"), ident)
            mm.then_inc(S["c_tr"], 1)
            weigh(3)
            pe.wait_ge(S["c_out"], 1)
            for b in range(NB):
                for g in range(NG):
                    at = (5 + b) * 512 + g * 256
                    mm = pe.matmul(psf[:, at:at + 256], pcT[:, b, g, :],
                                   vbd[:, g, :, :].rearrange("p r d -> p (r d)"), start=True, stop=True)
            mm.then_inc(S["co_done"], 1)

            turn_h(8, lambda b, k: h_tok[:, b, k * P:(k + 1) * P] if k < 4 else z[:, b, Z_H + (k - 4) * P:Z_H + (k - 3) * P],
                   lambda b, k: b if k < 4 else 2 + b)
            for j in range(2):
                by_tokens("wo", j, 5 if j == 0 else None)

            turn_x(10)
            for half in range(2):
                h_stands(6, half)
            last = DFF // CHUNK - 1
            for j in range(last + 2):
                if j <= last:
                    by_columns("up", j)
                if j >= 1:
                    for u in range(PARTS):
                        pe.wait_ge(S["a_lo_ready"], (STEPS + j - 1) * PARTS + u + 1)
                        split_landed(NTH["down", j - 1], u)
                        row_part(u, j == 1 and u == 0, j == last + 1 and u == PARTS - 1)

        @block.scalar
        def _(act):
            own = Chain(act, act_own)

            def squares(b0, width, view, row):
                for b in range(NB):
                    act.activation(view(b)[1], view(b)[0], ACT.Square,
                                   accum_out=st[:, row, b0 + b:b0 + b + 1]).then_inc(S["sumsq"], 1)

            def add_squares(j, wait, count, junk):
                act.wait_ge(S[wait], count)
                cols = slice(j * CHUNK, (j + 1) * CHUNK)
                for b in range(NB):
                    act.activation(junk[:, b, 0:CHUNK], x_tok[:, b, cols], ACT.Square,
                                   accum_out=st[:, 0, NB * j + b:NB * j + b + 1]).then_inc(S["sumsq"], 1)

            def root(cols, src, dst, wait, count, done):
                act.wait_ge(S[wait], count)
                rows = (cols + 15) // 16
                cols = min(cols, 16)
                act.activation(st[:, dst:dst + rows, 0:cols], st[:, src:src + rows, 0:cols], ACT.Sqrt)\
                    .then_inc(S[done], 1)

            def split(kind, j, acts=None, last=None, parts=range(PARTS)):
                n = NTH[kind, j]
                act.wait_ge(w_in_slot[n % RING], 16 * (n // RING + 1))
                for u in parts:
                    if acts is not None:
                        if last is not None:
                            act.wait_ge(parts_used, SPLIT_BEFORE[last] + u + 1)
                        act.copy(a_hi[:, u, :], acts[:, u, :]).then_inc(S["a_hi_ready"], 1)
                    if SPLIT_BEFORE[n]:
                        act.wait_ge(parts_used, SPLIT_BEFORE[n] + u + 1 - PARTS)
                    act.copy(split_part(kind, w_hi, u, width(kind, j)),
                             part_of(kind, wring[:, n % RING, :], u, width(kind, j))).then_inc(split_hi, 1)

            def h_round(r, order=(0, 1), gain=None, full=0):
                for n, half in enumerate(order):
                    cols = slice(half * 4, half * 4 + 4)
                    if full:
                        act.wait_ge(S["h_scaled"], full - 1 + n)
                        ins = act.copy(hT_hi[:, cols, :], h_full[:, cols, :])
                    else:
                        act.wait_ge(S["h_turned"], 2 * r - 1 + n)
                    if gain is not None:
                        for k in range(half * 4, half * 4 + 4):
                            at = 4 * 512 + k * T
                            ins = act.activation(hT_hi[:, k, :], psf[:, at:at + T], ACT.Copy, scale=gain(k))
                    elif not full:
                        ins = act.copy(hT_hi[:, cols, :].rearrange("p k t -> p (k t)"),
                                       psf[:, (4 + 2 * half) * 512:(6 + 2 * half) * 512])
                    ins.then_inc(S["tr_hi"], 1)

            def copy_round(r, dst):
                act.wait_ge(S["tr_done"], r)
                act.copy(dst, psf[:, 4 * 512:6 * 512]).then_inc(S["tr_copied_act"], 1)

            def empty(kind, j, dst, src, func=ACT.Copy, bias=0.0):
                stands(act, kind, j)
                act.activation(dst, src, func, bias=bias).then_inc(emptied_by["act"], 1)

            act.wait_ge(ld_c, 48)
            act.activation(csilu[:, 1, :], csilu[:, 0, :], ACT.Silu).then_inc(S["silu_c"], 1)
            act.wait_ge(ld_x, 16)
            squares(0, D, lambda b: (x_tok[:, b, :], h_tok[:, b, :]), 0)
            root(NB, 1, 2, "var", 1, "std")
            h_round(1, full=2)
            split("win", S_Q)

            def take_win(j):
                b0 = pair("win", j)
                empty("win", j, proj[:, :, j * HW:(j + 1) * HW], ps[:, b0:b0 + 2, :])

            def log_break(b4):
                t = tiles[:, 2 * b4, :]
                act.wait_ge(S["sb_z"], b4 + 1)
                own(act.activation(t, psf[:, 4 * 512:7 * 512], ACT.Abs))
                own(act.activation(t, t, ACT.Exp, scale=-1.0))
                act.activation(t, t, ACT.Ln, bias=1.0).then_inc(S["sb_L"], 1)

            def weight_exp(b4):
                t = tiles[:, 2 * b4, :]
                act.wait_ge(S["sb_logw"], b4 + 1)
                act.activation(t, t, ACT.Exp).then_inc(S["sb_exp"], 1)

            split("win", S_K)
            take_win(S_Q)
            act.wait_ge(S["angles"], 1)
            act.activation(trig[:, :, :, :], turns, ACT.Sin).then_inc(S["trig_ready"], 1)
            split("win", R_Q)
            take_win(S_K)
            root(32, 4, 6, "var_s", 1, "std_s")
            split("win", R_K)
            take_win(R_Q)
            copy_round(1, qT.rearrange("p c t -> p (c t)"))
            log_break(0)
            split("win", S_V)
            take_win(R_K)
            weight_exp(0)
            log_break(1)
            split("win", R_V)
            take_win(S_V)
            weight_exp(1)
            split("win", R_G, parts=range(0, 2))
            copy_round(2, qT.rearrange("p c t -> p (c t)"))
            split("win", R_G, parts=range(2, PARTS))
            take_win(R_V)
            root(16, 5, 7, "var_s", 2, "std_s")
            split("wout", 0)
            take_win(R_G)
            act.wait_ge(emptied_by["act"], emptied_count("win", R_G))
            act.activation(proj[:, :, 3 * HW:4 * HW], proj[:, :, 3 * HW:4 * HW], ACT.Silu).then_inc(S["ret_gate"], 1)
            root(16, 4, 6, "var_s", 3, "std_s")
            h_round(2, (1, 0))
            act.wait_ge(S["ada_used"], ADA_FIRST + ADA.index(ADA_GATE1[-1]) + 1)
            act.copy(GATE1, psf[:, 0:D]).then_inc(S["gate_out"], 1)
            split("wout", 1)
            for j in range(2):
                if j == 1:
                    split("wq", 0)
                add_squares(j, "x1_ready", j + 1, tiles[:, 2:4, :])
            root(NB, 1, 2, "var", 2, "std")
            h_round(3, full=4)

            def take_scores(j):
                bank = 4 + 2 * (j % 2)
                act.wait_ge(S["sub_done"], j + 1)
                act.copy(score[:, :, 2 * j:2 * j + 2, :].rearrange("p b h n -> p b (h n)"), ps[:, bank:bank + 2, :])\
                    .then_inc(S["sub_out"], 1)

            for j in range(4):
                split(*(("wq", j + 1) if j < 3 else ("dn", 0)))
                b0 = pair("wq", j)
                empty("wq", j, qryT[:, 4 * j:4 * j + 4, :].rearrange("p c t -> p (c t)"),
                      psf[:, b0 * 512:b0 * 512 + 1024])
                if j == 1:
                    act.wait_ge(S["ada_used"], ADA_FIRST + len(ADA))
                    act.copy(GATE2, psf[:, 6 * 512:6 * 512 + D]).then_inc(S["gate_out"], 1)
                if j >= 1:
                    take_scores(j - 1)

            def down_gelu(k):
                b0 = 2 * ((EMPTIED[down0][0] + k) % 2)
                act.activation(acts[k % LEAD].rearrange("p f t -> p (f t)"), psf[:, b0 * 512:b0 * 512 + 1024],
                               ACT.Gelu).then_inc(emptied_by["act"], 1)

            split("dn", 1)
            stands(act, "dn", 0)
            down_gelu(0)
            take_scores(3)
            for j in range(1, LEAD - 1):
                split("dn", j + 1)
                stands(act, "dn", j)
                down_gelu(j)
                if j == LEAD - 3:
                    act.wait_ge(S["score_max"], NB)
                    act.activation(sel[:, :, 2, :], sel[:, :, 2, :], ACT.Exp).then_inc(S["exp_done"], 1)
            stands(act, "dn", LEAD - 1)
            act.wait_ge(S["sel_turned"], 1)
            down_gelu(LEAD - 1)
            act.sem_inc(S["spread_out"], 2)
            for u in range(2):
                act.sem_inc(gates_stored[u], 16)
            act.sem_inc(gates_landed[0], 16)
            with act.Fori(0, T // (4 * TT)) as turn:
                for q in range(4):
                    group, e, u = turn * 4 + q, q % 2, q // 2
                    if e == 0:
                        act.wait_ge(gates_stored[u], turn * 16 + 16)
                    act.wait_ge(S["onehot_used"], turn * 8 + (OB + 2 * q + 2))
                    at = (4 + 2 * e) * 512
                    act.copy(spread[u][:, :, e * TT:(e + 1) * TT],
                             psf[:, at:at + TT * NKEY].rearrange("p (t n) -> p n t", n=NKEY)).then_inc(S["spread_out"], 1)
                    if e == 1:
                        act.wait_ge(S["spread_out"], group + 3)
                        act.dma_start(gates_dram[bass.ds(turn * 2 + u, 1), :, :].rearrange("g p n -> p (g n)"),
                                      spread[u].rearrange("p n t -> p (n t)")).then_inc(gates_stored[u], 16)
            def expert_split(i, k, up, parts, last_up=None):
                par, landed = ring_turn(i, up)
                act.wait_ge(w_in_slot[par], landed)
                for u in range(PARTS):
                    if last_up is not None:
                        act.wait_ge(parts_used, last_up + (u + 1))
                        act.copy(a_hi[:, u, :], acts[k][:, u, :]).then_inc(S["a_hi_ready"], 1)
                    act.wait_ge(parts_used, parts + (u + 1 - PARTS))
                    act.copy(w_hi[:, u, :], wring[:, par, u * PART:(u + 1) * PART]).then_inc(split_hi, 1)

            def expert_acts(i, k):
                down, up = slot_parts(i)
                if has_down(i):
                    expert_split(i, k, 0, down)
                act.wait_ge(S["weighed"], i + 1)
                expert_split(i, k, 1, up, (down if has_down(i) else up) - PARTS)
                if has_down(i):
                    act.wait_ge(parts_used, up)
                    act.wait_ge(S["a_lo_ready"], i * PARTS + PARTS)
                    down_gelu((k + LEAD) % LEAD)
                if k % 2 == 0 and not (isinstance(i, int) and i + 2 >= STEPS):
                    act.wait_ge(S["weighed"], i + 1)
                    act.dma_start(gates_in[:, (k // 2 + 1) % 2, :, :, :].rearrange("p g f t -> p g (f t)"),
                                  gates_dram[:, :, bass.ds(i * (EF * 16) + 2 * EF * 16, 2 * EF * 16)]
                                  .rearrange("g p n -> p g n")).then_inc(gates_landed[(k // 2 + 1) % 2], 16)

            expert_steps(act.Fori, expert_acts)

            split("win2", 0)
            for b in range(NB):
                act.wait_ge(S["x2_ready"], b + 1)
                act.activation(ptile[:, b, 0:D], x_tok[:, b, :], ACT.Square, accum_out=st[:, 0, b:b + 1])\
                    .then_inc(S["sumsq"], 1)
            root(NB, 1, 2, "var", 3, "std")
            h_round(4, gain=gain(G_MIX))

            def take_win2(j):
                b0, n = pair("win2", j), width("win2", j)
                empty("win2", j, z[:, :, j * CHUNK:j * CHUNK + n], ps[:, b0:b0 + 2, 0:n])

            for j in range(3):
                split("win2", j + 1)
                take_win2(j)
            act.wait_ge(S["c_tr"], 1)
            kv = psf[:, 4 * 512:6 * 512].rearrange("p (v g t) -> p v g t", v=2, g=NG)
            act.copy(kvA[0:64, :, :, :], kv[0:64, :, :, :])
            act.copy(kvA[64:P, :, :, 0:T - 1], kv[64:P, :, :, 1:T]).then_inc(S["kv_copied"], 1)
            split("win2", 4)
            take_win2(3)
            root(32, 4, 6, "zrms", 1, "zstd")
            act.wait_ge(emptied_by["act"], emptied_count("win2", 2))
            act.activation(gatec[:, :, :, :].rearrange("p b h k -> p b (h k)"), z[:, :, Z_G:Z_H], ACT.Sigmoid)\
                .then_inc(S["ret_gate"], 1)
            split("win2", 5)
            take_win2(4)
            take_win2(5)
            copy_round(3, qT2.rearrange("p c t -> p (c t)"))
            act.wait_ge(ld_cmp, 64)
            act.wait_ge(S["blk_ready"], 1)
            stands(act, "cmp", 1)
            for v in range(2):
                for f in range(2):
                    at = 3 * 512 + (2 * v + f) * 32
                    src = psf[:, at:at + 2 * NCMP].rearrange("p (g n) -> p g n", g=NG)
                    dst = hdnT[:, f, :].rearrange("p (g n) -> p g n", g=NG)[:, :, 0:NCMP]
                    if v == 1:
                        src = src.unsqueeze(2).to_broadcast([P, NG, R, NCMP])
                        dst = hdnV[:, f, :, :, 0:NCMP]
                    ins = act.activation(dst, src, ACT.Gelu_apprx_tanh, bias=cbias[:, v, f:f + 1])
            ins.then_inc(S["hdn_out"], 1)
            act.wait_ge(S["kvar"], 1)
            act.activation(kcst[:, 2:3], kcst[:, 1:2], ACT.Sqrt).then_inc(S["kstd"], 1)
            for g in range(NG):
                for r in range(R):
                    ins = act.copy(vbd[32 * r:32 * r + 32, g, r, :], ps[32 * r:32 * r + 32, 7, (2 + g) * HD:(3 + g) * HD])
            ins.then_inc(S["vcmp_out"], 1)

            def exp_batch(i):
                act.wait_ge(S["s_max"], i + 1)
                for b in range(NB):
                    for r in range(R):
                        lo, n = (r * P, P) if b == 0 else (512 + r * T, T)
                        t = ptile[:, i % 2, lo:lo + n]
                        ins = act.activation(t, t, ACT.Exp, bias=mx[:, i % 2, b, r:r + 1],
                                             accum_out=sm[:, i % 2, b, r:r + 1])
                ins.then_inc(S["p_ready"], 1)

            def take_turned(i):
                act.wait_ge(S["pt_done"], i + 1)
                if i >= 1:
                    act.wait_ge(S["o_done"], i)
                base = bank_set(i) * 512
                act.copy(pT.rearrange("p k r t -> p (k r t)"), psf[:, base:base + 3 * 512]).then_inc(S["pt_out"], 1)

            exp_batch(0)
            act.wait_ge(S["c_tr"], 2)
            act.copy(kcmpT[:, :], ps[:, 7, 256:320]).then_inc(S["kct_copied"], 1)
            act.wait_ge(S["c_max"], 1)
            act.activation(pcs, pcs, ACT.Exp).then_inc(S["c_exp"], 1)
            take_turned(0)
            for i in range(1, 4):
                exp_batch(i)
                take_turned(i)
            act.wait_ge(S["c_tr"], 3)
            act.copy(pcT.rearrange("p b g t -> p (b g t)"), ps[:, 4, :]).then_inc(S["c_out"], 1)
            act.wait_ge(S["conv_out"], 1)
            act.wait_ge(S["o_out"], 5)
            for b in range(NB):
                act.activation(tmp[:, b, :], h_tok[:, b, 0:HW], ACT.Square, accum_out=st[:, 0, b:b + 1])
                act.activation(sh1[:, b, :], z[:, b, Z_H:Z_H + HW], ACT.Square, accum_out=st[:, 0, 2 + b:3 + b])\
                    .then_inc(S["sumsq"], 1)
            root(4, 1, 2, "var", 4, "std")
            split("wo", 0)
            h_round(5, gain=gain(G_OUT))
            split("wo", 1)
            for j in range(2):
                if j == 1:
                    split("up", 0)
                add_squares(j, "x1_ready", j + 3, ptile)
            root(NB, 1, 2, "var", 5, "std")
            h_round(6, gain=gain(G_FFN))
            for j in range(DFF // CHUNK + 1):
                if 1 <= j < DFF // CHUNK:
                    split("up", j)
                if j >= 1:
                    act.wait_ge(S["u2_ready"], j)
                    split("down", j - 1, uT[:, (j - 1) % 2, :, :], NTH["down", j - 2] if j >= 2 else None)
                if j < DFF // CHUNK:
                    b0 = pair("up", j)
                    if j >= 2:
                        act.wait_ge(S["a_lo_ready"], (STEPS + j - 1) * PARTS)
                    empty("up", j, uT[:, j % 2, :, :].rearrange("p f t -> p (f t)"),
                          psf[:, b0 * 512:b0 * 512 + 1024], ACT.Relu)

        @block.gpsimd
        def _(pool):
            own = Chain(pool, pool_own)
            def ada_weights(j):
                n = ADA.index(j)
                if n and ADA[n - 1] in sum_place:
                    pool.wait_ge(S["ada_summed"], summed(ADA[n - 1]))
                else:
                    pool.wait_ge(S["ada_used"], ADA_FIRST + n if n else 1)
                pool.dma_start(pages[:, :].rearrange("p (k n) -> p k n", k=KC), ada_rows(j)).then_inc(ada_later_in, 16)

            for j in ADA[0:3]:
                ada_weights(j)
            pool.wait_ge(S["trig_ready"], 1)
            pool.wait_ge(emptied_by["act"], emptied_count("win", R_K))
            for b in range(NB):
                src = proj[:, b, 0:2 * HW].rearrange("p (h f d) -> p h f d", f=2, d=HD // 2)
                dst = h_tok[:, b, :].rearrange("p (h f d) -> p h f d", f=2, d=HD // 2)
                sin, cos = (trig[:, f, b, :].unsqueeze(1).to_broadcast([P, 2 * NH, HD // 2]) for f in range(2))
                own(pool.tensor_tensor(dst[:, :, 0, :], src[:, :, 0, :], cos, ALU.mult))
                own(pool.tensor_tensor(rot[0], src[:, :, 1, :], sin, ALU.mult))
                own(pool.tensor_tensor(dst[:, :, 0, :], dst[:, :, 0, :], rot[0], ALU.subtract))
                own(pool.tensor_tensor(dst[:, :, 1, :], src[:, :, 1, :], cos, ALU.mult))
                own(pool.tensor_tensor(rot[1], src[:, :, 0, :], sin, ALU.mult))
                pool.tensor_tensor(dst[:, :, 1, :], dst[:, :, 1, :], rot[1], ALU.add).then_inc(S["rot_ready"], 1)
            for j in ADA[3:]:
                ada_weights(j)
            for n in BY_POOL:
                for u in range(PARTS):
                    pool.wait_ge(split_hi, SPLIT_BEFORE[n] + u + 1)
                    hi, lo = (split_part(STREAM[n][0], v, u) for v in (w_hi, w_lo))
                    pool.tensor_tensor(lo, part_of(STREAM[n][0], wring[:, n % RING, :], u), hi, ALU.subtract)\
                        .then_inc(split_lo_pool, 1)
            with pool.Fori(0, T // (2 * OB * OT)) as turn:
                for q in range(2 * OB):
                    e = q % OB
                    pool.wait_ge(S["onehot_raw"], turn * (2 * OB) + (q + 1))
                    pool.tensor_tensor(onehot[:, 1, e, :, :], onehot[:, 1, e, :, :],
                                       cur[:, q // OB, 2, e * OT:(e + 1) * OT].unsqueeze(2).to_broadcast([P, OT, NKEY]),
                                       ALU.mult).then_inc(S["onehot_ready"], 1)
            for u in range(2):
                pool.wait_ge(gates_stored[u], 16 + 16 * (T // (4 * TT)))
            pool.dma_start(gates_in[:, 0, :, :, :].rearrange("p g f t -> p g (f t)"),
                           gates_dram[:, :, 0:2 * EF * 16].rearrange("g p n -> p g n")).then_inc(ld_gates, 16)
            pool.wait_ge(S["h_turned"], 8)
            own(pool.memset(sh1[0:1, 0, :], 0.0))
            own(pool.memset(sh2[0:2, 0, :], 0.0))
            pool.wait_ge(emptied_by["act"], emptied_count("win2", 4))
            u = z[:, :, Z_H:Z_H + HW]
            pool.tensor_tensor(u, z[:, :, Z_C:Z_C + HW], u, ALU.mult).then_inc(S["u_ready"], 1)
            pool.wait_ge(S["u_ready"], 1)
            for k, v in ((1, sh1), (2, sh2)):
                pool.dma_start(v[k:P, :, :], u[0:P - k, :, :]).then_inc(S["u_shifted"], 16)
                pool.dma_start(v[0:k, 1, :], u[P - k:P, 0, :]).then_inc(S["u_shifted"], 16)
            pool.wait_ge(ld_late, 16)
            pool.wait_ge(S["u_shifted"], 64)
            pool.wait_ge(emptied_by["act"], emptied_count("win2", 5))

            def tap(k):
                return convw[:, k, :].unsqueeze(1).to_broadcast([P, NB, HW])

            own(pool.tensor_tensor(u, u, tap(2), ALU.mult))
            own(pool.tensor_tensor(sh1, sh1, tap(1), ALU.mult))
            own(pool.tensor_tensor(sh2, sh2, tap(0), ALU.mult))
            own(pool.tensor_tensor(sh1, sh1, sh2, ALU.add))
            own(pool.tensor_tensor(u, u, sh1, ALU.add))
            pool.tensor_tensor(u, u, z[:, :, Z_B:Z_B + HW], ALU.mult).then_inc(S["conv_out"], 1)

        @block.vector
        def _(dve):
            own = Chain(dve, dve_own)

            def rstd(turn, n, width):
                dve.tensor_scalar(st[:, 1, 0:n], st[:, 0, 0:n], 1.0 / width, EPS, ALU.mult, ALU.add)\
                    .then_inc(S["var"], 1)
                dve.wait_ge(S["std"], turn)
                own(dve.reciprocal(st[:, 3, 0:n], st[:, 2, 0:n]))

            def copy_round(r, dst):
                dve.wait_ge(S["tr_done"], r)
                dve.tensor_copy(dst, psf[:, 6 * 512:8 * 512]).then_inc(S["tr_copied_dve"], 1)

            def split(kind, j, acts=None, step=None, parts=range(PARTS)):
                n = NTH[kind, j]
                for u in parts:
                    if acts is not None:
                        act_rest(acts, u, step)
                    dve.wait_ge(split_hi, SPLIT_BEFORE[n] + u + 1)
                    hi, lo = (split_part(kind, v, u, width(kind, j)) for v in (w_hi, w_lo))
                    dve.tensor_tensor(lo, part_of(kind, wring[:, n % RING, :], u, width(kind, j)), hi, ALU.subtract)\
                        .then_inc(split_lo, 1)

            def h_round(r, order=(0, 1), gain=None, shift=None):
                if shift is not None:
                    for half in range(2):
                        dve.wait_ge(S["h_turned"], 2 * r - 1 + half)
                        for k in range(half * 4, half * 4 + 4):
                            at = 4 * 512 + k * T
                            ins = dve.tensor_scalar(h_full[:, k, :], psf[:, at:at + T], gain(k), shift(k), ALU.mult, ALU.add)
                        ins.then_inc(S["h_scaled"], 1)
                for n, half in enumerate(order):
                    cols = slice(half * 4, half * 4 + 4)
                    dve.wait_ge(S["tr_hi"], 2 * r - 1 + n)
                    if gain is not None and shift is None:
                        for k in range(half * 4, half * 4 + 4):
                            at = 4 * 512 + k * T
                            ins = dve.scalar_tensor_tensor(hT_lo[:, k, :], psf[:, at:at + T], gain(k), hT_hi[:, k, :],
                                                           ALU.mult, ALU.subtract)
                    else:
                        full = psf[:, (4 + 2 * half) * 512:(6 + 2 * half) * 512] if shift is None \
                            else h_full[:, cols, :].rearrange("p k t -> p (k t)")
                        ins = dve.tensor_tensor(hT_lo[:, cols, :].rearrange("p k t -> p (k t)"), full,
                                                hT_hi[:, cols, :].rearrange("p k t -> p (k t)"), ALU.subtract)
                    ins.then_inc(S["h_split"], 1)

            def over_heads(row, n=NH):
                v = st[:, row, 0:NB * n].rearrange("p (b h) -> p b h", b=NB)
                return v.unsqueeze(3).to_broadcast([P, NB, n, HD])

            def head_gain(k, n=NH):
                return small[:, k, :].unsqueeze(1).unsqueeze(1).to_broadcast([P, NB, n, HD])

            def head_sums(row, v, square, n=NH):
                own(dve.tensor_tensor(square, v, v, ALU.mult))
                own(dve.tensor_reduce(st[:, row, 0:NB * n].rearrange("p (b h) -> p b h", b=NB), square, AX.X, ALU.add))

            def scales(turn, n, width, sums, halves=False):
                dve.wait_ge(S["sumsq"], sums)
                if halves:
                    own(dve.tensor_tensor(st[:, 0, 0:n], st[:, 0, 0:n], st[:, 0, n:2 * n], ALU.add))
                rstd(turn, n, width)
                for b in range(NB):
                    for k in range(b, n, NB):
                        ins = dve.tensor_scalar(diag[:, k, :], ident, st[:, 3, k:k + 1], None, ALU.mult)
                    ins.then_inc(S["h_ready"], 1)

            dve.wait_ge(ld_ident, 16)
            scales(1, NB, D, 2)

            def take_columns(slots, used, bank):
                cols = slice(GROUPS * slots[0], GROUPS * (slots[-1] + 1))
                dve.wait_ge(S["ada_used"], used)
                return dve.tensor_tensor(modc[:, cols], ps[:, bank, cols], adab[:, cols], ALU.add)

            def modulation(turn, scale, which):
                cols = slice(scale, scale + KC)
                dve.scalar_tensor_tensor(modc[:, cols], modc[:, cols], 1.0, gains[:, which, :], ALU.add, ALU.mult)\
                    .then_inc(S["mod_ready"], 1)
                dve.wait_ge(S["mod_ready"], turn)

            def sum_rows(j):
                if j in ADA_SECOND[1:]:
                    dve.wait_ge(S["ada_used"], ADA_FIRST + ADA_SECOND.index(j))
                w, s = ada_landed(dve, j), csilu[:, 1, :]
                own(dve.tensor_scalar(w[:, 0, :], w[:, 0, :], s[:, 0:1], None, ALU.mult))
                for k in range(1, KC):
                    ins = dve.scalar_tensor_tensor(w[:, 0, :] if k < KC - 1 else sum_place[j], w[:, k, :], s[:, k:k + 1],
                                                   w[:, 0, :], ALU.mult, ALU.add)
                    if k < KC - 1:
                        own(ins)
                ins.then_inc(S["ada_summed"], 1)

            dve.wait_ge(S["silu_c"], 1)
            for j in range(ADA_FIRST):
                sum_rows(j)
            dve.wait_ge(ld_c, 48)
            dve.wait_ge(ld_gain, 16)
            own(take_columns(range(ADA_FIRST), ADA_FIRST, 3))
            modulation(1, M_SCALE, G_1)
            h_round(1, gain=column(modc, M_SCALE), shift=column(modc, M_SHIFT))
            split("win", S_Q)

            dve.wait_ge(ld_pos, 16)
            dve.wait_ge(ld_const, 16)
            own(dve.tensor_copy(posf[:, :], posi[:, :]))
            for b in range(NB):
                own(dve.tensor_scalar(ang[:, b, :], con("freq"), posf[:, b:b + 1], None, ALU.mult))
            for f, quarter in enumerate((0.0, 0.25)):
                t = turns[:, f, :, :]
                own(dve.tensor_scalar(t, ang, 1.0 / TWO_PI, quarter, ALU.mult, ALU.add))
                own(dve.tensor_scalar(t, t, MAGIC, None, ALU.add))
                own(dve.tensor_scalar(t, t, MAGIC, None, ALU.subtract))
                w = ang2[:, f, :, :]
                own(dve.scalar_tensor_tensor(w, t, -C1, ang, ALU.mult, ALU.add))
                own(dve.scalar_tensor_tensor(w, t, -C2, w, ALU.mult, ALU.add))
                own(dve.scalar_tensor_tensor(w, t, -C3, w, ALU.mult, ALU.add))
                own(dve.tensor_scalar(w, w, quarter * TWO_PI, np.pi, ALU.add, ALU.min))
                ins = dve.tensor_scalar(t, w, -np.pi, None, ALU.max)
                if f == 0:
                    own(ins)
            ins.then_inc(S["angles"], 1)

            def sb_norms():
                dve.wait_ge(S["std_s"], 1)
                own(dve.reciprocal(st[:, 8:10, :], st[:, 6:8, :]))
                for k, v in enumerate((sq_, sk_)):
                    own(dve.tensor_tensor(v, v, over_heads(8 + k), ALU.mult))
                    dve.tensor_tensor(v, v, head_gain(k), ALU.mult).then_inc(S["sbq_ready"], 1)

            def sb_logs(b4):
                t = [tiles[:, 2 * b4 + k, :] for k in range(2)]
                zed = psf[:, 4 * 512:7 * 512]
                dve.wait_ge(S["sb_L"], b4 + 1)
                own(dve.scalar_tensor_tensor(t[0], zed, 0.0, t[0], ALU.min, ALU.subtract))
                own(dve.tensor_tensor(t[1], t[0], zed, ALU.subtract))
                mask = con("before").unsqueeze(1).to_broadcast([P, 4, P])
                for n in (0, 2):
                    v = t[1][:, n * 512:(n + 1) * 512].rearrange("p (h i) -> p h i", h=4)
                    ins = dve.tensor_tensor(v, v, mask, ALU.mult)
                ins.then_inc(S["sb_ls"], 1)

            def sb_weights(b4):
                t = tiles[:, 2 * b4, :]
                dve.wait_ge(S["sb_cum"], b4 + 1)
                dve.tensor_tensor(t, t, psf[:, 4 * 512:7 * 512], ALU.add).then_inc(S["sb_logw"], 1)

            def sb_mask(b4):
                t = tiles[:, 2 * b4, :]
                mask = con("before").unsqueeze(1).to_broadcast([P, 4, P])
                dve.wait_ge(S["sb_exp"], b4 + 1)
                for n in (0, 2):
                    v = t[:, n * 512:(n + 1) * 512].rearrange("p (h i) -> p h i", h=4)
                    ins = dve.tensor_tensor(v, v, mask, ALU.mult)
                ins.then_inc(S["sb_w"], 1)

            split("win", S_K)
            sq_, sk_ = (heads(proj[:, :, (4 + k) * HW:(5 + k) * HW]) for k in range(2))
            flat = tiles[:, 2, 0:1024].rearrange("p (b h d) -> p b h d", b=NB, d=HD)
            dve.wait_ge(emptied_by["act"], emptied_count("win", S_Q))
            head_sums(4, sq_, flat)
            sum_rows(6)
            dve.wait_ge(ld_early, 112)
            own(dve.tensor_scalar(small[:, 0, :], small[:, 0, :], HD ** -0.5, None, ALU.mult))
            own(dve.tensor_scalar(small[:, 3, :], small[:, 3, :], HD ** -0.5, None, ALU.mult))
            split("win", R_Q)
            dve.wait_ge(emptied_by["act"], emptied_count("win", S_K))
            head_sums(5, sk_, flat)
            dve.tensor_scalar(st[:, 4:6, :], st[:, 4:6, :], 1.0 / HD, EPS, ALU.mult, ALU.add).then_inc(S["var_s"], 1)
            sb_norms()
            split("win", R_K)
            copy_round(1, kT.rearrange("p c t -> p (c t)"))
            sum_rows(7)
            sb_logs(0)
            split("win", S_V)
            sb_weights(0)
            sb_mask(0)
            sum_rows(8)
            sb_logs(1)
            split("win", R_V)
            sb_weights(1)
            sb_mask(1)
            take_columns(ADA_SECOND[0:3], ADA_FIRST + 3, 7).then_inc(S["mod_taken"], 1)
            sum_rows(9)
            split("win", R_G, parts=range(0, 2))
            ys, yr = heads(proj[:, :, HW:2 * HW]), heads(proj[:, :, 0:HW])
            sqr = tiles[:, 3, 0:1024].rearrange("p (b h d) -> p b h d", b=NB, d=HD)
            dve.wait_ge(S["rot_ready"], 2)
            for b4 in range(2):
                dve.wait_ge(S["sb_y"], b4 + 1)
                for b in range(NB):
                    ins = dve.tensor_copy(every_other(proj[:, b, HW:2 * HW], b4),
                                          ps[:, b4, b * 256:(b + 1) * 256].rearrange("p (h d) -> p h d", d=HD))
                ins.then_inc(S["sb_y_out"], 1)
            copy_round(2, kT.rearrange("p c t -> p (c t)"))
            split("win", R_G, parts=range(2, PARTS))
            dve.wait_ge(S["sb_y_out"], 2)
            head_sums(5, ys, sqr)
            dve.tensor_scalar(st[:, 5, :], st[:, 5, :], 1.0 / HD, EPS, ALU.mult, ALU.add).then_inc(S["var_s"], 1)

            def ret_decay(b4):
                dve.wait_ge(S["ret_scores"], b4 + 1)
                for n in range(3):
                    ins = dve.tensor_tensor(tiles[:, b4, n * 512:(n + 1) * 512].rearrange("p (h i) -> p h i", h=4),
                                            ps[:, 4 + n, :].rearrange("p (h i) -> p h i", h=4),
                                            decay[:, n % 2, b4::2, :], ALU.mult)
                ins.then_inc(S["ret_decayed"], 1)

            ret_decay(0)
            dve.wait_ge(S["std_s"], 2)
            own(dve.reciprocal(st[:, 9, :], st[:, 7, :]))
            own(dve.tensor_tensor(ys, ys, over_heads(9), ALU.mult))
            dve.tensor_tensor(ys, ys, head_gain(2), ALU.mult).then_inc(S["y_ready"], 1)
            split("wout", 0, parts=range(0, 2))
            ret_decay(1)
            split("wout", 0, parts=range(2, PARTS))
            for b4 in range(2):
                dve.wait_ge(S["ret_y"], b4 + 1)
                for b in range(NB):
                    ins = dve.tensor_copy(every_other(proj[:, b, 0:HW], b4),
                                          ps[:, 2 + b4, b * 256:(b + 1) * 256].rearrange("p (h d) -> p h d", d=HD))
                ins.then_inc(S["ret_y_out"], 1)
            dve.wait_ge(S["ret_y_out"], 2)
            ysum = st[:, 4, :].rearrange("p (b h) -> p b h", b=NB)
            own(dve.tensor_reduce(ysum, yr, AX.X, ALU.add))
            own(dve.tensor_scalar(st[:, 4, :], st[:, 4, :], 1.0 / HD, None, ALU.mult))
            own(dve.tensor_tensor(yr, yr, over_heads(4), ALU.subtract))
            head_sums(4, yr, sqr)
            dve.tensor_scalar(st[:, 4, :], st[:, 4, :], 1.0 / HD, EPS, ALU.mult, ALU.add).then_inc(S["var_s"], 1)
            own(take_columns(ADA_SECOND[3:], ADA_FIRST + len(ADA_SECOND), 7))
            modulation(2, M_SCALE2, G_2)
            dve.wait_ge(S["std_s"], 3)
            own(dve.reciprocal(st[:, 8, :], st[:, 6, :]))
            own(dve.tensor_tensor(yr, yr, over_heads(8), ALU.mult))
            dve.wait_ge(S["ret_gate"], 1)
            yw = proj[:, :, 0:HW]
            own(dve.tensor_tensor(yw, yw, rgain.unsqueeze(1).to_broadcast([P, NB, HW]), ALU.mult))
            dve.tensor_tensor(yw, yw, proj[:, :, 3 * HW:4 * HW], ALU.mult).then_inc(S["y_ready"], 1)
            h_round(2, (1, 0))
            split("wout", 1)

            dve.wait_ge(S["gate_out"], 1)
            for j in range(2):
                if j == 1:
                    split("wq", 0, parts=range(PARTS - 1))
                b0, cols = pair("wout", j), slice(j * CHUNK, (j + 1) * CHUNK)
                stands(dve, "wout", j)
                gated = tiles[:, 0, 0:1024].rearrange("p (b n) -> p b n", b=NB)
                own(dve.tensor_tensor(gated, ps[:, b0:b0 + 2, :],
                                      GATE1[:, cols].unsqueeze(1).to_broadcast([P, NB, CHUNK]), ALU.mult))
                own(dve.tensor_tensor(x_tok[:, :, cols], x_tok[:, :, cols], gated, ALU.add))
                dve.sem_inc(emptied_by["dve"], 1)
                dve.sem_inc(S["x1_ready"], 1)
            scales(2, NB, D, 6, halves=True)
            split("wq", 0, parts=range(PARTS - 1, PARTS))
            h_round(3, gain=column(modc, M_SCALE2), shift=column(modc, M_SHIFT2))
            sum_rows(10)
            split("wq", 1)
            sum_rows(11)

            class TwoChains:

                def __init__(self):
                    self.sems, self.n = [S["choose0"], S["choose1"]], 0

                def __call__(self, op):
                    for b in range(NB):
                        if self.n:
                            dve.wait_ge(self.sems[b], self.n)
                        op(b).then_inc(self.sems[b], 1)
                    self.n += 1

                def finish(self):
                    for b in range(NB):
                        dve.wait_ge(self.sems[b], self.n)
                        dve.sem_clear(self.sems[b])
                    self.n = 0

            both = TwoChains()

            def top16(vals, work, values, index):
                both(lambda b: dve.max(values(b)[:, 0:8], vals(b)))
                both(lambda b: dve.max_index(index(b)[:, 0:8], values(b)[:, 0:8], vals(b)))
                both(lambda b: dve.match_replace(work(b), values(b)[:, 0:8], vals(b), -3.0e38))
                both(lambda b: dve.max(values(b)[:, 8:16], work(b)))
                both(lambda b: dve.max_index(index(b)[:, 8:16], values(b)[:, 8:16], work(b)))

            with dve.Fori(0, PH // 2) as turn:
                dve.wait_ge(S["sub_out"], turn + 1)
                for hh in range(2):
                    head = turn * 2 + hh
                    both(lambda b: dve.tensor_copy(sc2[:, b, :], score[:, b, bass.ds(head, 1), :]
                                                   .rearrange("p c n -> p (c n)")))
                    for half in range(2):
                        top16(lambda b: sc2[:, b, half * NKEY:(half + 1) * NKEY], lambda b: cand2[:, b, 0:NKEY],
                              lambda b: top[:, b, half, :], lambda b: topi[:, b, half, :])
                    both(lambda b: dve.tensor_tensor(cand[:, b, :].rearrange("p (i j) -> p i j", i=PK),
                                                     top[:, b, 0, :].unsqueeze(2).to_broadcast([P, PK, PK]),
                                                     top[:, b, 1, :].unsqueeze(1).to_broadcast([P, PK, PK]), ALU.add))
                    top16(lambda b: cand[:, b, :], lambda b: cand2[:, b, :], lambda b: best1[:, b, :],
                          lambda b: besti1[:, b, :])
                    both(lambda b: dve.tensor_copy(topf[:, b, bass.ds(head, 1), :, :].rearrange("p h k n -> p (h k) n"),
                                                   topi[:, b, :, :]))
                    both(lambda b: dve.tensor_copy(best[:, b, bass.ds(head, 1), :].rearrange("p h n -> p (h n)"),
                                                   best1[:, b, :]))
                    both(lambda b: dve.tensor_copy(besti[:, b, 0, bass.ds(head, 1), :].rearrange("p h n -> p (h n)"),
                                                   besti1[:, b, :]))
                both.finish()
            gate = [sel[:, b, 2, :].rearrange("p (h k) -> p h k", h=PH) for b in range(NB)]
            for b in range(NB):
                dve.tensor_tensor(gate[b], best[:, b, :, :], best[:, b, :, 0:1].to_broadcast([P, PH, PK]), ALU.subtract)\
                    .then_inc(S["score_max"], 1)
            both(lambda b: dve.tensor_scalar(besti[:, b, 1, :, :], besti[:, b, 0, :, :], 15, None, ALU.bitwise_and))
            both(lambda b: dve.tensor_scalar(besti[:, b, 0, :, :], besti[:, b, 0, :, :], 4, None, ALU.logical_shift_right))
            both(lambda b: dve.tensor_copy(bestf[:, b, :, :, :], besti[:, b, :, :, :]))
            for half in range(2):
                both(lambda b: dve.tensor_tensor(pick[:, b], bestf[:, b, half, :, :].unsqueeze(3)
                                                 .to_broadcast([P, PH, PK, PK]),
                                                 con("iota")[:, 0:PK].unsqueeze(1).unsqueeze(1)
                                                 .to_broadcast([P, PH, PK, PK]), ALU.is_equal))
                both(lambda b: dve.tensor_tensor(pick[:, b], pick[:, b], topf[:, b, :, half, :].unsqueeze(2)
                                                 .to_broadcast([P, PH, PK, PK]), ALU.mult))
                both(lambda b: dve.tensor_reduce(sel[:, b, half, :].rearrange("p (h k) -> p h k", h=PH), pick[:, b],
                                                 AX.X, ALU.add))
            dve.wait_ge(S["exp_done"], 1)
            both(lambda b: dve.tensor_reduce(gsum[:, b, :], gate[b], AX.X, ALU.add))
            both(lambda b: dve.reciprocal(gsum[:, b, :], gsum[:, b, :]))
            both.finish()
            for b in range(NB):
                dve.tensor_tensor(gate[b], gate[b], gsum[:, b, :].unsqueeze(2).to_broadcast([P, PH, PK]), ALU.mult)\
                    .then_inc(S["sel_ready"], 1)
            dve.wait_ge(S["sel_turned"], 1)
            own(dve.tensor_copy(selT.rearrange("p k (b t) -> p k b t", b=NB),
                                ps[:, 4:6, 0:3 * P].rearrange("p b (k t) -> p k b t", k=3)))
            dve.sem_inc(S["onehot_used"], OB)
            with dve.Fori(0, T // (2 * OB * OT)) as turn:
                for q in range(2 * OB):
                    e, u = q % OB, q // OB
                    dve.wait_ge(S["onehot_used"], turn * (2 * OB) + (q + 1))
                    if e == 0:
                        dve.tensor_copy(cur[:, u, :, :],
                                        selT[:, :, bass.ds(turn * (2 * OB * OT) + u * OB * OT, OB * OT)])\
                            .then_inc(S["cur_ready"], 1)
                        dve.wait_ge(S["cur_ready"], turn * 2 + (u + 1))
                    dve.tensor_tensor(onehot[:, :, e, :, :],
                                      con("iota").unsqueeze(1).unsqueeze(1).to_broadcast([P, 2, OT, NKEY]),
                                      cur[:, u, 0:2, e * OT:(e + 1) * OT].unsqueeze(3).to_broadcast([P, 2, OT, NKEY]),
                                      ALU.is_equal).then_inc(S["onehot_raw"], 1)
            dve.sem_inc(S["late_free"], 1)

            def weigh(i, k):
                act_k = acts[k].rearrange("p f (g t) -> p f g t", t=16)
                gates = gates_in[:, k // 2 % 2, :, (k % 2) * EF:(k % 2 + 1) * EF, :].rearrange("p g f t -> p f g t")
                dve.wait_ge(emptied_by["act"], i + (out_next - LEAD))
                if k == 0:
                    dve.wait_ge(ld_gates, 16)
                landed = 16 * (i // 4 + 1) if isinstance(i, int) else i * 4 + (16 - 4 * k + 16 * (k // 4))
                dve.wait_ge(gates_landed[k // 2 % 2], landed)
                dve.tensor_tensor(act_k, act_k, gates, ALU.mult).then_inc(S["weighed"], 1)

            def act_rest(source, u, step):
                dve.wait_ge(S["a_hi_ready"], step * PARTS + (u + 1))
                dve.tensor_tensor(a_lo[:, u, :], source[:, u, :], a_hi[:, u, :], ALU.subtract)\
                    .then_inc(S["a_lo_ready"], 1)

            def expert_rests(i, up, parts, source=None, step=None):
                par, _ = ring_turn(i, up)
                for u in range(PARTS):
                    if source is not None:
                        act_rest(source, u, step)
                    dve.wait_ge(split_hi, parts + (u + 1))
                    dve.tensor_tensor(w_lo[:, u, :], wring[:, par, u * PART:(u + 1) * PART], w_hi[:, u, :],
                                      ALU.subtract).then_inc(split_lo, 1)

            def expert_acts(i, k):
                down, up = slot_parts(i)
                if has_down(i):
                    expert_rests(i, 0, down)
                weigh(i, k)
                expert_rests(i, 1, up, acts[k], i)
            expert_steps(dve.Fori, expert_acts)
            for v in (hdnT, hdnV, vbd, pcmp):
                own(dve.memset(v, 0.0))
            split("win2", 0, parts=range(PARTS - 1))
            stands(dve, "ex", STEPS - 1)
            for b in range(NB):
                own(dve.tensor_tensor(h_tok[:, b, :], psf[:, 1024 * (2 + b):1024 * (3 + b)], GATE2, ALU.mult))
                dve.tensor_tensor(x_tok[:, b, :], x_tok[:, b, :], h_tok[:, b, :], ALU.add).then_inc(S["x2_ready"], 1)

            scales(3, NB, D, 8)
            split("win2", 0, parts=range(PARTS - 1, PARTS))
            h_round(4, gain=gain(G_MIX))
            split("win2", 1)
            split("win2", 2)
            zq = heads(z[:, :, Z_Q:Z_Q + HW])
            zk = [heads(z[:, :, c:c + NG * HD]) for c in (Z_KS, Z_KW)]
            dve.wait_ge(emptied_by["act"], emptied_count("win2", 0))
            head_sums(4, zq, sqq)

            def key_sums(r):
                tk = tmp_k
                own(dve.tensor_tensor(tk, zk[r], zk[r], ALU.mult))
                return dve.tensor_reduce(st[:, 5, 4 * r:4 * r + 4].rearrange("p (b g) -> p b g", b=NB), tk, AX.X, ALU.add)

            dve.wait_ge(emptied_by["act"], emptied_count("win2", 1))
            for v, c in enumerate((Z_KC, Z_VC)):
                for b in range(NB):
                    src = z[:, b, c:c + NG * HD].rearrange("p (g d) -> p g d", g=NG)
                    ins = dve.tensor_copy(kvdup[:, b, v, :, :, :], src.unsqueeze(2).to_broadcast([P, NG, 2, HD]))
            ins.then_inc(S["kv_ready"], 1)
            own(key_sums(0))
            split("win2", 3)
            dve.wait_ge(S["kv_copied"], 1)
            dve.wait_ge(ld_cmp, 64)
            for v in range(2):
                for hi in range(2):
                    win = kvA[:, v, :, :].rearrange("p g (n m two) -> p two m g n", two=2, m=8)
                    code = peT[:, v, 8 * hi:8 * hi + 8].unsqueeze(2).unsqueeze(2).to_broadcast([P, 8, NG, NCMP])
                    dst = blkT[:, v, 8 * hi:8 * hi + 8, :].rearrange("p m (g n) -> p m g n", g=NG)
                    ins = dve.tensor_tensor(dst, win[:, 0, :, :, hi:hi + NCMP], code, ALU.add)
            ins.then_inc(S["blk_ready"], 1)
            split("win2", 4)
            dve.wait_ge(emptied_by["act"], emptied_count("win2", 2))
            own(key_sums(1))
            dve.tensor_scalar(st[:, 4:6, :], st[:, 4:6, :], 1.0 / HD, EPS, ALU.mult, ALU.add).then_inc(S["zrms"], 1)
            split("win2", 5)
            dve.wait_ge(S["zstd"], 1)
            own(dve.reciprocal(st[:, 8:10, :], st[:, 6:8, :]))
            own(dve.tensor_tensor(zq, zq, over_heads(8), ALU.mult))
            dve.tensor_tensor(zq, zq, head_gain(3), ALU.mult)
            for r in range(2):
                spread_r = st[:, 9, 4 * r:4 * r + 4].rearrange("p (b g) -> p b g", b=NB)
                own(dve.tensor_tensor(zk[r], zk[r], spread_r.unsqueeze(3).to_broadcast([P, NB, NG, HD]), ALU.mult))
                for b in range(NB):
                    ins = dve.tensor_tensor(kdup[:, b, r, :, :, :],
                                            zk[r][:, b, :, :].unsqueeze(2).to_broadcast([P, NG, 2, HD]),
                                            small[:, 5 + r, :].unsqueeze(1).unsqueeze(1).to_broadcast([P, NG, 2, HD]),
                                            ALU.mult)
            ins.then_inc(S["kv_ready"], 1)
            copy_round(3, kT2.rearrange("p r g t -> p (r g t)"))

            def bias_batch(i):
                pt, base = ptile[:, i % 2, :], bank_set(i) * 512
                dve.wait_ge(S["s_done"], i + 1)
                if i >= 2:
                    dve.wait_ge(S["pt_done"], i - 1)
                lo, hi = CONST["dist"]
                dist = const[:, lo:hi].rearrange("p (b s) -> p b s", b=NB)
                for b in range(NB):
                    for r in range(R):
                        at, n = (r * P, P) if b == 0 else (512 + r * T, T)
                        slope = 2.0 ** -(2 * r + i % 2 + 1)
                        ins = dve.scalar_tensor_tensor(pt[:, at:at + n], dist[:, b, 0:n], slope,
                                                       psf[:, base + at:base + at + n], ALU.mult, ALU.add)
                own(ins)
                dve.tensor_reduce(mx[:, i % 2, 0, :], pt[:, 0:512].rearrange("p (r s) -> p r s", r=R), AX.X, ALU.max,
                                  negate=True)
                dve.tensor_reduce(mx[:, i % 2, 1, :], pt[:, 512:1536].rearrange("p (r s) -> p r s", r=R), AX.X,
                                  ALU.max, negate=True).then_inc(S["s_max"], 1)

            def add_branch(coef, src, dst, fresh):
                c = coef.unsqueeze(3).to_broadcast([P, NB, coef.shape[2], HD])
                if fresh:
                    return dve.tensor_tensor(dst, src, c, ALU.mult)
                t = tmp[:, :, 0:coef.shape[2] * HD].rearrange("p b (h d) -> p b h d", d=HD)
                own(dve.tensor_tensor(t, src, c, ALU.mult))
                return dve.tensor_tensor(dst, dst, t, ALU.add)

            oh = heads(h_tok[:, :, 0:HW])

            def take_out(i):
                br, par = i // 2, i % 2
                s = sm[:, i % 2, :, :]
                dve.wait_ge(S["p_ready"], i + 1)
                own(dve.tensor_scalar(s, s, 1e-30, None, ALU.max))
                own(dve.reciprocal(s, s))
                own(dve.tensor_tensor(s, s, gatec[:, :, par::2, br + 1], ALU.mult))
                dve.wait_ge(S["o_done"], i + 1)
                own(add_branch(s, ps[:, bank_set(i) + 3, :].rearrange("p (b r d) -> p b r d", b=NB, r=R),
                               oh[:, :, par::2, :], br == 0))
                dve.sem_inc(S["o_out"], 1)

            def compressed_norm():
                dve.wait_ge(S["kcmp"], 1)
                own(dve.tensor_copy(kcn[:, 0, :], ps[0:64, 7, 0:HD]))
                own(dve.tensor_tensor(kcq[:, :], kcn[:, 0, :], kcn[:, 0, :], ALU.mult))
                own(dve.tensor_reduce(kcst[:, 0:1], kcq[:, :], AX.X, ALU.add))
                dve.tensor_scalar(kcst[:, 1:2], kcst[:, 0:1], 1.0 / HD, EPS, ALU.mult, ALU.add).then_inc(S["kvar"], 1)
                dve.wait_ge(S["kstd"], 1)
                own(dve.reciprocal(kcst[:, 3:4], kcst[:, 2:3]))
                own(dve.scalar_tensor_tensor(kcn[:, 0, :], kcn[:, 0, :], kcst[:, 3:4], small[0:64, 4, :],
                                             ALU.mult, ALU.mult))
                dve.tensor_copy(kcn[:, 1, :], kcn[:, 0, :]).then_inc(S["kcn_ready"], 1)

            def by_head(v):
                return v.rearrange("p (b h) n -> p b h n", b=NB)

            def compressed_scores():
                dve.wait_ge(S["cs_done"], 1)
                lo, hi = CONST["cdist"]
                dist = const[:, lo:hi].rearrange("p (b n) -> p b n", b=NB)
                for h in range(NH):
                    raw = ps[:, 3 + 4 * (h % 2), 0:NB * R * CSTEP].rearrange("p (b h n) -> p b h n", b=NB, n=CSTEP)
                    ins = dve.scalar_tensor_tensor(by_head(pcs)[:, :, h, :], dist, 2.0 ** -(h + 1),
                                                   raw[:, :, h // 2, :], ALU.mult, ALU.add)
                own(ins)
                own(dve.tensor_reduce(cst[:, 0, :], pcs, AX.X, ALU.max))
                dve.tensor_tensor(pcs, pcs, cst[:, 0, :].unsqueeze(2).to_broadcast([P, NB * NH, CSTEP]),
                                  ALU.subtract).then_inc(S["c_max"], 1)

            def compressed_weights():
                lo, hi = CONST["cmask"]
                mask = const[:, lo:hi].rearrange("p (b n) -> p b n", b=NB)
                dve.wait_ge(S["c_exp"], 1)
                dst = pcmp[:, :, :, 0:CSTEP]
                dve.tensor_tensor(dst, by_head(pcs), mask.unsqueeze(2).to_broadcast([P, NB, NH, CSTEP]), ALU.mult)\
                    .then_inc(S["c_ready"], 1)
                dve.wait_ge(S["c_ready"], 1)
                total, coef = (cst[:, k, :].rearrange("p (b h) -> p b h", b=NB) for k in (1, 2))
                own(dve.tensor_reduce(total, dst, AX.X, ALU.add))
                own(dve.tensor_scalar(total, total, 1e-30, None, ALU.max))
                own(dve.reciprocal(total, total))
                own(dve.tensor_tensor(coef, total, gatec[:, :, :, 0], ALU.mult))
                return coef

            bias_batch(0)
            compressed_norm()
            bias_batch(1)
            compressed_scores()
            coef = compressed_weights()
            dve.wait_ge(S["ret_gate"], 2)
            take_out(0)
            bias_batch(2)
            take_out(1)
            bias_batch(3)
            take_out(2)
            take_out(3)
            dve.wait_ge(S["co_done"], 1)
            own(add_branch(coef, psf[:, 5 * 512:7 * 512].rearrange("p (b h d) -> p b h d", b=NB, d=HD), oh, False))
            dve.sem_inc(S["o_out"], 1)

            scales(4, 2 * NB, HW, 10)
            split("wo", 0)
            h_round(5, gain=gain(G_OUT))
            split("wo", 1)
            for j in range(2):
                if j == 1:
                    split("up", 0, parts=range(PARTS - 1))
                b0, cols = pair("wo", j), slice(j * CHUNK, (j + 1) * CHUNK)
                stands(dve, "wo", j)
                own(dve.tensor_tensor(x_tok[:, :, cols], x_tok[:, :, cols], ps[:, b0:b0 + 2, :], ALU.add))
                dve.sem_inc(emptied_by["dve"], 1)
                dve.sem_inc(S["x1_ready"], 1)
            scales(5, NB, D, 14, halves=True)
            split("up", 0, parts=range(PARTS - 1, PARTS))
            h_round(6, gain=gain(G_FFN))
            for j in range(DFF // CHUNK + 1):
                if 1 <= j < DFF // CHUNK:
                    split("up", j)
                if j >= 1:
                    split("down", j - 1, uT[:, (j - 1) % 2, :, :], STEPS + j - 1)
                if j < DFF // CHUNK:
                    t = uT[:, j % 2, :, :].rearrange("p f t -> p (f t)")
                    dve.wait_ge(emptied_by["act"], emptied_count("up", j))
                    dve.tensor_tensor(t, t, t, ALU.mult).then_inc(S["u2_ready"], 1)
            stands(dve, "down", DFF // CHUNK - 1)
            for b in range(NB):
                dve.tensor_tensor(x_tok[:, b, :], x_tok[:, b, :], psf[:, (4 + 2 * b) * 512:(6 + 2 * b) * 512], ALU.add)\
                    .then_inc(S["x_out"], 1)


def kernel(**inputs):
    from concourse import bacc
    from concourse.bass_utils import run_bass_kernel_spmd

    def of(name):
        return np.asarray(inputs[name])

    def put(a):
        return np.ascontiguousarray(a)

    arrays = {
        "x": of("x")[0],
        "c": of("c").reshape(KC, P).T,
        "positions": of("positions")[0],
        "ada_w": of("ada_w")[0],
        "ada_b": of("ada_b").reshape(6 * KC, P).T,
        "ada_b_rows": of("ada_b").reshape(12, CHUNK),
        "gains": np.stack([of(name)[0].reshape(KC, P).T for name in
                           ("norm1_gain", "norm2_gain", "g_mix_norm_2", "g_out_2", "g_ffn_norm_2")], axis=1),
        "w_in": of("w_in")[0],
        "ret_gain": of("ret_norm_gain")[0],
        "sb_q": of("sb_q_gain")[0],
        "sb_k": of("sb_k_gain")[0],
        "sb_out": of("sb_out_gain")[0],
        "w_out": of("w_out")[0],
        "w_query": of("peer_w_query")[0],
        "keys": of("peer_sub_keys")[0].transpose(3, 0, 1, 2).reshape(P, -1),
        "peer_down": of("peer_down")[0].reshape(STEPS, EF, P, KC, P).transpose(0, 4, 1, 3, 2).reshape(STEPS * P, SLOT),
        "peer_up": of("peer_up")[0],
        "w_in2": of("w_in_2")[0],
        "g_q": of("g_q_2")[0],
        "g_k": of("g_k_2").reshape(-1),
        "pe": of("pe_cmp_2")[0].reshape(2, NPAIR, 2, HD).transpose(2, 3, 0, 1).reshape(P, 2, NPAIR),
        "w_cmp1": of("w_cmp1_2")[0],
        "b_cmp1": of("b_cmp1_2")[0].reshape(2, 2, P).transpose(2, 0, 1),
        "w_cmp2": of("w_cmp2_2")[0],
        "b_cmp2": of("b_cmp2_2").reshape(1, 2, HD),
        "conv_w": of("conv_w_2").reshape(-1),
        "w_o": of("w_o_2")[0],
        "w_up": of("w_up_2")[0],
        "w_down": of("w_down_2")[0],
        "const": constants(),
        "decay": decay_table(),
    }
    arrays = {name: put(a) for name, a in arrays.items()}
    nc = bacc.Bacc("TRN2", target_bir_lowering=False, num_devices=1)
    aps = {name: nc.dram_tensor("in_" + name, a.shape, mybir.dt.from_np(a.dtype), kind="ExternalInput").ap()
           for name, a in arrays.items()}
    out = nc.dram_tensor("out", (T, D), F32, kind="ExternalOutput").ap()
    two_blocks(nc, aps, out)
    result = run_bass_kernel_spmd(nc, [{"in_" + name: a for name, a in arrays.items()}], core_ids=[0])
    return result.results[0]["out"].reshape(1, T, D)
```
